# Optimizing a Trainium2 kernel written in Bass

```python
import math
import jax, jax.numpy as jnp
from jax import lax
import numpy as np
import jax
import jax.numpy as jnp

D_MODEL = 1024
BATCH = 1
SEQ = 256
DEPTH = 2

MIX_WIDTH = D_MODEL
LRU_WIDTH = MIX_WIDTH // 2
LRU_BLOCKS = 8
LRU_BLOCK_DIM = LRU_WIDTH // LRU_BLOCKS
CONV_WIDTH = 4
LRU_C = 8.0
N_HEADS = 8
HEAD_DIM = (MIX_WIDTH - LRU_WIDTH) // N_HEADS
N_KV = 2
Q_PER_KV = N_HEADS // N_KV
NSA_WIDTH = N_HEADS * HEAD_DIM
KV_WIDTH = N_KV * HEAD_DIM
N_BRANCHES = 3
CMP_BLOCK = 32
CMP_STRIDE = 16
SEL_BLOCK = 64
SEL_TOPN = 16
WINDOW = 512
Q_BLOCK = 128
FORCE_BONUS = 1e4
NEG = -1e30
PEER_HEADS = 8
PEER_KEYS = 128
PEER_TOPK = 16
PEER_KEY_DIM = 128
N_EXPERTS = PEER_KEYS * PEER_KEYS
PEER_CHUNK = 512
IN_SPLITS = (LRU_WIDTH, LRU_WIDTH, NSA_WIDTH, KV_WIDTH, KV_WIDTH, KV_WIDTH, KV_WIDTH, KV_WIDTH, KV_WIDTH, N_HEADS * N_BRANCHES)
IN_COLS = sum(IN_SPLITS)
ALPHA = (2 * DEPTH) ** 0.25
BETA = (8 * DEPTH) ** -0.25
LN_EPS = 1e-5


def _layer_norm(x, g, b):
    xf = x.astype(jnp.float32)
    mu = jnp.mean(xf, -1, keepdims=True)
    var = jnp.mean(jnp.square(xf - mu), -1, keepdims=True)
    return ((xf - mu) * lax.rsqrt(var + LN_EPS) * g.astype(jnp.float32) + b.astype(jnp.float32)).astype(x.dtype)

def _rms_norm(x, g):
    xf = x.astype(jnp.float32)
    return (xf * lax.rsqrt(jnp.mean(jnp.square(xf), -1, keepdims=True) + LN_EPS) * g.astype(jnp.float32)).astype(x.dtype)

def _alibi_slopes(n):
    return jnp.asarray(np.array([2.0 ** (-8.0 * (h + 1) / n) for h in range(n)], np.float32))

def _rg_lru(xb, gate, conv_w, conv_b, wa, ba, wx, bx, lam):
    B, S, C = xb.shape
    xc = lax.conv_general_dilated(xb, conv_w[:, None, :], window_strides=(1,), padding=[(CONV_WIDTH - 1, 0)],
                                  dimension_numbers=('NWC', 'WIO', 'NWC'), feature_group_count=C) + conv_b
    xr = xc.reshape(B, S, LRU_BLOCKS, LRU_BLOCK_DIM)
    r = jax.nn.sigmoid(jnp.einsum('bsnd,nde->bsne', xr, wa) + ba.reshape(LRU_BLOCKS, LRU_BLOCK_DIM)).reshape(B, S, C)
    i = jax.nn.sigmoid(jnp.einsum('bsnd,nde->bsne', xr, wx) + bx.reshape(LRU_BLOCKS, LRU_BLOCK_DIM)).reshape(B, S, C)
    log_a = -LRU_C * r.astype(jnp.float32) * jax.nn.softplus(-lam.astype(jnp.float32))
    a = jnp.exp(log_a)
    u = jnp.sqrt(-jnp.expm1(2.0 * log_a)) * (i * xc).astype(jnp.float32)

    def combine(left, right):
        a1, b1 = left
        a2, b2 = right
        return a1 * a2, a2 * b1 + b2

    _, h = lax.associative_scan(combine, (a, u), axis=1)
    return h.astype(xb.dtype) * jax.nn.gelu(gate)

def _compress(k, pos, w1, b1, w2, b2):
    B, S, G, hd = k.shape
    nc = (S - CMP_BLOCK) // CMP_STRIDE + 1
    idx = np.arange(nc)[:, None] * CMP_STRIDE + np.arange(CMP_BLOCK)[None, :]
    blk = k[:, idx] + pos[None, None, :, None, :]
    flat = blk.transpose(0, 1, 3, 2, 4).reshape(B, nc, G, CMP_BLOCK * hd)
    return jax.nn.gelu(flat @ w1 + b1) @ w2 + b2

def _selection_matrix(n_cmp, n_sel):
    cs = np.arange(n_cmp)[:, None] * CMP_STRIDE
    ss = np.arange(n_sel)[None, :] * SEL_BLOCK
    ov = np.clip(np.minimum(cs + CMP_BLOCK, ss + SEL_BLOCK) - np.maximum(cs, ss), 0, None)
    return (ov / CMP_STRIDE).astype(np.float32)

def _nsa(q, kc, vc, ks, vs, kw, vw, gates):
    B, S = q.shape[:2]
    G, R, hd = N_KV, Q_PER_KV, HEAD_DIM
    nb = S // Q_BLOCK
    qb_all = (q * (hd ** -0.5)).reshape(B, nb, Q_BLOCK, G, R, hd).transpose(1, 0, 2, 3, 4, 5)
    g_all = jax.nn.sigmoid(gates).reshape(B, nb, Q_BLOCK, G, R, N_BRANCHES).transpose(1, 0, 2, 3, 4, 5)
    slopes = _alibi_slopes(N_HEADS).reshape(G, R)
    nc = kc.shape[1]
    cmp_end = jnp.arange(nc) * CMP_STRIDE + CMP_BLOCK - 1
    n_sel = S // SEL_BLOCK
    n_top = min(SEL_TOPN, n_sel)
    sel_mat = jnp.asarray(_selection_matrix(nc, n_sel))
    ks_blk = ks.transpose(0, 2, 1, 3).reshape(B, G, n_sel, SEL_BLOCK, hd)
    vs_blk = vs.transpose(0, 2, 1, 3).reshape(B, G, n_sel, SEL_BLOCK, hd)
    kw_pad = jnp.pad(kw, ((0, 0), (WINDOW, 0), (0, 0), (0, 0)))
    vw_pad = jnp.pad(vw, ((0, 0), (WINDOW, 0), (0, 0), (0, 0)))
    gather = jax.vmap(jax.vmap(lambda blk, ix: blk[ix]))
    blk_id = jnp.arange(n_sel)

    def one_block(args):
        qb, q_blk, g_blk = args
        t = qb * Q_BLOCK + jnp.arange(Q_BLOCK)
        s = jnp.einsum('bqgrd,bcgd->bgrqc', q_blk, kc).astype(jnp.float32)
        dist_c = (t[:, None] - cmp_end[None, :]).astype(jnp.float32)
        s = s - slopes[:, :, None, None] * jnp.abs(dist_c)
        valid_c = cmp_end[None, :] <= t[:, None]
        p_c = jax.nn.softmax(jnp.where(valid_c, s, NEG), axis=-1) * valid_c.any(-1)[:, None].astype(jnp.float32)
        o_c = jnp.einsum('bgrqc,bcgd->bqgrd', p_c.astype(vc.dtype), vc)
        imp = jnp.einsum('bgrqc,cj->bgqj', p_c, sel_mat)
        cur = t // SEL_BLOCK
        vblk = blk_id[None, :] <= cur[:, None]
        forced = (blk_id[None, :] == 0) | (blk_id[None, :] == cur[:, None]) | (blk_id[None, :] == cur[:, None] - 1)
        imp = jnp.where(vblk, imp + jnp.where(forced, FORCE_BONUS, 0.0), NEG)
        _, idx = lax.top_k(imp, n_top)
        k_sel = gather(ks_blk, idx)
        v_sel = gather(vs_blk, idx)
        tok = idx[..., None] * SEL_BLOCK + jnp.arange(SEL_BLOCK)
        dist_s = (t[None, None, :, None, None] - tok)[:, :, None]
        s = jnp.einsum('bqgrd,bgqnld->bgrqnl', q_blk, k_sel).astype(jnp.float32)
        s = s - slopes[None, :, :, None, None, None] * jnp.abs(dist_s).astype(jnp.float32)
        s = jnp.where(dist_s >= 0, s, NEG)
        p_s = jax.nn.softmax(s.reshape(s.shape[:4] + (n_top * SEL_BLOCK,)), axis=-1).reshape(s.shape)
        o_s = jnp.einsum('bgrqnl,bgqnld->bqgrd', p_s.astype(v_sel.dtype), v_sel)
        k_w = lax.dynamic_slice_in_dim(kw_pad, qb * Q_BLOCK, WINDOW + Q_BLOCK, axis=1)
        v_w = lax.dynamic_slice_in_dim(vw_pad, qb * Q_BLOCK, WINDOW + Q_BLOCK, axis=1)
        pos = qb * Q_BLOCK - WINDOW + jnp.arange(WINDOW + Q_BLOCK)
        dist_w = t[:, None] - pos[None, :]
        valid_w = (dist_w >= 0) & (dist_w < WINDOW) & (pos >= 0)[None, :]
        s = jnp.einsum('bqgrd,bkgd->bgrqk', q_blk, k_w).astype(jnp.float32)
        s = s - slopes[:, :, None, None] * dist_w.astype(jnp.float32)
        p_w = jax.nn.softmax(jnp.where(valid_w, s, NEG), axis=-1)
        o_w = jnp.einsum('bgrqk,bkgd->bqgrd', p_w.astype(v_w.dtype), v_w)
        return g_blk[..., 0:1] * o_c + g_blk[..., 1:2] * o_s + g_blk[..., 2:3] * o_w

    out = lax.map(one_block, (jnp.arange(nb), qb_all, g_all))
    return out.transpose(1, 0, 2, 3, 4, 5).reshape(B, S, N_HEADS * hd)

def _peer(x, wq, subkeys, u_tab, v_tab):
    B, S, D = x.shape
    T = B * S
    xf = x.reshape(T, D)
    q = (xf @ wq).reshape(T, PEER_HEADS, 2, PEER_KEY_DIM)
    s = jnp.einsum('thcd,ckd->thck', q, subkeys).astype(jnp.float32)
    sv, si = lax.top_k(s, PEER_TOPK)
    cand = (sv[:, :, 0, :, None] + sv[:, :, 1, None, :]).reshape(T, PEER_HEADS, PEER_TOPK * PEER_TOPK)
    cv, ci = lax.top_k(cand, PEER_TOPK)
    ea = jnp.take_along_axis(si[:, :, 0], ci // PEER_TOPK, axis=-1)
    eb = jnp.take_along_axis(si[:, :, 1], ci % PEER_TOPK, axis=-1)
    experts = (ea * PEER_KEYS + eb).reshape(T, PEER_HEADS * PEER_TOPK)
    gate = jax.nn.softmax(cv, axis=-1).reshape(T, PEER_HEADS * PEER_TOPK).astype(x.dtype)
    chunk = math.gcd(T, PEER_CHUNK)
    nch = T // chunk

    def one_chunk(args):
        xc, ec, gc = args
        act = jax.nn.gelu(jnp.einsum('cd,ced->ce', xc, u_tab[ec]))
        return jnp.einsum('ce,ced->cd', act * gc, v_tab[ec])

    y = lax.map(one_chunk, (xf.reshape(nch, chunk, D), experts.reshape(nch, chunk, -1), gate.reshape(nch, chunk, -1)))
    return y.reshape(B, S, D)

def first_inputs(seed: int = 0) -> dict:
    key = jax.random.key(seed)
    ks = jax.random.split(key, 40)
    L = DEPTH

    def nrm(k, shape, scale):
        return jax.random.normal(k, shape, jnp.float32) * scale

    col_scale = np.concatenate([np.full(n, s, np.float32) for n, s in zip(
        IN_SPLITS, (BETA, 1.0, 1.0, 1.0, BETA, 1.0, BETA, 1.0, BETA, 1.0))])
    u = jax.random.uniform(ks[9], (L, LRU_WIDTH), jnp.float32, 0.9, 0.999)
    a0 = u ** (1.0 / LRU_C)
    fan_c = CMP_BLOCK * HEAD_DIM
    return {
        'x': nrm(ks[0], (BATCH, SEQ, D_MODEL), 1.0),
        'w_in': nrm(ks[1], (L, D_MODEL, IN_COLS), D_MODEL ** -0.5) * jnp.asarray(col_scale),
        'b_in': nrm(ks[2], (L, IN_COLS), 0.01),
        'conv_w': nrm(ks[3], (L, CONV_WIDTH, LRU_WIDTH), CONV_WIDTH ** -0.5),
        'conv_b': nrm(ks[4], (L, LRU_WIDTH), 0.01),
        'lru_wa': nrm(ks[5], (L, LRU_BLOCKS, LRU_BLOCK_DIM, LRU_BLOCK_DIM), LRU_BLOCK_DIM ** -0.5),
        'lru_ba': nrm(ks[6], (L, LRU_WIDTH), 0.01),
        'lru_wx': nrm(ks[7], (L, LRU_BLOCKS, LRU_BLOCK_DIM, LRU_BLOCK_DIM), LRU_BLOCK_DIM ** -0.5),
        'lru_bx': nrm(ks[8], (L, LRU_WIDTH), 0.01),
        'lru_lambda': jnp.log(a0) - jnp.log1p(-a0),
        'cmp_pos_k': nrm(ks[10], (L, CMP_BLOCK, HEAD_DIM), 0.02),
        'cmpk_w1': nrm(ks[11], (L, fan_c, HEAD_DIM), fan_c ** -0.5),
        'cmpk_b1': nrm(ks[12], (L, HEAD_DIM), 0.01),
        'cmpk_w2': nrm(ks[13], (L, HEAD_DIM, HEAD_DIM), HEAD_DIM ** -0.5),
        'cmpk_b2': nrm(ks[14], (L, HEAD_DIM), 0.01),
        'cmp_pos_v': nrm(ks[15], (L, CMP_BLOCK, HEAD_DIM), 0.02),
        'cmpv_w1': nrm(ks[16], (L, fan_c, HEAD_DIM), fan_c ** -0.5),
        'cmpv_b1': nrm(ks[17], (L, HEAD_DIM), 0.01),
        'cmpv_w2': nrm(ks[18], (L, HEAD_DIM, HEAD_DIM), HEAD_DIM ** -0.5),
        'cmpv_b2': nrm(ks[19], (L, HEAD_DIM), 0.01),
        'gn_lru_g': 1.0 + nrm(ks[20], (L, LRU_WIDTH), 0.02),
        'gn_nsa_g': 1.0 + nrm(ks[21], (L, NSA_WIDTH), 0.02),
        'w_out': nrm(ks[22], (L, MIX_WIDTH, D_MODEL), BETA * MIX_WIDTH ** -0.5),
        'ln1_g': 1.0 + nrm(ks[23], (L, D_MODEL), 0.02),
        'ln1_b': nrm(ks[24], (L, D_MODEL), 0.02),
        'peer_wq': nrm(ks[25], (L, D_MODEL, PEER_HEADS * 2 * PEER_KEY_DIM), D_MODEL ** -0.5),
        'peer_subkeys': nrm(ks[26], (L, 2, PEER_KEYS, PEER_KEY_DIM), PEER_KEY_DIM ** -0.5),
        'peer_u': nrm(ks[27], (L, N_EXPERTS, D_MODEL), D_MODEL ** -0.5),
        'peer_v': nrm(ks[28], (L, N_EXPERTS, D_MODEL), BETA * PEER_HEADS ** -0.5),
        'ln2_g': 1.0 + nrm(ks[29], (L, D_MODEL), 0.02),
        'ln2_b': nrm(ks[30], (L, D_MODEL), 0.02),
    }

def first_block(x, w_in, b_in, conv_w, conv_b, lru_wa, lru_ba, lru_wx, lru_bx, lru_lambda,
              cmp_pos_k, cmpk_w1, cmpk_b1, cmpk_w2, cmpk_b2,
              cmp_pos_v, cmpv_w1, cmpv_b1, cmpv_w2, cmpv_b2,
              gn_lru_g, gn_nsa_g, w_out, ln1_g, ln1_b,
              peer_wq, peer_subkeys, peer_u, peer_v, ln2_g, ln2_b):
    B, S, _ = x.shape
    offsets = np.cumsum(IN_SPLITS)[:-1].tolist()
    for l in range(DEPTH):
        h = x @ w_in[l] + b_in[l]
        lru_x, lru_gate, q, kc_raw, vc_raw, ks_, vs_, kw_, vw_, gts = jnp.split(h, offsets, axis=-1)
        y_lru = _rg_lru(lru_x, lru_gate, conv_w[l], conv_b[l], lru_wa[l], lru_ba[l],
                        lru_wx[l], lru_bx[l], lru_lambda[l])
        kv = lambda t: t.reshape(B, S, N_KV, HEAD_DIM)
        kc = _compress(kv(kc_raw), cmp_pos_k[l], cmpk_w1[l], cmpk_b1[l], cmpk_w2[l], cmpk_b2[l])
        vc = _compress(kv(vc_raw), cmp_pos_v[l], cmpv_w1[l], cmpv_b1[l], cmpv_w2[l], cmpv_b2[l])
        y_nsa = _nsa(q.reshape(B, S, N_HEADS, HEAD_DIM), kc, vc, kv(ks_), kv(vs_), kv(kw_), kv(vw_),
                     gts.reshape(B, S, N_HEADS, N_BRANCHES))
        mix = jnp.concatenate([_rms_norm(y_lru, gn_lru_g[l]), _rms_norm(y_nsa, gn_nsa_g[l])], axis=-1) @ w_out[l]
        x = _layer_norm(ALPHA * x + mix, ln1_g[l], ln1_b[l])
        x = _layer_norm(ALPHA * x + _peer(x, peer_wq[l], peer_subkeys[l], peer_u[l], peer_v[l]), ln2_g[l], ln2_b[l])
    return x


DEPTH_2 = 1

GRID_W = 64
CTX_LEN = 256
EPS = 1e-6
N_MOD = 6

MLA_V = 128
MLA_HEADS = D_MODEL // MLA_V
MLA_NOPE = 128
MLA_ROPE = 64
MLA_QK = MLA_NOPE + MLA_ROPE
MLA_Q_RANK = 3 * D_MODEL // 4
MLA_KV_RANK = D_MODEL // 4
MLA_WIDTH = MLA_HEADS * MLA_V
ROPE_BASE = 10000.0

HG_DK = 128
HG_HEADS = D_MODEL // HG_DK
HG_DV = D_MODEL // HG_HEADS
HG_FDIM = HG_HEADS * HG_DK
HG_WIDTH = HG_HEADS * HG_DV
HG_CHUNK = 64

N_EXPERTS_2 = 32
TOP_K = 4
D_EXPERT = D_MODEL
SWIGLU_LIMIT = 7.0
SWIGLU_ALPHA = 1.702
MOE_BLOCK = 128

IN_SPLITS_2 = (MLA_Q_RANK, MLA_KV_RANK + MLA_ROPE, HG_FDIM, HG_FDIM, HG_FDIM, HG_WIDTH, HG_WIDTH, D_MODEL, D_MODEL)
D_IN = MLA_Q_RANK + MLA_KV_RANK + MLA_ROPE + 3 * HG_FDIM + 2 * HG_WIDTH + 2 * D_MODEL


def rmsnorm(x, g):
    xf = x.astype(jnp.float32)
    y = xf * lax.rsqrt(jnp.mean(xf * xf, axis=-1, keepdims=True) + EPS)
    return (y * g.astype(jnp.float32)).astype(x.dtype)

def split_cols(p):
    return jnp.split(p, np.cumsum(IN_SPLITS_2)[:-1].tolist(), axis=-1)

def axial_rope_tables(rows):
    row = jnp.repeat(jnp.arange(rows), GRID_W).astype(jnp.float32)
    col = jnp.tile(jnp.arange(GRID_W), rows).astype(jnp.float32)
    n_freq = MLA_ROPE // 4
    inv = ROPE_BASE ** (-jnp.arange(n_freq, dtype=jnp.float32) / n_freq)
    ang = jnp.concatenate([row[:, None] * inv, col[:, None] * inv], axis=-1)
    return jnp.cos(ang), jnp.sin(ang)

def apply_rope(x, cos, sin):
    half = MLA_ROPE // 2
    x1 = x[..., :half].astype(jnp.float32)
    x2 = x[..., half:].astype(jnp.float32)
    return jnp.concatenate([x1 * cos - x2 * sin, x1 * sin + x2 * cos], axis=-1).astype(x.dtype)

def mla_queries(q_in, q_norm_g, w_q_b, cos, sin):
    b, n, _ = q_in.shape
    q = (rmsnorm(q_in, q_norm_g) @ w_q_b).reshape(b, n, MLA_HEADS, MLA_QK)
    q_nope, q_rope = q[..., :MLA_NOPE], q[..., MLA_NOPE:]
    if cos is not None:
        q_rope = apply_rope(q_rope, cos[:, None, :], sin[:, None, :])
    return jnp.concatenate([q_nope, q_rope], axis=-1)

def mla_keys_values(kv_in, kv_norm_g, w_kv_b, cos, sin):
    b, n, _ = kv_in.shape
    c_kv, k_rope = kv_in[..., :MLA_KV_RANK], kv_in[..., MLA_KV_RANK:]
    kv = (rmsnorm(c_kv, kv_norm_g) @ w_kv_b).reshape(b, n, MLA_HEADS, MLA_NOPE + MLA_V)
    k_nope, v = kv[..., :MLA_NOPE], kv[..., MLA_NOPE:]
    if cos is not None:
        k_rope = apply_rope(k_rope, cos, sin)
    k_rope = jnp.broadcast_to(k_rope[:, :, None, :], (b, n, MLA_HEADS, MLA_ROPE))
    return jnp.concatenate([k_nope, k_rope], axis=-1), v

def block_attention(q, k, v):
    b, n, h, dk = q.shape
    nb = n // Q_BLOCK
    scale = dk ** -0.5
    q_blocks = q.reshape(b, nb, Q_BLOCK, h, dk).transpose(1, 0, 2, 3, 4)

    def one_block(qb):
        s = jnp.einsum('bqhd,bkhd->bhqk', qb, k, preferred_element_type=jnp.float32) * scale
        p = jax.nn.softmax(s, axis=-1).astype(v.dtype)
        return jnp.einsum('bhqk,bkhd->bqhd', p, v)

    out = lax.map(one_block, q_blocks)
    return out.transpose(1, 0, 2, 3, 4).reshape(b, n, h * v.shape[-1])

def hgrn2_chunk_scan(q, k, v, log_f, s0):
    b, n, h, dk = q.shape
    dv = v.shape[-1]
    nc = n // HG_CHUNK

    def chunks(a):
        return a.reshape(b, nc, HG_CHUNK, h, a.shape[-1]).transpose(1, 0, 3, 2, 4)

    lower_tri = jnp.tril(jnp.ones((HG_CHUNK, HG_CHUNK), dtype=bool))[:, :, None]

    def step(state, inp):
        qc, kc, vc, gc = inp
        cum = jnp.cumsum(gc, axis=2)
        o_inter = jnp.einsum('bhtk,bhkv->bhtv', qc * jnp.exp(cum), state)
        rel = cum[:, :, :, None, :] - cum[:, :, None, :, :]
        decay = jnp.where(lower_tri, jnp.exp(jnp.minimum(rel, 0.0)), 0.0)
        att = jnp.einsum('bhtk,bhtsk,bhsk->bhts', qc, decay, kc)
        o_intra = jnp.einsum('bhts,bhsv->bhtv', att, vc)
        last = cum[:, :, -1:, :]
        state = jnp.exp(last[:, :, 0, :])[..., None] * state + jnp.einsum('bhsk,bhsv->bhkv', kc * jnp.exp(last - cum), vc)
        return state, o_inter + o_intra

    s_final, o = lax.scan(step, s0, (chunks(q), chunks(k), chunks(v), chunks(log_f)))
    return o.transpose(1, 0, 3, 2, 4).reshape(b, n, h, dv), s_final

def hgrn2_gates(z, lb):
    b, n = z.shape[:2]
    f = lb + (1.0 - lb) * jax.nn.sigmoid(z.astype(jnp.float32))
    return (1.0 - f).reshape(b, n, HG_HEADS, HG_DK), jnp.log(f).reshape(b, n, HG_HEADS, HG_DK)

def hgrn2_qv(p):
    b, n = p[2].shape[:2]
    q = (jax.nn.silu(p[2].astype(jnp.float32)) * HG_DK ** -0.5).reshape(b, n, HG_HEADS, HG_DK)
    v = p[5].astype(jnp.float32).reshape(b, n, HG_HEADS, HG_DV)
    return q, v

def hgrn2_readout(o, g, hg_norm_g):
    b, n = g.shape[:2]
    gate = jax.nn.silu(g.astype(jnp.float32)).reshape(b, n, HG_HEADS, HG_DV)
    return (rmsnorm(o, hg_norm_g) * gate).reshape(b, n, HG_WIDTH).astype(g.dtype)

def merge_branches(p, y_mla, y_hg, w_out):
    g_mla = jax.nn.sigmoid(p[7].astype(jnp.float32))
    g_hg = jax.nn.sigmoid(p[8].astype(jnp.float32))
    y = g_mla * y_mla.astype(jnp.float32) + g_hg * y_hg.astype(jnp.float32)
    return y.astype(p[7].dtype) @ w_out

def token_mixer(h_lat, h_ctx, cos, sin, lb_fwd, lb_bwd, w_in, q_norm_g, w_q_b, kv_norm_g, w_kv_b, hg_norm_g, w_out, with_ctx_out):
    lat = split_cols(h_lat @ w_in)
    ctx = split_cols(h_ctx @ w_in)
    k_lat, v_lat = mla_keys_values(lat[1], kv_norm_g, w_kv_b, cos, sin)
    k_ctx, v_ctx = mla_keys_values(ctx[1], kv_norm_g, w_kv_b, None, None)
    q_lat = mla_queries(lat[0], q_norm_g, w_q_b, cos, sin)
    y_mla_lat = block_attention(q_lat, jnp.concatenate([k_lat, k_ctx], axis=1), jnp.concatenate([v_lat, v_ctx], axis=1))
    q_l, v_l = hgrn2_qv(lat)
    q_c, v_c = hgrn2_qv(ctx)
    kf_l, gf_l = hgrn2_gates(lat[3], lb_fwd)
    kb_l, gb_l = hgrn2_gates(lat[4], lb_bwd)
    kf_c, gf_c = hgrn2_gates(ctx[3], lb_fwd)
    kb_c, gb_c = hgrn2_gates(ctx[4], lb_bwd)
    b = h_lat.shape[0]
    s0 = jnp.zeros((b, HG_HEADS, HG_DK, HG_DV), jnp.float32)
    flip = lambda a: jnp.flip(a, axis=1)
    o_cf, s_cf = hgrn2_chunk_scan(q_c, kf_c, v_c, gf_c, s0)
    o_cb, s_cb = hgrn2_chunk_scan(flip(q_c), flip(kb_c), flip(v_c), flip(gb_c), s0)
    o_lf, _ = hgrn2_chunk_scan(q_l, kf_l, v_l, gf_l, s_cf)
    o_lb, _ = hgrn2_chunk_scan(flip(q_l), flip(kb_l), flip(v_l), flip(gb_l), s_cb)
    y_hg_lat = hgrn2_readout(o_lf + flip(o_lb), lat[6], hg_norm_g)
    out_lat = merge_branches(lat, y_mla_lat, y_hg_lat, w_out)
    if not with_ctx_out:
        return out_lat, None
    q_ctx = mla_queries(ctx[0], q_norm_g, w_q_b, None, None)
    y_mla_ctx = block_attention(q_ctx, k_ctx, v_ctx)
    y_hg_ctx = hgrn2_readout(o_cf + flip(o_cb), ctx[6], hg_norm_g)
    return out_lat, merge_branches(ctx, y_mla_ctx, y_hg_ctx, w_out)

def moe_ffn(h, w_router, b_router, w_gate_up, b_gate_up, w_down, b_down):
    shp = h.shape
    t = h.reshape(-1, shp[-1])
    n_tok = t.shape[0]
    n_pair = n_tok * TOP_K
    logits = (t @ w_router + b_router).astype(jnp.float32)
    top_val, top_idx = lax.top_k(logits, TOP_K)
    probs = jax.nn.softmax(top_val, axis=-1)
    flat_e = top_idx.reshape(-1)
    flat_tok = jnp.arange(n_pair, dtype=jnp.int32) // TOP_K
    order = jnp.argsort(flat_e)
    sorted_e = flat_e[order]
    counts = jnp.bincount(flat_e, length=N_EXPERTS_2)
    padded = (counts + MOE_BLOCK - 1) // MOE_BLOCK * MOE_BLOCK
    start = jnp.cumsum(counts) - counts
    pad_end = jnp.cumsum(padded)
    pad_start = pad_end - padded
    dest_sorted = pad_start[sorted_e] + jnp.arange(n_pair, dtype=jnp.int32) - start[sorted_e]
    dest = jnp.zeros((n_pair,), jnp.int32).at[order].set(dest_sorted.astype(jnp.int32))
    n_rows = n_pair + N_EXPERTS_2 * MOE_BLOCK
    n_blocks = n_rows // MOE_BLOCK
    row_tok = jnp.full((n_rows,), n_tok, jnp.int32).at[dest].set(flat_tok)
    t_ext = jnp.concatenate([t, jnp.zeros((1, t.shape[-1]), t.dtype)], axis=0)
    x_rows = t_ext[row_tok].reshape(n_blocks, MOE_BLOCK, -1)
    block_start = jnp.arange(n_blocks, dtype=jnp.int32) * MOE_BLOCK
    block_e = jnp.minimum(jnp.searchsorted(pad_end, block_start, side='right'), N_EXPERTS_2 - 1)

    def expert_block(args):
        xb, e = args
        gu = xb @ w_gate_up[e] + b_gate_up[e]
        x_glu = jnp.minimum(gu[:, 0::2], SWIGLU_LIMIT)
        x_lin = jnp.clip(gu[:, 1::2], -SWIGLU_LIMIT, SWIGLU_LIMIT)
        act = x_glu * jax.nn.sigmoid(SWIGLU_ALPHA * x_glu) * (x_lin + 1)
        return act @ w_down[e] + b_down[e]

    y_rows = lax.map(expert_block, (x_rows, block_e)).reshape(n_rows, -1)
    y_pairs = y_rows[dest].reshape(n_tok, TOP_K, -1)
    out = jnp.einsum('tk,tkd->td', probs.astype(y_pairs.dtype), y_pairs)
    return out.reshape(shp)

def second_inputs(seed: int = 0) -> dict:
    key = jax.random.key(seed)
    ks = jax.random.split(key, 24)
    f32 = jnp.float32
    nrm = lambda k, shape, scale: jax.random.normal(k, shape, f32) * scale
    gain = lambda k, shape: 1.0 + 0.02 * jax.random.normal(k, shape, f32)
    return {
        'x': nrm(ks[0], (BATCH, SEQ, D_MODEL), 1.0),
        'c': nrm(ks[1], (BATCH, D_MODEL), 1.0),
        'ctx': nrm(ks[2], (BATCH, CTX_LEN, D_MODEL), 1.0),
        'c_ctx': nrm(ks[3], (D_MODEL,), 1.0),
        'w_mod': nrm(ks[4], (DEPTH_2, D_MODEL, N_MOD * D_MODEL), 0.5 * D_MODEL ** -0.5),
        'b_mod': nrm(ks[5], (DEPTH_2, N_MOD * D_MODEL), 0.02),
        'norm_mix_g': gain(ks[6], (DEPTH_2, D_MODEL)),
        'w_in': nrm(ks[7], (DEPTH_2, D_MODEL, D_IN), D_MODEL ** -0.5),
        'mla_q_norm_g': gain(ks[8], (DEPTH_2, MLA_Q_RANK)),
        'w_q_b': nrm(ks[9], (DEPTH_2, MLA_Q_RANK, MLA_HEADS * MLA_QK), MLA_Q_RANK ** -0.5),
        'mla_kv_norm_g': gain(ks[10], (DEPTH_2, MLA_KV_RANK)),
        'w_kv_b': nrm(ks[11], (DEPTH_2, MLA_KV_RANK, MLA_HEADS * (MLA_NOPE + MLA_V)), MLA_KV_RANK ** -0.5),
        'hg_lb_logits': nrm(ks[12], (2, DEPTH_2 + 1, HG_FDIM), 1.0),
        'hg_norm_g': gain(ks[13], (DEPTH_2, HG_DV)),
        'w_out': nrm(ks[14], (DEPTH_2, D_MODEL, D_MODEL), D_MODEL ** -0.5),
        'norm_ffn_g': gain(ks[15], (DEPTH_2, D_MODEL)),
        'w_router': nrm(ks[16], (DEPTH_2, D_MODEL, N_EXPERTS_2), D_MODEL ** -0.5),
        'b_router': nrm(ks[17], (DEPTH_2, N_EXPERTS_2), 0.01),
        'w_gate_up': nrm(ks[18], (DEPTH_2, N_EXPERTS_2, D_MODEL, 2 * D_EXPERT), D_MODEL ** -0.5),
        'b_gate_up': nrm(ks[19], (DEPTH_2, N_EXPERTS_2, 2 * D_EXPERT), 0.01),
        'w_down': nrm(ks[20], (DEPTH_2, N_EXPERTS_2, D_EXPERT, D_MODEL), D_EXPERT ** -0.5),
        'b_down': nrm(ks[21], (DEPTH_2, N_EXPERTS_2, D_MODEL), 0.01),
        'final_norm_g': gain(ks[22], (D_MODEL,)),
    }

def second_block(x, c, ctx, c_ctx, w_mod, b_mod, norm_mix_g, w_in, mla_q_norm_g, w_q_b, mla_kv_norm_g, w_kv_b, hg_lb_logits, hg_norm_g, w_out, norm_ffn_g, w_router, b_router, w_gate_up, b_gate_up, w_down, b_down, final_norm_g):
    rows = x.shape[1] // GRID_W
    cos, sin = axial_rope_tables(rows)
    lb = jnp.cumsum(jax.nn.softmax(hg_lb_logits.astype(jnp.float32), axis=1), axis=1)
    silu_c = jax.nn.silu(c)
    silu_cc = jax.nn.silu(c_ctx)
    n_ctx = ctx.shape[1]
    for l in range(DEPTH_2):
        last = l == DEPTH_2 - 1
        mod_lat = jnp.split((silu_c @ w_mod[l] + b_mod[l])[:, None, :], N_MOD, axis=-1)
        mod_ctx = jnp.split((silu_cc @ w_mod[l] + b_mod[l])[None, None, :], N_MOD, axis=-1)
        h_lat = rmsnorm(x, norm_mix_g[l]) * (1 + mod_lat[1]) + mod_lat[0]
        h_ctx = rmsnorm(ctx, norm_mix_g[l]) * (1 + mod_ctx[1]) + mod_ctx[0]
        mix_lat, mix_ctx = token_mixer(h_lat, h_ctx, cos, sin, lb[0, l], lb[1, l], w_in[l], mla_q_norm_g[l], w_q_b[l], mla_kv_norm_g[l], w_kv_b[l], hg_norm_g[l], w_out[l], not last)
        x = x + mod_lat[2] * mix_lat
        h_lat = rmsnorm(x, norm_ffn_g[l]) * (1 + mod_lat[4]) + mod_lat[3]
        if last:
            x = x + mod_lat[5] * moe_ffn(h_lat, w_router[l], b_router[l], w_gate_up[l], b_gate_up[l], w_down[l], b_down[l])
        else:
            ctx = ctx + mod_ctx[2] * mix_ctx
            h_ctx = rmsnorm(ctx, norm_ffn_g[l]) * (1 + mod_ctx[4]) + mod_ctx[3]
            y = moe_ffn(jnp.concatenate([h_ctx, h_lat], axis=1), w_router[l], b_router[l], w_gate_up[l], b_gate_up[l], w_down[l], b_down[l])
            ctx = ctx + mod_ctx[5] * y[:, :n_ctx]
            x = x + mod_lat[5] * y[:, n_ctx:]
    return rmsnorm(x, final_norm_g)


def setup_inputs(seed=0):
    out = dict(first_inputs(seed))
    for name, value in second_inputs(seed + 1).items():
        if name != "x":
            out[name + "_2"] = value
    return out


def reference(
    x, w_in, b_in, conv_w, conv_b, lru_wa, lru_ba, lru_wx, lru_bx, lru_lambda, cmp_pos_k,
    cmpk_w1, cmpk_b1, cmpk_w2, cmpk_b2, cmp_pos_v, cmpv_w1, cmpv_b1, cmpv_w2, cmpv_b2, gn_lru_g,
    gn_nsa_g, w_out, ln1_g, ln1_b, peer_wq, peer_subkeys, peer_u, peer_v, ln2_g, ln2_b, c_2,
    ctx_2, c_ctx_2, w_mod_2, b_mod_2, norm_mix_g_2, w_in_2, mla_q_norm_g_2, w_q_b_2,
    mla_kv_norm_g_2, w_kv_b_2, hg_lb_logits_2, hg_norm_g_2, w_out_2, norm_ffn_g_2, w_router_2,
    b_router_2, w_gate_up_2, b_gate_up_2, w_down_2, b_down_2, final_norm_g_2,
):
    x = first_block(
        x, w_in, b_in, conv_w, conv_b, lru_wa, lru_ba, lru_wx, lru_bx, lru_lambda, cmp_pos_k,
        cmpk_w1, cmpk_b1, cmpk_w2, cmpk_b2, cmp_pos_v, cmpv_w1, cmpv_b1, cmpv_w2, cmpv_b2,
        gn_lru_g, gn_nsa_g, w_out, ln1_g, ln1_b, peer_wq, peer_subkeys, peer_u, peer_v, ln2_g,
        ln2_b,
    )
    return second_block(
        x, c_2, ctx_2, c_ctx_2, w_mod_2, b_mod_2, norm_mix_g_2, w_in_2, mla_q_norm_g_2, w_q_b_2,
        mla_kv_norm_g_2, w_kv_b_2, hg_lb_logits_2, hg_norm_g_2, w_out_2, norm_ffn_g_2,
        w_router_2, b_router_2, w_gate_up_2, b_gate_up_2, w_down_2, b_down_2, final_norm_g_2,
    )


_drawn_inputs = setup_inputs


def setup_inputs(seed=0):
    import zlib

    import numpy as np

    out = dict(_drawn_inputs(seed))
    spreads = {}
    factors = {'lru_ba': 8.0,
     'lru_bx': 7.646,
     'cmp_pos_k': 7.918,
     'cmpk_b1': 8.0,
     'cmpk_b2': 200.0,
     'cmpv_b1': 3.554,
     'gn_lru_g': 3.535,
     'gn_nsa_g': 3.478,
     'ctx_2': 3.578,
     'norm_mix_g_2': 8.0,
     'mla_q_norm_g_2': 8.0,
     'mla_kv_norm_g_2': 8.0,
     'hg_lb_logits_2': 4.856,
     'hg_norm_g_2': 6.984,
     'norm_ffn_g_2': 16.516,
     'b_router_2': 33.584,
     'b_gate_up_2': 64.0,
     'b_down_2': 200.0,
     'final_norm_g_2': 27.806}
    for name, (base, spread) in spreads.items():
        noise = np.random.default_rng([zlib.crc32(name.encode()), seed]).standard_normal(out[name].shape)
        drawn = base * np.exp(spread * noise) if base else spread * noise
        out[name] = jnp.asarray(drawn.astype(out[name].dtype))
    for name, factor in factors.items():
        out[name] = (out[name] * factor).astype(out[name].dtype)
    return out
```

```python
from contextlib import ExitStack

import numpy as np
import concourse.bass as bass
from concourse import mybir

F32 = mybir.dt.float32
BF16 = mybir.dt.bfloat16
U32 = mybir.dt.uint32
ALU = mybir.AluOpType
ACT = mybir.ActivationFunctionType
AX = mybir.AxisListType

ALPHA = 4.0 ** 0.25
NSLOT = 4
PIECE = 4096
LEVELS = [64, 32, 16, 8, 4, 2, 1]

C_ID, C_ONE, C_IOTA, C_I16, C_PERM, C_VAL, C_E5, C_E6, C_CB, C_MF, C_MB, C_COS, C_SIN = (
    0, 128, 256, 384, 400, 528, 529, 530, 531, 771, 1027, 1283, 1539)
NC_COLS = 1795
(P_BIN, P_CW, P_CB, P_BA, P_BX, P_LAM, P_POSK, P_POSV, P_B1K, P_B2K, P_B1V, P_GL, P_GN, P_B2V, P_BTOK,
 P_W2K, P_W2V, P_SK, P_WA, P_WX) = (0, 16, 32, 36, 40, 44, 48, 80, 112, 113, 114, 115, 119, 123, 187,
                                    467, 595, 659, 915, 1427)
NP_COLS = 1939
(Q_CC, Q_BMOD, Q_NMG, Q_QNG, Q_KVG, Q_LBL, Q_HGN, Q_NFG, Q_BR, Q_WR, Q_BGU, Q_FNG) = (
    0, 16, 64, 72, 78, 80, 112, 113, 121, 153, 409, 921)
NQ_COLS = 929


class Queue:

    def __init__(self, sem, in_order):
        self.sem, self.in_order, self.n, self.ops, self.fence = sem, in_order, 0, [], []

    def do(self, fn, *waits, inc=True):
        w = list(waits) + self.fence
        self.fence = []
        if self.in_order and self.n:
            w.append((self.sem, self.n))
        self.ops.append((w, fn, inc))
        if inc:
            self.n += 1
        return (self.sem, self.n + (not inc))

    def last(self):
        return (self.sem, self.n)

    def emit(self, eng):
        seen = {}

        def wait(w):
            if w is None:
                return
            if isinstance(w, list):
                for x in w:
                    wait(x)
                return
            s, v = w
            if v > seen.get(s, 0):
                eng.wait_ge(s, v)
                seen[s] = v

        for w, fn, inc in self.ops:
            wait(w)
            r = fn(eng)
            if inc:
                r.then_inc(self.sem, 1)


class Held:

    def __init__(self, ap):
        self.ap, self.ready, self.free = ap, None, []


def bc(ap, axis, n):
    ap = ap.unsqueeze(axis)
    shape = list(ap.shape)
    shape[axis] = n
    return ap.broadcast_to(shape)


def build(nc, d, out):
    with ExitStack() as ctx:
        def sb(name, cols, dt=F32):
            return ctx.enter_context(nc.sbuf_tensor(name, [128, cols], dt))

        def sem(name):
            return ctx.enter_context(nc.semaphore(name))

        P = Queue(sem("s_pe"), False)
        V = Queue(sem("s_dve"), True)
        A = Queue(sem("s_act"), True)
        G = Queue(sem("s_pool"), True)
        S = []
        ring = sb("ring", NSLOT * PIECE)
        s_ring = [sem(f"s_ring{i}") for i in range(NSLOT)]
        xtok = sb("xtok", 2048)
        xT_t = sb("xT", 2048)
        cst = sb("cst", NC_COLS)
        pp = sb("pp", NP_COLS)
        ARENA = (212000 - 4 * (NSLOT * PIECE + 4096 + NC_COLS + NP_COLS)) // 4 // 8 * 8
        arena = sb("arena", ARENA)
        banks = [Held(ctx.enter_context(nc.psum_tensor(f"bank{i}", [128, 512], F32))) for i in range(8)]
        x3 = xtok[:, :].rearrange("p (t n) -> p t n", t=2)
        xT = xT_t[:, :].rearrange("p (c t) -> p c t", c=8)

        top = [0]

        def fence():
            toks = [q.last() for q in (P, V, A, G)]
            for q in (P, V, A, G):
                q.fence = q.fence + toks
            top[0] = 0
            return toks

        def ar(cols, dt=F32):
            a = top[0]
            top[0] += (cols + 7) // 8 * 8
            assert top[0] <= ARENA, (top[0], ARENA)
            return arena[:, a:a + cols]

        def ar3(a, b):
            return ar(a * b).rearrange("p (a b) -> p a b", a=a)

        def ar4(a, b, c):
            return ar(a * b * c).rearrange("p (a b c) -> p a b c", a=a, b=b)

        uses = [[] for _ in range(NSLOT)]
        n_load = [0]

        def load(src, cols):
            i = n_load[0] % NSLOT
            n_load[0] += 1
            h = Held(ring[:, i * PIECE:i * PIECE + cols])
            prev = uses[i][-1] if uses[i] else None
            uses[i].append(h)
            h.ready = (s_ring[i], 16 * len(uses[i]))
            S.append((prev.free if prev else [], h.ap, src, s_ring[i]))
            return h

        n_once = [0]

        def load_once(dst, src, waits=()):
            n_once[0] += 1
            s = sem(f"s_once{n_once[0]}")
            S.append((list(waits), dst, src, s))
            return (s, 16)

        s_out = sem("s_out")
        n_out = [0]

        def store(dst, src, *waits):
            n_out[0] += 16
            S.append((list(waits), dst, src, s_out))


        rot = {"n": 0, "set": list(range(8))}

        def bank():
            b = banks[rot["set"][rot["n"] % len(rot["set"])]]
            rot["n"] += 1
            return b

        def mm(b, o, pairs, *waits):
            w = list(waits) + [list(b.free)] if b is not None else list(waits)
            n = len(pairs)
            t = None
            for i, (l, r) in enumerate(pairs):
                t = P.do(lambda e, l=l, r=r, i=i: e.matmul(o, l, r, start=(i == 0), stop=(i == n - 1)),
                         *(w if i == 0 else ()), inc=(i == n - 1))
            return t

        def tr(b, o, src, *waits):
            n = src.shape[0]
            return P.do(lambda e: e.transpose(o, src, ident[0:n, 0:n]), *waits, list(b.free))

        def act(o, i, f, *w, bias=None, scale=1.0, acc=None):
            kw = {}
            if bias is not None:
                kw["bias"] = bias
            if acc is not None:
                kw["accum_out"] = acc
            return A.do(lambda e: e.activation(o, i, f, scale=scale, **kw), *w)

        def tt(o, a, b, op, *w, q=None):
            return (q or V).do(lambda e: e.tensor_tensor(o, a, b, op), *w)

        def ts(o, a, s1, s2, o1, o2, *w, q=None):
            if o2 is None:
                return (q or V).do(lambda e: e.tensor_scalar(o, a, s1, None, o1), *w)
            return (q or V).do(lambda e: e.tensor_scalar(o, a, s1, s2, o1, o2), *w)

        def stt(o, a, s, b, o1, o2, *w):
            return V.do(lambda e: e.scalar_tensor_tensor(out=o, in0=a, scalar=s, in1=b, op0=o1, op1=o2), *w)

        def cp(o, i, *w, q=None):
            return (q or V).do(lambda e: e.tensor_copy(o, i), *w)

        def red(o, i, op, *w, neg=False):
            return V.do(lambda e: e.tensor_reduce(o, i, AX.X, op, negate=neg), *w)

        def recip(o, i, *w):
            return V.do(lambda e: e.reciprocal(o, i), *w)

        MUL, ADD, SUB, MAX, MIN, EQ = ALU.mult, ALU.add, ALU.subtract, ALU.max, ALU.min, ALU.is_equal

        ident = cst[:, C_ID:C_ID + 128]
        ones = cst[:, C_ONE:C_ONE + 128]
        iota = cst[:, C_IOTA:C_IOTA + 128]
        t_cst = load_once(cst[:, :], d["cst"])
        t_x = load_once(x3, d["x"].rearrange("(t p) n -> p t n", p=128))
        t_xT = load_once(xT, d["xT"].rearrange("(c p) t -> p c t", p=128))
        for q in (P, V, A, G):
            q.fence = [t_cst, t_x, t_xT]

        def transposes(dst4, src, n, *waits, evac=None):
            last = None
            for a in range(0, n, 4):
                b = bank()
                k = min(4, n - a)
                for j in range(k):
                    t = tr(b, b.ap[:, j * 128:j * 128 + 128], src(a + j), *(waits if a == 0 and j == 0 else ()))
                last = evac(a, k, b.ap[:, 0:k * 128].rearrange("p (k t) -> p k t", k=k), t)
                b.free = [last]
            return last

        def layer_norm(z, g_ap, b_ap, st, mv, dst, *w):
            for t in range(2):
                for h in range(2):
                    V.do(lambda e, t=t, h=h: e.bn_stats(st[:, 2 * t + h, :], z[:, t, h * 512:h * 512 + 512]), *w)
                V.do(lambda e, t=t: e.bn_aggr(mv[:, t, 0:2], st[:, 2 * t:2 * t + 2, :]))
            act(mv[:, :, 2:3], mv[:, :, 1:2], ACT.Sqrt, V.last(), bias=cst[:, C_E5:C_E5 + 1])
            recip(mv[:, :, 3:4], mv[:, :, 2:3], A.last())
            for t in range(2):
                ts(z[:, t, :], z[:, t, :], mv[:, t, 0:1], mv[:, t, 3:4], SUB, MUL)
            tt(z, z, bc(g_ap, 1, 2), MUL)
            return tt(dst, z, bc(b_ap, 1, 2), ADD)

        def to_xT(src3, waits):
            def evac(a, k, ps, t):
                tk, c0 = a // 8, a % 8
                return cp(xT[:, c0:c0 + k, tk * 128:tk * 128 + 128], ps, t) if (a // 4) % 2 else \
                    act(xT[:, c0:c0 + k, tk * 128:tk * 128 + 128], ps, ACT.Copy, t)
            transposes(None, lambda i: src3[:, i // 8, (i % 8) * 128:(i % 8) * 128 + 128], 16, *waits, evac=evac)

        def mixing(l, t_pp):
            fence()
            xpad = ar3(4, 259)
            gT = ar3(4, 256)
            qT = ar3(4, 256)
            kT = ar3(4, 256)
            vtok = ar3(2, 256)
            gates = ar3(2, 24)
            alibi = ar3(8, 256)
            t_al = load_once(alibi, d["alibi"].rearrange("p (h k) -> p h k", h=8),
                             [q.last() for q in (P, V, A, G)])

            def par(c, n=1):
                return pp[:, c:c + n]

            V.do(lambda e: e.memset(xpad[:, :, 0:3], 0.0))
            cw = []
            for j in range(4):
                pc = load(d["w_inA"][l, j], 4096)
                w = pc.ap.rearrange("p (c n) -> p c n", c=8)
                for half in range(2):
                    b = bank()
                    for k in range(2):
                        ct = half * 2 + k
                        t = mm(b, b.ap[:, k * 256:k * 256 + 256],
                               [(w[:, dc, ct * 128:ct * 128 + 128], xT[:, dc, :]) for dc in range(8)],
                               pc.ready, t_pp)
                    for k in range(2):
                        ct = half * 2 + k
                        dst = [xpad[:, ct, 3:259], gT[:, ct, :], qT[:, ct, :], kT[:, ct, :]][j]
                        src = b.ap[:, k * 256:k * 256 + 256]
                        if half:
                            e1 = ts(dst, src, par(P_BIN + 4 * j + ct), None, ADD, None, t, t_pp)
                        else:
                            e1 = act(dst, src, ACT.Identity, t, t_pp, bias=par(P_BIN + 4 * j + ct))
                    b.free = [e1]
                pc.free = [t]
            pc = load(d["w_inB"][l], 2240)
            w = pc.ap.rearrange("p (c n) -> p c n", c=8)
            for tk in range(2):
                b = bank()
                t = mm(b, b.ap[:, 0:280], [(xT[:, dc, tk * 128:tk * 128 + 128], w[:, dc, :]) for dc in range(8)],
                       pc.ready)
                tt(vtok[:, tk, :], b.ap[:, 0:256], par(P_BTOK, 256), ADD, t)
                tt(gates[:, tk, :], b.ap[:, 256:280], par(P_BTOK + 256, 24), ADD)
                b.free = [V.last()]
            pc.free = [t]
            act(gates, gates, ACT.Sigmoid, V.last())

            xc = ar3(4, 256)
            r = ar3(4, 256)
            ig = ar3(4, 256)
            aa = ar3(4, 256)
            th = ar3(4, 256)
            sp = ar(32)
            t_x = A.last()
            lam = par(P_LAM, 4)
            ts(sp[:, 0:4], lam, -1.0, None, MUL, None)
            tt(sp[:, 4:8], lam, sp[:, 0:4], MIN)
            act(sp[:, 8:12], sp[:, 4:8], ACT.Exp, V.last())
            ts(sp[:, 12:16], sp[:, 8:12], 2.0, None, ADD, None, A.last())
            recip(sp[:, 16:20], sp[:, 12:16])
            tt(sp[:, 12:16], sp[:, 8:12], sp[:, 16:20], MUL)
            tt(sp[:, 16:20], sp[:, 12:16], sp[:, 12:16], MUL)
            V.do(lambda e: e.memset(sp[:, 20:24], 2.0 / 17))
            for c in (15, 13, 11, 9, 7, 5, 3, 1):
                tt(sp[:, 20:24], sp[:, 20:24], sp[:, 16:20], MUL)
                ts(sp[:, 20:24], sp[:, 20:24], 2.0 / c, None, ADD, None)
            tt(sp[:, 20:24], sp[:, 20:24], sp[:, 12:16], MUL)
            ts(sp[:, 0:4], sp[:, 0:4], 0.0, None, MAX, None)
            tt(sp[:, 20:24], sp[:, 20:24], sp[:, 0:4], ADD)
            ts(sp[:, 20:24], sp[:, 20:24], -8.0, None, MUL, None)
            for ct in range(4):
                for j in range(4):
                    src = xpad[:, ct, j:j + 256]
                    wj = par(P_CW + 4 * j + ct)
                    if j == 0:
                        ts(xc[:, ct, :], src, wj, par(P_CB + ct), MUL, ADD, t_x)
                    else:
                        stt(xc[:, ct, :], src, wj, xc[:, ct, :], MUL, ADD)
            t_xc = V.last()
            for wcol, bcol, dst in ((P_WA, P_BA, r), (P_WX, P_BX, ig)):
                for ct in range(4):
                    b = bank()
                    t = mm(b, b.ap[:, 0:256], [(par(wcol + 128 * ct, 128), xc[:, ct, :])], t_xc)
                    b.free = [act(dst[:, ct, :], b.ap[:, 0:256], ACT.Sigmoid, t, bias=par(bcol + ct))]
            t_ri = A.last()
            for ct in range(4):
                ts(r[:, ct, :], r[:, ct, :], sp[:, 20 + ct:21 + ct], None, MUL, None, t_ri)
            tt(ig, ig, xc, MUL)
            t1 = V.last()
            act(th, r, ACT.Tanh, t1, scale=-1.0)
            act(aa, r, ACT.Exp)
            t2 = A.last()
            ts(r, th, 1.0, None, ADD, None, t2)
            recip(r, r)
            tt(r, r, th, MUL)
            act(th, r, ACT.Sqrt, V.last(), scale=2.0)
            tt(ig, ig, th, MUL, A.last())
            for ct in range(4):
                V.do(lambda e, ct=ct: e.tensor_tensor_scan(xc[:, ct, :], aa[:, ct, :], ig[:, ct, :], 0.0, MUL, ADD))
            act(gT, gT, ACT.Gelu_apprx_tanh)
            tt(xc, xc, gT, MUL, A.last())
            tt(th, xc, xc, MUL)
            ylT = xpad[:, :, 0:256]
            for ct in range(4):
                ts(ylT[:, ct, :], xc[:, ct, :], par(P_GL + ct), None, MUL, None)
            t_yl = V.last()
            ss = ar(16)
            b = bank()
            for tk in range(2):
                t = mm(b, b.ap[:, tk:tk + 1], [(th[:, ct, tk * 128:tk * 128 + 128], ones[:, 0:1]) for ct in range(4)],
                       t_yl)
            act(ss[:, 0:2], b.ap[:, 0:2], ACT.Sqrt, t, scale=1.0 / 512, bias=cst[:, C_E5:C_E5 + 1])
            b.free = [A.last()]
            recip(ss[:, 2:4], ss[:, 0:2], A.last())

            gk = ar(32)
            kcT = ar(16)
            vc = ar(128)
            kp = xc[:, 0:2, :].rearrange("p a b -> p (a b)")[:, 0:480].rearrange("p (c j) -> p c j", j=32)
            kz = ar(32 * 30).rearrange("p (j g c) -> p j g c", j=32, g=2)
            P_w = V.last()
            for n, (pos, b1, w2) in enumerate(((P_POSK, P_B1K, P_W2K), (P_POSV, P_B1V, P_W2V))):
                pc = load(d["cmp_w1"][l, n], 2048)
                w1 = pc.ap.rearrange("p (j e) -> p j e", j=32)
                V.do(lambda e: e.memset(kz, 0.0), P.last())
                for hf in range(2):
                    win = kT[:, n, hf * 16:hf * 16 + 240].rearrange("p (c j) -> p j c", j=16)
                    for g in range(2):
                        s = slice(64 * g, 64 * g + 64)
                        tt(kz[s, hf * 16:hf * 16 + 16, g, :], win[s, :, :],
                           bc(par(pos + hf * 16, 16), 2, 15)[s, :, :], ADD)
                b = bank()
                t = mm(b, b.ap[0:64, 0:30], [(w1[:, j, :], kz[:, j, :, :]) for j in range(32)], pc.ready, V.last())
                pc.free = [t]
                act(gk[0:64, 0:30], b.ap[0:64, 0:30], ACT.Gelu_apprx_tanh, t, bias=pp[0:64, b1:b1 + 1])
                b.free = [A.last()]
                if n == 0:
                    b = bank()
                    t = mm(b, b.ap[:, 0:30], [(pp[0:64, w2:w2 + 128], gk[0:64, 0:30])], A.last())
                    for g in range(2):
                        s = slice(64 * g, 64 * g + 64)
                        ts(kcT[s, 0:15], b.ap[s, 15 * g:15 * g + 15], pp[s, P_B2K:P_B2K + 1], None, ADD, None, t)
                    b.free = [V.last()]
                else:
                    b = bank()
                    for g in range(2):
                        t = mm(b, b.ap[0:15, 64 * g:64 * g + 64],
                               [(gk[0:64, 15 * g:15 * g + 15], pp[0:64, w2:w2 + 64])], A.last())
                    tt(vc[0:15, :].rearrange("p (g d) -> p g d", g=2),
                       b.ap[0:15, 0:128].rearrange("p (g d) -> p g d", g=2),
                       bc(pp[0:15, P_B2V:P_B2V + 64], 1, 2), ADD, t)
                    b.free = [V.last()]
            t_c = V.last()

            s_ = ar3(8, 256)
            pT = ar4(2, 8, 128)
            osum = ar3(2, 512)
            tmp = ar(512).rearrange("p (h d) -> p h d", h=8)
            st = ar(64)
            for tk in range(2):
                for br in range(3):
                    nk = 15 if br == 0 else 128 * (tk + 1)
                    per = 4 if br == 0 else 2
                    bs = []
                    for g in range(2):
                        for j0 in range(0, 4, per):
                            b = bank()
                            for jj in range(per):
                                j = j0 + jj
                                sl = slice(64 * g, 64 * g + 64)
                                key = kcT[sl, 0:15] if br == 0 else kT[sl, 1 + br, 0:nk]
                                t = mm(b, b.ap[:, jj * nk:jj * nk + nk], [(qT[sl, j, tk * 128:tk * 128 + 128], key)], t_c)
                            bias = cst[:, C_CB + tk * 120:C_CB + tk * 120 + 120].rearrange("p (h c) -> p h c", h=8) \
                                if br == 0 else alibi[:, :, 256 - nk:256]
                            h0 = 4 * g + j0
                            stt(s_[:, h0:h0 + per, 0:nk], b.ap[:, 0:per * nk].rearrange("p (h k) -> p h k", h=per), 0.125,
                                bias[:, h0:h0 + per, :], MUL, ADD, t, t_al, A.last(), P.last() if h0 == 0 else None)
                            b.free = [V.last()]
                    red(st[:, 0:8], s_[:, :, 0:nk], MAX, neg=True)
                    t = V.last()
                    for h in range(8):
                        act(s_[:, h, 0:nk], s_[:, h, 0:nk], ACT.Exp, t, bias=st[:, h:h + 1],
                            acc=st[:, 8 + h:9 + h])
                    t_p = A.last()
                    recip(st[:, 16:24], st[:, 8:16], t_p)
                    tt(st[:, 24:32], st[:, 16:24], gates[:, tk, br:24:3], MUL)
                    if br == 0 and tk == 0:
                        ts(st[:, 24:32], st[:, 24:32], cst[:, C_VAL:C_VAL + 1], None, MUL, None)
                    b_o = bank()
                    if br == 0:
                        for h0 in (0, 4):
                            b = bank()
                            for h in range(h0, h0 + 4):
                                t = tr(b, b.ap[0:15, (h - h0) * 128:(h - h0) * 128 + 128], s_[:, h, 0:15], t_p)
                            cp(pT[0:15, 0, h0:h0 + 4, :], b.ap[0:15, :].rearrange("p (h t) -> p h t", h=4), t)
                            b.free = [V.last()]
                        for h in range(8):
                            g = h // 4
                            t = mm(b_o, b_o.ap[:, h * 64:h * 64 + 64],
                                   [(pT[0:15, 0, h, :], vc[0:15, 64 * g:64 * g + 64])], V.last())
                    else:
                        for kt in range(tk + 1):
                            for h0 in (0, 4):
                                b = bank()
                                for h in range(h0, h0 + 4):
                                    t = tr(b, b.ap[:, (h - h0) * 128:(h - h0) * 128 + 128],
                                           s_[:, h, kt * 128:kt * 128 + 128], t_p)
                                cp(pT[:, kt, h0:h0 + 4, :], b.ap[:, :].rearrange("p (h t) -> p h t", h=4), t)
                                b.free = [V.last()]
                        vo = (br - 1) * 128
                        for h in range(8):
                            g = h // 4
                            t = mm(b_o, b_o.ap[:, h * 64:h * 64 + 64],
                                   [(pT[:, kt, h, :], vtok[:, kt, vo + 64 * g:vo + 64 * g + 64]) for kt in range(tk + 1)],
                                   V.last())
                    o3 = osum[:, tk, :].rearrange("p (h d) -> p h d", h=8)
                    dst = o3 if br == 0 else tmp
                    tt(dst, b_o.ap[:, :].rearrange("p (h d) -> p h d", h=8), bc(st[:, 24:32], 2, 64), MUL, t)
                    b_o.free = [V.last()]
                    if br:
                        tt(o3, o3, tmp, ADD)
                V.do(lambda e, tk=tk: e.tensor_tensor_reduce(
                    tmp.rearrange("p h d -> p (h d)"), osum[:, tk, :], osum[:, tk, :], 1.0, 0.0, MUL, ADD,
                    ss[:, 4 + tk:5 + tk]))
            act(ss[:, 6:8], ss[:, 4:6], ACT.Sqrt, V.last(), scale=1.0 / 512, bias=cst[:, C_E5:C_E5 + 1])
            recip(ss[:, 8:10], ss[:, 6:8], A.last())
            ynT = qT
            t_o = V.last()
            for tk in range(2):
                b = bank()
                for c in range(4):
                    t = tr(b, b.ap[:, c * 128:c * 128 + 128], osum[:, tk, c * 128:c * 128 + 128], t_o)
                for c in range(4):
                    ts(ynT[:, c, tk * 128:tk * 128 + 128], b.ap[:, c * 128:c * 128 + 128], par(P_GN + c), None,
                       MUL, None, t)
                b.free = [V.last()]
            t_yn = V.last()
            z = s_.rearrange("p h k -> p (h k)").rearrange("p (t n) -> p t n", t=2)
            lst = ar3(4, 6)
            mv = ar3(2, 4)
            ln = load(d["ln"][l, 0].partition_broadcast(128), 2048)
            pcs = [load(d["w_out"][l, k], 4096) for k in range(2)]
            ts(z, x3, ALPHA, None, MUL, None, A.last(), P.last())
            for k, yT in ((0, ylT), (1, ynT)):
                w = pcs[k].ap.rearrange("p (c n) -> p c n", c=4)
                for tk in range(2):
                    for dh in range(2):
                        b = bank()
                        t = mm(b, b.ap[:, :], [(yT[:, c, tk * 128:tk * 128 + 128], w[:, c, dh * 512:dh * 512 + 512])
                                               for c in range(4)], pcs[k].ready, t_yn)
                        zz = z[:, tk, dh * 512:dh * 512 + 512]
                        sc = ss[:, 2 + tk:3 + tk] if k == 0 else ss[:, 8 + tk:9 + tk]
                        stt(zz, b.ap[:, :], sc, zz, MUL, ADD, t)
                        b.free = [V.last()]
                pcs[k].free = [t]
            layer_norm(z, ln.ap[:, 0:1024], ln.ap[:, 1024:2048], lst, mv, x3, ln.ready)
            ln.free = [V.last()]
            to_xT(x3, [V.last()])

        def peer(l):
            fence()
            rot["set"] = list(range(8))
            eg = ar4(3, 2, 128).rearrange("p k t n -> p k (t n)")
            gs = ar4(3, 1, 256).rearrange("p k o n -> p k (o n)")
            gsb = ar(384).bitcast(BF16).rearrange("p (k n) -> p k n", k=3)
            gel = [Held(ar(256)) for _ in range(4)]
            pt = [Held(ar(256)) for _ in range(4)]
            Aoh = [Held(ar(1024).bitcast(BF16).rearrange("p (t a) -> p t a", t=16)) for _ in range(2)]
            Boh = [Held(ar(768).bitcast(BF16).rearrange("p (k t b) -> p k t b", k=3, t=16)) for _ in range(2)]
            eqb = ar(512).rearrange("p (t b) -> p t b", t=16)
            mark = top[0]
            qT = ar3(16, 256)
            s_ = ar4(2, 16, 128)
            sk = pp[:, P_SK:P_SK + 256].rearrange("p (c k) -> p c k", c=2)
            for j in range(4):
                pc = load(d["peer_wq"][l, j], 4096)
                w = pc.ap.rearrange("p (c n) -> p c n", c=8)
                for hf in range(2):
                    b = bank()
                    for k in range(2):
                        ct = hf * 2 + k
                        t = mm(b, b.ap[:, k * 256:k * 256 + 256],
                               [(w[:, dc, ct * 128:ct * 128 + 128], xT[:, dc, :]) for dc in range(8)],
                               pc.ready, A.last(), V.last())
                    b.free = [act(qT[:, 4 * j + 2 * hf:4 * j + 2 * hf + 2, :],
                                  b.ap[:, :].rearrange("p (k t) -> p k t", k=2), ACT.Copy, t)]
                pc.free = [t]
            t_q = A.last()
            for tk in range(2):
                for h4 in range(4):
                    b = bank()
                    for k in range(4):
                        hc = 4 * h4 + k
                        t = mm(b, b.ap[:, k * 128:k * 128 + 128],
                               [(qT[:, hc, tk * 128:tk * 128 + 128], sk[:, hc % 2, :])], t_q)
                    b.free = [act(s_[:, tk, 4 * h4:4 * h4 + 4, :], b.ap[:, :].rearrange("p (k t) -> p k t", k=4),
                                  ACT.Copy, t)]
            t_s = A.last()
            t_pp_free = P.last()
            work = ar(256)
            sv = ar(256).rearrange("p (h c k) -> p h c k", h=8, c=2)
            si = ar(256).bitcast(U32).rearrange("p (h c k) -> p h c k", h=8, c=2)
            sif = ar(256).rearrange("p (h c k) -> p h c k", h=8, c=2)
            cand = ar(2048).rearrange("p (h a b) -> p h a b", h=8, a=16)
            cv = ar3(8, 16)
            ci = ar(128).bitcast(U32).rearrange("p (h k) -> p h k", h=8)
            cj = ar(256).bitcast(U32).rearrange("p (c n) -> p c n", c=2)
            cf = ar(256).rearrange("p (c h k) -> p c h k", c=2, h=8)
            ea = ar(384).rearrange("p (c n) -> p c n", c=3)
            sm = ar(32)

            def top16(src, vals, idx, wk):
                V.do(lambda e: e.max(vals[:, 0:8], src))
                V.do(lambda e: e.max_index(idx[:, 0:8], vals[:, 0:8], src))
                V.do(lambda e: e.match_replace(wk, vals[:, 0:8], src, -3.0e38))
                V.do(lambda e: e.max(vals[:, 8:16], wk))
                V.do(lambda e: e.max_index(idx[:, 8:16], vals[:, 8:16], wk))

            V.fence = V.fence + [t_s]
            for tk in range(2):
                for hc in range(16):
                    top16(s_[:, tk, hc, :], sv[:, hc // 2, hc % 2, :], si[:, hc // 2, hc % 2, :], work[:, 0:128])
                cp(sif, si)
                tt(cand, bc(sv[:, :, 0, :], 3, 16), bc(sv[:, :, 1, :], 2, 16), ADD)
                for h in range(8):
                    top16(cand[:, h, :, :].rearrange("p a b -> p (a b)"), cv[:, h, :], ci[:, h, :], work)
                ts(cj[:, 0, :], ci.rearrange("p h k -> p (h k)"), 4, None, ALU.logical_shift_right, None)
                ts(cj[:, 1, :], ci.rearrange("p h k -> p (h k)"), 15, None, ALU.bitwise_and, None)
                cp(cf.rearrange("p c h k -> p c (h k)"), cj)
                for c in range(2):
                    eq = cand.rearrange("p h a b -> p (h a) b")
                    tt(eq, bc(cf[:, c, :, :].rearrange("p h k -> p (h k)"), 2, 16),
                       bc(cst[:, C_I16:C_I16 + 16], 1, 128), EQ)
                    tt(cand, cand, bc(sif[:, :, c, :], 2, 16), MUL)
                    red(ea[:, c, :], eq, ADD)
                cp(sm[:, 16:24], cv[:, :, 0])
                tt(cv, cv, bc(sm[:, 16:24], 2, 16), SUB, A.last())
                g3 = ea[:, 2, :].rearrange("p (h k) -> p h k", h=8)
                act(g3, cv, ACT.Exp, V.last())
                red(sm[:, 0:8], g3, ADD, A.last())
                recip(sm[:, 8:16], sm[:, 0:8])
                tt(g3, g3, bc(sm[:, 8:16], 2, 16), MUL)
                b = bank()
                for c in range(3):
                    t = tr(b, b.ap[:, c * 128:c * 128 + 128], ea[:, c, :], V.last())
                cp(eg[:, :, tk * 128:tk * 128 + 128], b.ap[:, 0:384].rearrange("p (c t) -> p c t", c=3), t)
                b.free = [V.last()]
            cp(gsb[:, 0, :], eg[:, 2, :])
            cp(gs[:, 0, :], gsb[:, 0, :])
            tt(eg[:, 2, :], eg[:, 2, :], gs[:, 0, :], SUB)
            cp(gsb[:, 1, :], eg[:, 2, :])
            cp(gs[:, 1, :], gsb[:, 1, :])
            tt(gs[:, 2, :], eg[:, 2, :], gs[:, 1, :], SUB)
            t_g = V.last()
            toks = fence()
            top[0] = mark
            Gq = [Held(ar3(32, 256)) for _ in range(2)]
            acc = [banks[i] for i in range(4)]
            bG = [banks[4], banks[5]]
            bU = [banks[6], banks[7]]

            def build_group(q, tg):
                n = q * 16 + tg
                ah, bh, g = Aoh[n % 2], Boh[n % 2], Gq[q % 2]
                t0 = tg * 16
                ah.ready = tt(ah.ap, bc(iota, 1, 16), bc(eg[:, 0, t0:t0 + 16], 2, 128), EQ, list(ah.free), t_g)
                tt(eqb, bc(iota[:, q * 32:q * 32 + 32], 1, 16), bc(eg[:, 1, t0:t0 + 16], 2, 32), EQ)
                for k in range(3):
                    tt(bh.ap[:, k, :, :], eqb, bc(gs[:, k, t0:t0 + 16], 2, 32), MUL, list(bh.free))
                t_b = V.last()
                b = bG[n % 2]
                for i in range(16):
                    t = mm(b if i == 0 else None, b.ap[:, i * 32:i * 32 + 32],
                           [(ah.ap[:, i, :], bh.ap[:, k, i, :]) for k in range(3)], ah.ready, t_b)
                ah.free, bh.free = [t], [t]
                g.ready = act(g.ap[:, :, t0:t0 + 16].rearrange("p b t -> p t b"),
                              b.ap[:, :].rearrange("p (t b) -> p t b", t=16), ACT.Copy, t, list(g.free))
                b.free = [A.last()]

            for tg in range(16):
                build_group(0, tg)
            up = {}

            def stage1(c):
                if c % 4 == 0:
                    up["u"] = load(d["peer_u"][l, c // 4], 4096)
                    up["v", c // 4] = load(d["peer_v"][l, c // 4], 4096)
                u = up["u"]
                w = u.ap.rearrange("p (i c a) -> p i c a", i=4, c=8)
                b = bU[c % 2]
                t = mm(b, b.ap[:, 0:256], [(w[:, c % 4, dc, :], xT[:, dc, :]) for dc in range(8)], u.ready)
                if c % 4 == 3:
                    u.free = [t]
                ge, p_, g = gel[c % 4], pt[c % 4], Gq[(c // 32) % 2]
                ge.ready = act(ge.ap, b.ap[:, 0:256], ACT.Gelu_apprx_tanh, t, list(ge.free))
                b.free = [A.last()]
                p_.ready = tt(p_.ap, ge.ap, g.ap[:, c % 32, :], MUL, ge.ready, g.ready, list(p_.free))
                ge.free = [V.last()]
                if c % 32 == 31:
                    g.free = [V.last()]

            def stage2(c):
                v = up["v", c // 4]
                w = v.ap.rearrange("p (i n) -> p i n", i=4)
                p_ = pt[c % 4]
                for tk in range(2):
                    for dh in range(2):
                        b = acc[2 * tk + dh]
                        t = P.do(lambda e, b=b, tk=tk, dh=dh: e.matmul(
                            b.ap[:, :], p_.ap[:, tk * 128:tk * 128 + 128], w[:, c % 4, dh * 512:dh * 512 + 512],
                            start=(c == 0), stop=(c == 127)), p_.ready, v.ready, list(b.free) if c == 0 else None,
                            inc=(tk == 1 and dh == 1))
                p_.free = [t]
                if c % 4 == 3:
                    v.free = [t]
                return t

            for c in range(130):
                if c < 128:
                    stage1(c)
                    q = c // 32 + 1
                    if q < 4 and c % 2 == 1:
                        build_group(q, (c % 32) // 2)
                if c >= 2:
                    t = stage2(c - 2)
            z = Gq[0].ap.rearrange("p b t -> p (b t)")[:, 0:2048].rearrange("p (t n) -> p t n", t=2)
            lst = Gq[1].ap[:, 0, 0:24].rearrange("p (a b) -> p a b", a=4)
            mv = Gq[1].ap[:, 1, 0:8].rearrange("p (a b) -> p a b", a=2)
            ln = load(d["ln"][l, 1].partition_broadcast(128), 2048)
            for tk in range(2):
                for dh in range(2):
                    b = acc[2 * tk + dh]
                    stt(z[:, tk, dh * 512:dh * 512 + 512], x3[:, tk, dh * 512:dh * 512 + 512], ALPHA, b.ap[:, :],
                        MUL, ADD, t)
                    b.free = [V.last()]
            layer_norm(z, ln.ap[:, 0:1024], ln.ap[:, 1024:2048], lst, mv, x3, ln.ready)
            ln.free = [V.last()]
            rot["n"] = 0
            to_xT(x3, [V.last()])
            return t_pp_free

        def second():
            toks = fence()
            rot["set"] = list(range(8))
            t_qq = load_once(pp[:, 0:NQ_COLS], d["qq"], toks)
            for q in (P, V, A, G):
                q.fence = q.fence + [t_qq]
            keep = [0]

            def kp_(n):
                a = keep[0]
                keep[0] += n
                assert keep[0] <= 2048
                return xtok[:, a:a + n]

            def par(c, n=1):
                return pp[:, c:c + n]

            mod = kp_(96).rearrange("p (j v) -> p j v", v=2)
            coef = kp_(40).rearrange("p (k c) -> p k c", k=5)
            lb = kp_(64).rearrange("p (k d h) -> p k d h", k=4, d=2)
            sc = kp_(16)
            eps6 = cst[:, C_E6:C_E6 + 1]

            act(sc, par(Q_CC, 16), ACT.Silu)
            t_sc = A.last()
            bm = bank()
            for j in range(12):
                pc = load(d["w_mod"][j], 4096)
                w = pc.ap.rearrange("p (c n) -> p c n", c=8)
                for ct in range(4):
                    o = 2 * (4 * j + ct)
                    t = mm(bm, bm.ap[:, o:o + 2], [(w[:, dc, ct * 128:ct * 128 + 128], sc[:, 2 * dc:2 * dc + 2])
                                                   for dc in range(8)], pc.ready, t_sc)
                pc.free = [t]
            tt(mod, bm.ap[:, 0:96].rearrange("p (j v) -> p j v", v=2), bc(par(Q_BMOD, 48), 2, 2), ADD, t)
            bm.free = [V.last()]
            for k, (g, j, v) in enumerate(((Q_NMG, 8, 0), (Q_NMG, 8, 1), (Q_NFG, 32, 0))):
                stt(coef[:, k, :], mod[:, j:j + 8, v], 1.0, par(g, 8), ADD, MUL)
            l0, l1 = [pp[:, Q_LBL:Q_LBL + 32].rearrange("p (d e h) -> p d e h", d=2, e=2)[:, :, k, :] for k in (0, 1)]
            tt(lb[:, 0, :, :], l0, l1, MAX)
            tt(lb[:, 1, :, :], l0, lb[:, 0, :, :], SUB)
            tt(lb[:, 2, :, :], l1, lb[:, 0, :, :], SUB)
            act(lb[:, 1:3, :, :], lb[:, 1:3, :, :], ACT.Exp, V.last())
            tt(lb[:, 2, :, :], lb[:, 1, :, :], lb[:, 2, :, :], ADD, A.last())
            recip(lb[:, 3, :, :], lb[:, 2, :, :])
            tt(lb[:, 0, :, :], lb[:, 1, :, :], lb[:, 3, :, :], MUL)
            ts(lb[:, 1, :, :], lb[:, 0, :, :], -1.0, 1.0, MUL, ADD)

            def rms(src, n, cnt, dst, sq):
                c = src.shape[1]
                tt(sq, src, src, MUL)
                b = bank()
                t = mm(b, b.ap[:, 0:n], [(ones, sq[:, i, :]) for i in range(c)], V.last())
                act(dst, b.ap[:, 0:n], ACT.Sqrt, t, scale=1.0 / cnt, bias=eps6)
                b.free = [A.last()]
                return recip(dst, dst, A.last())

            def modulated(dst, src, k, shift, v, rstd, sq):
                rms(src, 256, 1024, rstd, sq)
                tt(sq, src, bc(rstd, 1, 8), MUL)
                for c in range(8):
                    ts(dst[:, c, :], sq[:, c, :], coef[:, k, c:c + 1], mod[:, shift + c, v:v + 1], MUL, ADD)

            ym = ar3(8, 256)
            hT = ar3(8, 512)
            rstd = ar(512)
            mark0 = top[0]
            sq = ar3(8, 256)
            cT = ar3(8, 256)
            t_c = load_once(cT, d["ctxT"].rearrange("(c p) t -> p c t", p=128), toks)
            modulated(hT[:, :, 0:256], xT, 0, 0, 0, rstd[:, 0:256], sq)
            V.fence = V.fence + [t_c]
            modulated(hT[:, :, 256:512], cT, 1, 0, 1, rstd[:, 256:512], sq)
            t_h = V.last()
            fence()
            top[0] = mark0

            def project(src, n_ct, n, evac, ndc=8, rhs=None):
                pc = load(src, ndc * n_ct * 128)
                w = pc.ap.rearrange("p (c n) -> p c n", c=ndc)
                r = rhs if rhs is not None else hT
                for ct in range(n_ct):
                    b = bank()
                    t = mm(b, b.ap[:, 0:n], [(w[:, dc, ct * 128:ct * 128 + 128], r[:, dc, 0:n]) for dc in range(ndc)],
                           pc.ready, V.last() if ct == 0 else None, A.last() if ct == 0 else None)
                    b.free = [evac(ct, b.ap[:, 0:n], t)]
                pc.free = [t]

            qn = ar3(8, 256)
            qr = ar3(8, 256)
            kn = ar3(8, 512)
            kr = ar(512)
            va = ar3(4, 1024)
            mark1 = top[0]
            qin = ar3(6, 256)
            ckv = ar3(2, 512)
            sq6 = ar3(6, 256)
            sw = ar(512)
            for j in range(2):
                project(d["w_q"][j], 3, 256, lambda ct, ps, t, j=j: act(qin[:, 3 * j + ct, :], ps, ACT.Copy, t))

            def ev_kv(ct, ps, t):
                return act(ckv[:, ct, :] if ct < 2 else kr, ps, ACT.Copy, t)

            project(d["w_kv"], 3, 512, ev_kv)
            V.fence = V.fence + [A.last()]
            rms(qin, 256, 768, rstd[:, 0:256], sq6)
            tt(qin, qin, bc(rstd[:, 0:256], 1, 6), MUL)
            for c in range(6):
                ts(qin[:, c, :], qin[:, c, :], par(Q_QNG + c), None, MUL, None)
            sqk = sq6.rearrange("p c t -> p (c t)")[:, 0:1024].rearrange("p (c t) -> p c t", c=2)
            rms(ckv, 512, 256, rstd, sqk)
            tt(ckv, ckv, bc(rstd, 1, 2), MUL)
            for c in range(2):
                ts(ckv[:, c, :], ckv[:, c, :], par(Q_KVG + c), None, MUL, None)

            perm = cst[:, C_PERM:C_PERM + 128]
            cos, sin = cst[:, C_COS:C_COS + 256], cst[:, C_SIN:C_SIN + 256]

            def rope(src, dsts, t):
                b = bank()
                t = mm(b, b.ap[:, 0:256], [(perm, src)], t)
                tt(sw[:, 0:256], b.ap[:, 0:256], sin, MUL, t)
                b.free = [V.last()]
                tt(sw[:, 256:512], src, cos, MUL)
                for s, o in dsts:
                    r = tt(o, sw[s, 0:256], sw[s, 256:512], ADD)
                return r

            lo, hi, al = slice(0, 64), slice(64, 128), slice(0, 128)
            rope(kr[:, 0:256], [(al, kr[:, 0:256])], A.last())
            V.do(lambda e: e.memset(qr, 0.0))
            for j in range(2):
                project(d["w_qb_n"][j], 4, 256, lambda ct, ps, t, j=j: act(qn[:, 4 * j + ct, :], ps, ACT.Copy, t),
                        ndc=6, rhs=qin)
            qrs = sq6

            project(d["w_qb_r"], 4, 256, lambda ct, ps, t: act(qrs[:, ct, :], ps, ACT.Copy, t), ndc=6, rhs=qin)
            for j in range(4):
                rope(qrs[:, j, :], [(lo, qr[lo, 2 * j, :]), (hi, qr[hi, 2 * j + 1, :])], A.last())
            pc = load(d["w_kvb"], 4096)
            w = pc.ap.rearrange("p (v c n) -> p v c n", v=2, c=2)
            for h in range(8):
                b = bank()
                t = mm(b, b.ap[:, :], [(w[:, 0, c, h * 128:h * 128 + 128], ckv[:, c, :]) for c in range(2)],
                       pc.ready, V.last())
                b.free = [act(kn[:, h, :], b.ap[:, :], ACT.Copy, t)]
            for k in range(4):
                for hf in range(2):
                    b = bank()
                    t = mm(b, b.ap[:, :], [(ckv[:, c, k * 128:k * 128 + 128], w[:, 1, c, hf * 512:hf * 512 + 512])
                                           for c in range(2)])
                    b.free = [cp(va[:, k, hf * 512:hf * 512 + 512], b.ap[:, :], t)]
            pc.free = [t]
            t_kv = [A.last(), V.last()]
            top[0] = mark1
            for q in (P, V, A):
                q.fence = q.fence + [P.last()] + t_kv
            pb = [Held(ar(512)) for _ in range(2)]
            pT = [Held(ar3(4, 256)) for _ in range(2)]
            st = ar(128)
            SC = 192.0 ** -0.5
            for h in range(8):
                pt_ = pT[h % 2]
                for tk in range(2):
                    n = 2 * h + tk
                    p_ = pb[n % 2]
                    ts_ = slice(tk * 128, tk * 128 + 128)
                    b = bank()
                    t = mm(b, b.ap[:, :], [(qn[:, h, ts_], kn[:, h, :]), (qr[:, h, ts_], kr)], t_kv)
                    c = 4 * n
                    red(st[:, c:c + 1], b.ap[:, :], MAX, t, neg=True)
                    ts(st[:, c + 1:c + 2], st[:, c:c + 1], SC, None, MUL, None)
                    act(p_.ap, b.ap[:, :], ACT.Exp, V.last(), list(p_.free), bias=st[:, c + 1:c + 2], scale=SC,
                        acc=st[:, c + 2:c + 3])
                    b.free = [A.last()]
                    recip(st[:, c + 3:c + 4], st[:, c + 2:c + 3], A.last())
                    ts(p_.ap, p_.ap, st[:, c + 3:c + 4], None, MUL, None)
                    t_n = V.last()
                    b = bank()
                    for k in range(4):
                        t = tr(b, b.ap[:, k * 128:k * 128 + 128], p_.ap[:, k * 128:k * 128 + 128], t_n)
                    p_.free = [t]
                    b.free = [cp(pt_.ap[:, :, ts_], b.ap[:, :].rearrange("p (k t) -> p k t", k=4), t, list(pt_.free))]
                b = bank()
                t = mm(b, b.ap[:, 0:256], [(va[:, k, h * 128:h * 128 + 128], pt_.ap[:, k, :]) for k in range(4)], V.last())
                pt_.free = [t]
                b.free = [act(ym[:, h, :], b.ap[:, 0:256], ACT.Copy, t)]
            fence()
            top[0] = mark0
            gsig = ar3(4, 256)
            for j in range(2):
                project(d["w_hg"][10 + j], 4, 256, lambda ct, ps, t: act(gsig[:, ct, :], ps, ACT.Sigmoid, t, V.last()))
                tt(ym[:, 4 * j:4 * j + 4, :], ym[:, 4 * j:4 * j + 4, :], gsig, MUL, A.last())
            fence()
            top[0] = mark0
            hm = ar4(2, 8, 128)
            t_hm = load_once(hm, d["hmask"].rearrange("r p (l t) -> p r l t", l=8), [q.last() for q in (P, V, A, G)])
            qh = ar3(4, 256)
            vh = ar3(4, 512)
            fk = ar4(2, 4, 256)
            gg = ar4(2, 4, 256)
            cum = ar4(2, 4, 256)
            kd = ar4(3, 4, 128)
            kdT = ar4(3, 4, 128)
            S2 = ar3(4, 128)
            S3 = ar3(4, 128)
            att = ar3(8, 128)
            Eb = [Held(ar(1024)) for _ in range(2)]
            qc = ar3(4, 256)
            ob = ar3(4, 256)
            gate = ar3(4, 256)
            sm = ar(32)
            nE = [0]
            for hh in range(2):
                def all_done():
                    w = [q.last() for q in (P, V, A)]
                    for q in (P, V, A):
                        q.fence = q.fence + w

                all_done()
                project(d["w_hg"][hh], 4, 256, lambda ct, ps, t: act(qh[:, ct, :], ps, ACT.Silu, t))
                ts(qh, qh, 128.0 ** -0.5, None, MUL, None, A.last())
                pc = load(d["w_hg"][6 + hh], 4096)
                w = pc.ap.rearrange("p (c n) -> p c n", c=8)
                for k in range(4):
                    b = bank()
                    t = mm(b, b.ap[:, :], [(hT[:, dc, k * 128:k * 128 + 128], w[:, dc, :]) for dc in range(8)], pc.ready)
                    b.free = [cp(vh[:, k, :], b.ap[:, :], t)]
                pc.free = [t]
                for r in range(2):
                    all_done()

                    def ev_f(ct, ps, t):
                        return act(fk[:, :, ct, :], ps.rearrange("p (s t) -> p s t", s=2), ACT.Sigmoid, t)

                    project(d["w_hg"][2 + 2 * r + hh], 4, 512, ev_f)
                    for c in range(4):
                        h = 4 * hh + c
                        ts(fk[:, :, c, :], fk[:, :, c, :], lb[:, 1, r, h:h + 1], lb[:, 0, r, h:h + 1], MUL, ADD, A.last())
                    act(gg, fk, ACT.Ln, V.last())
                    ts(fk, fk, -1.0, 1.0, MUL, ADD, A.last())
                    msk = cst[:, (C_MF, C_MB)[r]:(C_MF, C_MB)[r] + 256]
                    for s in range(2):
                        for c in range(4):
                            o, m, g = cum[:, s, c, :], msk, gg[:, s, c, :]
                            if r:
                                o, m, g = o[:, ::-1], m[:, ::-1], g[:, ::-1]
                            V.do(lambda e, o=o, m=m, g=g: e.tensor_tensor_scan(o, m, g, 0.0, MUL, ADD))
                    fst, last = (0, 127) if r == 0 else (1, 0)
                    ta = [(1, fst), (1, 1 - fst), (0, fst)]
                    for i, (s, k) in enumerate(ta):
                        cp(sm[:, 4 * i:4 * i + 4], cum[:, s, :, 128 * k + last])
                    act(sm[:, 16:20], sm[:, 8:12], ACT.Exp, V.last())
                    tt(sm[:, 0:4], sm[:, 0:4], sm[:, 4:8], ADD)
                    for i, (s, k) in enumerate(ta):
                        tt(kd[:, i, :, :], bc(sm[:, 4 * i:4 * i + 4], 2, 128), cum[:, s, :, 128 * k:128 * k + 128], SUB)
                    act(kd, kd, ACT.Exp, V.last())
                    act(qc, cum[:, 0, :, :], ACT.Exp)
                    for i, (s, k) in enumerate(ta):
                        tt(kd[:, i, :, :], kd[:, i, :, :], fk[:, s, :, 128 * k:128 * k + 128], MUL, A.last())
                    tt(qc, qc, qh, MUL)
                    t_k = V.last()
                    for i in range(3):
                        b = bank()
                        for c in range(4):
                            t = tr(b, b.ap[:, c * 128:c * 128 + 128], kd[:, i, c, :], t_k)
                        b.free = [act(kdT[:, i, :, :], b.ap[:, :].rearrange("p (c k) -> p c k", c=4), ACT.Copy, t)]
                    b2, b3 = bank(), bank()
                    for c in range(4):
                        cs = slice(c * 128, c * 128 + 128)
                        t2 = mm(b2, b2.ap[:, cs], [(kdT[:, i, c, :], vh[:, 2 + ta[i][1], cs]) for i in range(2)], A.last())
                        t3 = mm(b3, b3.ap[:, cs], [(kdT[:, 2, c, :], vh[:, fst, cs])], A.last())
                    cp(S2, b2.ap[:, :].rearrange("p (c v) -> p c v", c=4), t2)
                    b2.free = [V.last()]
                    for c in range(4):
                        stt(S3[:, c, :], S2[:, c, :], sm[:, 16 + c:17 + c], b3.ap[:, c * 128:c * 128 + 128], MUL, ADD, t3)
                    b3.free = [V.last()]
                    V.do(lambda e: e.memset(att, 0.0))
                    C = cum[:, 0, :, :].rearrange("p h t -> p (h t)")
                    K = fk[:, 0, :, :].rearrange("p h t -> p (h t)")
                    Q = qh.rearrange("p h t -> p (h t)")
                    t_kq = V.last()
                    for lv in [7] + list(range(7)):
                        if lv < 7:
                            w_ = LEVELS[lv]

                            def blk(x):
                                return x.rearrange("p (n t) -> p n t", t=2 * w_)

                            eb = Eb[nE[0] % 2]
                            nE[0] += 1
                            e3, c3 = blk(eb.ap), blk(C)
                            f, s = slice(0, w_), slice(w_, 2 * w_)
                            if r == 0:
                                ref = c3[:, :, w_ - 1:w_].broadcast_to([128, 512 // w_, w_])
                                tt(e3[:, :, f], ref, c3[:, :, f], SUB, list(eb.free), t_kq, q=G)
                                tt(e3[:, :, s], c3[:, :, s], ref, SUB, q=G)
                            else:
                                ref = c3[:, :, w_:w_ + 1].broadcast_to([128, 512 // w_, w_])
                                tt(e3[:, :, f], c3[:, :, f], ref, SUB, list(eb.free), t_kq, q=G)
                                tt(e3[:, :, s], ref, c3[:, :, s], SUB, q=G)
                            act(eb.ap, eb.ap, ACT.Exp, G.last())
                            x1, x2 = (K, Q) if r == 0 else (Q, K)
                            tt(e3[:, :, f], e3[:, :, f], blk(x1)[:, :, f], MUL, A.last())
                            tt(e3[:, :, s], e3[:, :, s], blk(x2)[:, :, s], MUL)
                            ls = rs = eb.ap
                        else:
                            ls, rs = K, Q
                        t_e = V.last()
                        for u0 in (0, 4):
                            b = bank()
                            for u in range(u0, u0 + 4):
                                us = slice(u * 128, u * 128 + 128)
                                t = mm(b, b.ap[:, (u - u0) * 128:(u - u0) * 128 + 128], [(ls[:, us], rs[:, us])], t_e)
                            V.do(lambda e, u0=u0, b=b, lv=lv, r=r: e.copy_predicated(
                                att[:, u0:u0 + 4, :], bc(hm[:, r, lv, :].bitcast(U32), 1, 4),
                                b.ap[:, :].rearrange("p (u t) -> p u t", u=4)), t, t_hm)
                            b.free = [V.last()]
                        if lv < 7:
                            eb.free = [t]
                    for c0 in (0, 2):
                        b = bank()
                        for c in (c0, c0 + 1):
                            for k in range(2):
                                o = (c - c0) * 256 + k * 128
                                t = mm(b, b.ap[:, o:o + 128],
                                       [(vh[:, k, c * 128:c * 128 + 128], att[:, 2 * c + k, :]),
                                        ((S2 if k == fst else S3)[:, c, :], qc[:, c, k * 128:k * 128 + 128])], V.last())
                        o3 = ob[:, c0:c0 + 2, :]
                        ps = b.ap[:, :].rearrange("p (c t) -> p c t", c=2)
                        b.free = [cp(o3, ps, t) if r == 0 else tt(o3, o3, ps, ADD, t)]
                all_done()
                o2 = Eb[0].ap.rearrange("p (c t) -> p c t", c=4)
                rs_ = Eb[1].ap.rearrange("p (c t) -> p c t", c=4)
                tt(o2, ob, ob, MUL)
                t_o2 = V.last()
                for c0 in (0, 2):
                    b = bank()
                    t = mm(b, b.ap[:, :], [(ones, o2[:, c0:c0 + 2, :])], t_o2)
                    act(rs_[:, c0:c0 + 2, :], b.ap[:, :].rearrange("p (c t) -> p c t", c=2), ACT.Sqrt, t,
                        scale=1.0 / 128, bias=eps6)
                    b.free = [A.last()]
                recip(rs_, rs_, A.last())
                tt(ob, ob, rs_, MUL)
                project(d["w_hg"][8 + hh], 4, 256, lambda ct, ps, t: act(gate[:, ct, :], ps, ACT.Silu, t))
                stt(ob, ob, par(Q_HGN), gate, MUL, MUL, A.last())
                project(d["w_hg"][12 + hh], 4, 256, lambda ct, ps, t: act(gate[:, ct, :], ps, ACT.Sigmoid, t, V.last()))
                tt(ob, ob, gate, MUL, A.last())
                tt(ym[:, 4 * hh:4 * hh + 4, :], ym[:, 4 * hh:4 * hh + 4, :], ob, ADD)
            t_y = V.last()
            for j in range(2):
                def ev_o(ct, ps, t, j=j):
                    c = 4 * j + ct
                    return stt(xT[:, c, :], ps, mod[:, 16 + c, 0:1], xT[:, c, :], MUL, ADD, t)

                project(d["w_o2"][j], 4, 256, ev_o, rhs=ym)
            toks = fence()
            h2 = ar3(8, 256)
            bd = ar(1024)
            gTt = ar(256)
            lg = ar3(2, 32)
            gd = ar3(2, 32)
            tv = ar(32)
            ti = ar(16).bitcast(U32)
            tf = ar(32)
            rstd = ar(256)
            sq = ar3(8, 256)
            aT = [Held(ar3(8, 256)) for _ in range(2)]
            gb = [Held(ar(256)) for _ in range(2)]
            gl = [Held(ar(256)) for _ in range(2)]
            ll = [Held(ar(256)) for _ in range(2)]
            sg = [Held(ar(256)) for _ in range(2)]
            V.do(lambda e: e.memset(bd, 0.0))
            V.do(lambda e: e.memset(gTt, 0.0))
            t_bd = load_once(bd[0:32, :], d["b_dn"], [V.last()])
            modulated(h2, xT, 2, 24, 0, rstd, sq)
            t_h2 = V.last()
            wr = par(Q_WR, 256).rearrange("p (c n) -> p c n", c=8)
            for tk in range(2):
                b = bank()
                t = mm(b, b.ap[:, 0:32], [(h2[:, dc, tk * 128:tk * 128 + 128], wr[:, dc, :]) for dc in range(8)], t_h2)
                tt(lg[:, tk, :], b.ap[:, 0:32], par(Q_BR, 32), ADD, t)
                b.free = [V.last()]
                V.do(lambda e, tk=tk: e.max(tv[:, 0:8], lg[:, tk, :]))
                V.do(lambda e, tk=tk: e.max_index(ti[:, 0:8], tv[:, 0:8], lg[:, tk, :]))
                cp(tf[:, 0:8], ti[:, 0:8])
                ts(tv[:, 8:9], tv[:, 0:1], -1.0, None, MUL, None)
                act(tv[:, 16:20], tv[:, 0:4], ACT.Exp, V.last(), bias=tv[:, 8:9], acc=tv[:, 20:21])
                recip(tv[:, 21:22], tv[:, 20:21], A.last())
                ts(tv[:, 16:20], tv[:, 16:20], tv[:, 21:22], None, MUL, None)
                for k in range(4):
                    o = gd[:, tk, :] if k == 0 else lg[:, tk, :]
                    ts(o, iota[:, 0:32], tf[:, k:k + 1], tv[:, 16 + k:17 + k], EQ, MUL)
                    if k:
                        tt(gd[:, tk, :], gd[:, tk, :], lg[:, tk, :], ADD)
                b = bank()
                t = tr(b, b.ap[0:32, 0:128], gd[:, tk, :], V.last())
                cp(gTt[0:32, tk * 128:tk * 128 + 128], b.ap[0:32, 0:128], t)
                b.free = [V.last()]
            t_g = V.last()
            acc = banks[0:4]
            rot["set"] = [5, 6, 7]
            for tk in range(2):
                for dh in range(2):
                    b = acc[2 * tk + dh]
                    P.do(lambda e, b=b, tk=tk, dh=dh: e.matmul(
                        b.ap[:, :], gTt[:, tk * 128:tk * 128 + 128], bd[:, dh * 512:dh * 512 + 512],
                        start=True, stop=False), t_g, t_bd, list(b.free))

            def up(e):
                g = gb[e % 2]
                b = banks[4]
                t = mm(b, b.ap[:, 0:256], [(ident[:, e:e + 1].broadcast_to([128, 128]), gTt)], t_g)
                act(g.ap, b.ap[:, 0:256], ACT.Copy, t, list(g.free))
                b.free = [A.last()]
                g.ready = A.last()
                a = aT[e % 2]
                for ft in range(8):
                    if ft % 2 == 0:
                        pc = load(d["w_gu"][e, ft // 2], 4096)
                        w = pc.ap.rearrange("p (f v c n) -> p f v c n", f=2, v=2, c=8)
                    b = bank()
                    for v in range(2):
                        t = mm(b, b.ap[:, v * 256:v * 256 + 256],
                               [(w[:, ft % 2, v, dc, :], h2[:, dc, :]) for dc in range(8)], pc.ready)
                    if ft % 2:
                        pc.free = [t]
                    x, y, z = gl[ft % 2], ll[ft % 2], sg[ft % 2]
                    bcol = Q_BGU + 16 * e + 2 * ft
                    ts(x.ap, b.ap[:, 0:256], par(bcol), 7.0, ADD, MIN, t)
                    t_x = V.last()
                    ts(y.ap, b.ap[:, 256:512], par(bcol + 1), 7.0, ADD, MIN)
                    b.free = [V.last()]
                    act(z.ap, x.ap, ACT.Sigmoid, t_x, list(z.free), scale=1.702)
                    ts(y.ap, y.ap, -7.0, 1.0, MAX, ADD)
                    tt(y.ap, y.ap, g.ap, MUL, g.ready)
                    tt(y.ap, y.ap, x.ap, MUL)
                    tt(a.ap[:, ft, :], y.ap, z.ap, MUL, A.last(), list(a.free) if ft == 0 else None)
                    z.free = [V.last()]
                g.free = [V.last()]
                a.ready = V.last()

            def down(e):
                a = aT[e % 2]
                for hf in range(2):
                    pc = load(d["w_dn"][e, hf], 4096)
                    w = pc.ap.rearrange("p (f n) -> p f n", f=4)
                    for f in range(4):
                        for tk in range(2):
                            for dh in range(2):
                                b = acc[2 * tk + dh]
                                end = hf == 1 and f == 3
                                t = P.do(lambda q, b=b, f=f, tk=tk, dh=dh, w=w, hf=hf, end=end: q.matmul(
                                    b.ap[:, :], a.ap[:, 4 * hf + f, tk * 128:tk * 128 + 128],
                                    w[:, f, dh * 512:dh * 512 + 512], start=False, stop=(e == 31 and end)),
                                    pc.ready, a.ready, inc=(f == 3))
                    pc.free = [t]
                a.free = [t]
                return t

            for e in range(33):
                if e < 32:
                    up(e)
                if e >= 1:
                    t = down(e - 1)
            toks = fence()
            rot["set"] = [4, 5, 6, 7]
            rot["n"] = 0
            m = ar3(2, 1024)
            for tk in range(2):
                for dh in range(2):
                    cp(m[:, tk, dh * 512:dh * 512 + 512], acc[2 * tk + dh].ap[:, :], t)
            t_m = V.last()

            def ev_m(a_, k, ps, t):
                tk, c0 = a_ // 8, a_ % 8
                for i in range(k):
                    o = xT[:, c0 + i, tk * 128:tk * 128 + 128]
                    r = stt(o, ps[:, i, :], mod[:, 40 + c0 + i, 0:1], o, MUL, ADD, t)
                return r

            transposes(None, lambda i: m[:, i // 8, (i % 8) * 128:(i % 8) * 128 + 128], 16, t_m, evac=ev_m)
            rstd = ar(256)
            sq = ar3(8, 256)
            rms(xT, 256, 1024, rstd, sq)
            for c in range(8):
                stt(sq[:, c, :], xT[:, c, :], par(Q_FNG + c), rstd, MUL, MUL)
            t_f = V.last()

            def ev_y(a_, k, ps, t):
                tk, c0 = a_ // 8, a_ % 8
                o = m[:, tk, c0 * 128:(c0 + k) * 128].rearrange("p (k t) -> p k t", k=k)
                return cp(o, ps, t)

            transposes(None, lambda i: sq[:, i % 8, (i // 8) * 128:(i // 8) * 128 + 128], 16, t_f, evac=ev_y)
            store(out.rearrange("(t p) n -> p t n", p=128), m, V.last())

        free_pp = []
        for l in range(2):
            t_pp = load_once(pp[:, :], d["pp"][l], free_pp)
            mixing(l, t_pp)
            free_pp = [peer(l)]
        second()

        block = ctx.enter_context(nc.Block())

        @block.sync
        def _(e):
            seen = {}

            def wait(w):
                if w is None:
                    return
                if isinstance(w, list):
                    for x in w:
                        wait(x)
                    return
                if w[1] > seen.get(w[0], 0):
                    e.wait_ge(*w)
                    seen[w[0]] = w[1]

            for w, dst, src, s in S:
                wait(list(w))
                e.dma_start(dst, src).then_inc(s, 16)
            if n_out[0]:
                e.wait_ge(s_out, n_out[0])

        @block.tensor
        def _(e):
            P.emit(e)

        @block.vector
        def _(e):
            V.emit(e)

        @block.scalar
        def _(e):
            A.emit(e)

        @block.gpsimd
        def _(e):
            G.emit(e)



def _constants():
    c = np.zeros((128, NC_COLS), np.float32)
    i = np.arange(128)
    c[:, C_ID:C_ID + 128] = np.eye(128)
    c[:, C_ONE:C_ONE + 128] = 1.0
    c[:, C_IOTA:C_IOTA + 128] = i[None, :]
    c[:, C_I16:C_I16 + 16] = np.arange(16)[None, :]
    c[i, C_PERM + (i // 64) * 64 + (i % 64 + 32) % 64] = 1.0
    c[:, C_VAL] = i >= 31
    c[:, C_E5] = 1e-5
    c[:, C_E6] = 1e-6
    slopes = np.array([2.0 ** (-8.0 * (h + 1) / 8) for h in range(8)], np.float32)
    end = np.arange(15) * 16 + 31
    for tk in range(2):
        t = tk * 128 + i
        dist = (t[:, None] - end[None, :]).astype(np.float32)
        b = np.where(dist[:, None, :] >= 0, -slopes[None, :, None] * np.abs(dist)[:, None, :], np.float32(-1e30))
        c[:, C_CB + tk * 120:C_CB + tk * 120 + 120] = b.reshape(128, 120)
    t = np.arange(256)
    c[:, C_MF:C_MF + 256] = (t % 128 != 0)[None, :]
    c[:, C_MB:C_MB + 256] = (t % 128 != 127)[None, :]
    inv = np.float32(10000.0) ** (-np.arange(16, dtype=np.float32) / np.float32(16))
    ang = np.concatenate([(t // 64).astype(np.float32)[:, None] * inv, (t % 64).astype(np.float32)[:, None] * inv], -1)
    cos, sin = np.cos(ang).astype(np.float32).T, np.sin(ang).astype(np.float32).T
    c[:, C_COS:C_COS + 256] = np.concatenate([cos, cos, cos, cos])
    c[:, C_SIN:C_SIN + 256] = np.concatenate([-sin, sin, -sin, sin])
    dist = 128 + i[:, None] - t[None, :]
    alibi = np.where(dist[:, None, :] >= 0, -slopes[None, :, None] * dist[:, None, :].astype(np.float32),
                     np.float32(-1e30)).astype(np.float32).reshape(128, 2048)
    m = np.zeros((2, 128, 8, 128), np.float32)
    for l, w in enumerate(LEVELS):
        same = (i[:, None] // (2 * w)) == (i[None, :] // (2 * w))
        first = (i % (2 * w)) < w
        m[0, :, l, :] = same & first[:, None] & ~first[None, :]
        m[1, :, l, :] = same & ~first[:, None] & first[None, :]
    m[:, :, 7, :] = np.eye(128)
    return c, alibi, m.reshape(2, 128, 1024)


def _cols(v, n):
    return v.reshape(n, 128).T


def _rows(w):
    return w.reshape(-1, 128, w.shape[1]).transpose(1, 0, 2).reshape(128, -1)


def _layout(x):
    a = {}
    a["cst"], a["alibi"], a["hmask"] = _constants()
    a["x"] = x["x"][0]
    a["xT"] = x["x"][0].T
    head = np.concatenate([np.concatenate([np.arange(64) + 64 * j, np.arange(64) + 64 * (4 + j)]) for j in range(4)])
    order = np.concatenate([np.arange(1024), 1024 + head, np.arange(1536, 1920), np.arange(2048, 2176)])
    tok = np.concatenate([np.arange(1920, 2048), np.arange(2176, 2328)])
    w = x["w_in"]
    a["w_inA"] = np.stack([np.stack([_rows(w[l][:, order[512 * j:512 * j + 512]]) for j in range(4)]) for l in range(2)])
    a["w_inB"] = np.stack([_rows(w[l][:, tok]) for l in range(2)])
    a["cmp_w1"] = np.stack([np.stack([np.concatenate([x[n][l].reshape(32, 64, 64).transpose(1, 0, 2)] * 2)
                                      .reshape(128, 2048) for n in ("cmpk_w1", "cmpv_w1")]) for l in range(2)])
    pp = np.zeros((2, 128, NP_COLS), np.float32)
    for l in range(2):
        p = pp[l]
        p[:, P_BIN:P_BIN + 16] = _cols(x["b_in"][l][order], 16)
        p[:, P_CW:P_CW + 16] = x["conv_w"][l].reshape(4, 4, 128).transpose(2, 0, 1).reshape(128, 16)
        for c, n in ((P_CB, "conv_b"), (P_BA, "lru_ba"), (P_BX, "lru_bx"), (P_LAM, "lru_lambda"), (P_GL, "gn_lru_g"),
                     (P_GN, "gn_nsa_g")):
            p[:, c:c + 4] = _cols(x[n][l], 4)
        p[:, P_POSK:P_POSK + 32] = np.concatenate([x["cmp_pos_k"][l].T] * 2)
        p[:, P_POSV:P_POSV + 32] = np.concatenate([x["cmp_pos_v"][l].T] * 2)
        for c, n in ((P_B1K, "cmpk_b1"), (P_B2K, "cmpk_b2"), (P_B1V, "cmpv_b1")):
            p[:, c] = np.concatenate([x[n][l]] * 2)
        p[:, P_B2V:P_B2V + 64] = x["cmpv_b2"][l][None, :]
        p[:, P_BTOK:P_BTOK + 280] = x["b_in"][l][tok][None, :]
        p[0:64, P_W2K:P_W2K + 128] = np.concatenate([x["cmpk_w2"][l]] * 2, 1)
        p[0:64, P_W2V:P_W2V + 64] = x["cmpv_w2"][l]
        p[:, P_SK:P_SK + 256] = x["peer_subkeys"][l].transpose(2, 0, 1).reshape(128, 256)
        for c, n in ((P_WA, "lru_wa"), (P_WX, "lru_wx")):
            for b in range(8):
                s = 64 * (b % 2)
                p[s:s + 64, c + 128 * (b // 2) + s:c + 128 * (b // 2) + s + 64] = x[n][l][b]
    a["pp"] = pp
    a["ln"] = np.stack([np.stack([np.concatenate([x["ln1_g"][l], x["ln1_b"][l]]),
                                  np.concatenate([x["ln2_g"][l], x["ln2_b"][l]])]) for l in range(2)])
    a["w_out"] = np.stack([np.stack([_rows(x["w_out"][l][512 * k:512 * k + 512]) for k in range(2)]) for l in range(2)])
    a["peer_wq"] = np.stack([np.stack([_rows(x["peer_wq"][l][:, 512 * j:512 * j + 512]) for j in range(4)])
                             for l in range(2)])
    a["peer_u"] = x["peer_u"].reshape(2, 128, 32, 4, 8, 128).transpose(0, 2, 5, 3, 4, 1).reshape(2, 32, 128, 4096)
    a["peer_v"] = x["peer_v"].reshape(2, 128, 32, 4096).transpose(0, 2, 1, 3)
    _layout2(x, a)
    return {k: np.ascontiguousarray(v) for k, v in a.items()}


def _layout2(x, a):
    x = {k[:-2]: v for k, v in x.items() if k.endswith("_2")}
    a["ctxT"] = x["ctx"][0].T
    q = np.zeros((128, NQ_COLS), np.float32)
    q[:, Q_CC:Q_CC + 16] = np.stack([_cols(x["c"][0], 8), _cols(x["c_ctx"], 8)], -1).reshape(128, 16)
    q[:, Q_BMOD:Q_BMOD + 48] = _cols(x["b_mod"][0], 48)
    q[:, Q_NMG:Q_NMG + 8] = _cols(x["norm_mix_g"][0], 8)
    q[:, Q_QNG:Q_QNG + 6] = _cols(x["mla_q_norm_g"][0], 6)
    q[:, Q_KVG:Q_KVG + 2] = _cols(x["mla_kv_norm_g"][0], 2)
    q[:, Q_LBL:Q_LBL + 32] = x["hg_lb_logits"].reshape(2, 2, 8, 128).transpose(3, 0, 1, 2).reshape(128, 32)
    q[:, Q_HGN] = x["hg_norm_g"][0]
    q[:, Q_NFG:Q_NFG + 8] = _cols(x["norm_ffn_g"][0], 8)
    q[:, Q_BR:Q_BR + 32] = x["b_router"][0][None, :]
    q[:, Q_WR:Q_WR + 256] = _rows(x["w_router"][0])
    q[:, Q_BGU:Q_BGU + 512] = x["b_gate_up"][0].reshape(32, 8, 128, 2).transpose(2, 0, 1, 3).reshape(128, 512)
    q[:, Q_FNG:Q_FNG + 8] = _cols(x["final_norm_g"], 8)
    a["qq"] = q
    w = x["w_mod"][0]
    a["w_mod"] = np.stack([_rows(w[:, 512 * j:512 * j + 512]) for j in range(12)])
    w = x["w_in"][0]
    a["w_q"] = np.stack([_rows(w[:, 384 * j:384 * j + 384]) for j in range(2)])
    a["w_kv"] = _rows(np.concatenate([w[:, 768:1088], w[:, 1024:1088]], 1))
    a["w_hg"] = np.stack([_rows(w[:, 1088 + 512 * j:1088 + 512 * j + 512]) for j in range(14)])
    w = x["w_q_b"][0].reshape(768, 8, 192)
    a["w_qb_n"] = np.stack([_rows(w[:, 4 * j:4 * j + 4, 0:128].reshape(768, 512)) for j in range(2)])
    a["w_qb_r"] = _rows(w[:, :, 128:192].reshape(768, 512))
    w = x["w_kv_b"][0].reshape(256, 8, 256)
    a["w_kvb"] = np.concatenate([_rows(w[:, :, 0:128].reshape(256, 1024)), _rows(w[:, :, 128:256].reshape(256, 1024))], 1)
    a["w_o2"] = np.stack([_rows(x["w_out"][0][:, 512 * j:512 * j + 512]) for j in range(2)])
    a["w_gu"] = x["w_gate_up"][0].reshape(32, 8, 128, 4, 2, 128, 2).transpose(0, 3, 2, 4, 6, 1, 5).reshape(32, 4, 128, 4096)
    a["w_dn"] = x["w_down"][0].reshape(32, 2, 4, 128, 1024).transpose(0, 1, 3, 2, 4).reshape(32, 2, 128, 4096)
    a["b_dn"] = x["b_down"][0]


def kernel(**inputs):
    import concourse.bacc as _bacc
    from concourse.bass_utils import run_bass_kernel_spmd as _run

    nc = _bacc.Bacc("TRN2", target_bir_lowering=False, num_devices=1)
    arrays, args = {}, {}
    for name, a in _layout({k: np.asarray(v) for k, v in inputs.items()}).items():
        arrays[f"in_{name}_dram"] = a
        args[name] = nc.dram_tensor(f"in_{name}_dram", a.shape, F32, kind="ExternalInput").ap()
    out = nc.dram_tensor("out_0_dram", (256, 1024), F32, kind="ExternalOutput").ap()
    build(nc, args, out)
    r = _run(nc, [arrays], core_ids=[0])
    return r.results[0]["out_0_dram"].reshape(1, 256, 1024)
```

```python
from contextlib import ExitStack

import numpy as np
import concourse.bass as bass
from concourse import mybir

F32 = mybir.dt.float32
BF16 = mybir.dt.bfloat16
U32 = mybir.dt.uint32
I32 = mybir.dt.int32
ALU = mybir.AluOpType
ACT = mybir.ActivationFunctionType
AX = mybir.AxisListType

ALPHA = 4.0 ** 0.25
NSLOT = 4
PIECE = 4096
AHEAD = 16
SLOTS = 64
EXTRA = 15
LEVELS = [64, 32, 16, 8, 4, 2, 1]

C_ID, C_ONE, C_IOTA, C_I16, C_PERM, C_VAL, C_E5, C_E6, C_CB, C_MF, C_MB, C_COS, C_SIN = (
    0, 128, 256, 384, 400, 528, 529, 530, 531, 771, 1027, 1283, 1539)
NC_COLS = 1795
(P_BIN, P_CW, P_CB, P_BA, P_BX, P_LAM, P_POSK, P_POSV, P_B1K, P_B2K, P_B1V, P_GL, P_GN, P_B2V, P_BTOK,
 P_W2K, P_W2V, P_SK, P_WA, P_WX) = (0, 16, 32, 36, 40, 44, 48, 80, 112, 113, 114, 115, 119, 123, 187,
                                    467, 595, 659, 915, 1427)
NP_COLS = 1939
(Q_CC, Q_BMOD, Q_NMG, Q_QNG, Q_KVG, Q_LBL, Q_HGN, Q_NFG, Q_BR, Q_WR, Q_FNG) = (
    0, 16, 64, 72, 78, 80, 112, 113, 121, 153, 409)
NQ_COLS = 417


class Queue:

    def __init__(self, sem, in_order):
        self.sem, self.in_order, self.n, self.ops, self.fence = sem, in_order, 0, [], []

    def do(self, fn, *waits, inc=True):
        w = list(waits) + self.fence
        self.fence = []
        if self.in_order and self.n:
            w.append((self.sem, self.n))
        self.ops.append((w, fn, self.sem if inc else None))
        if inc:
            self.n += 1
        return (self.sem, self.n + (not inc))

    def last(self):
        return (self.sem, self.n)

    def emit(self, eng):
        walk(eng, self.ops, lambda fn, inc, regs: self.issue(eng, fn, inc))

    def issue(self, eng, fn, inc):
        r = fn(eng)
        if inc:
            r.then_inc(inc, 1)


def walk(eng, ops, issue):
    seen, saved, stack, regs = {}, None, None, {}

    def wait(w):
        if w is None:
            return
        if isinstance(w, list):
            for x in w:
                wait(x)
            return
        s, v = w
        if v > seen.get(s, 0):
            eng.wait_ge(s, v)
            seen[s] = v

    for w, what, extra in ops:
        if what == "end":
            stack.close()
            seen = saved
            continue
        wait(list(w))
        if what == "begin":
            regs["n"] = eng.value_load(extra[0:1, 0:1], min_val=0, max_val=EXTRA)
            saved, stack = dict(seen), ExitStack()
        elif what == "if":
            k, ap = extra
            stack.enter_context(eng.If(regs["n"] > k))
            if ap is not None:
                regs["e"] = eng.value_load(ap[0:1, k + 1:k + 2], min_val=0, max_val=31)
        elif what is not None:
            issue(what, extra, regs)


class Held:

    def __init__(self, ap):
        self.ap, self.ready, self.free = ap, None, []


def bc(ap, axis, n):
    ap = ap.unsqueeze(axis)
    shape = list(ap.shape)
    shape[axis] = n
    return ap.broadcast_to(shape)


def build(nc, d, out):
    with ExitStack() as ctx:
        def sb(name, cols, dt=F32):
            return ctx.enter_context(nc.sbuf_tensor(name, [128, cols], dt))

        def sem(name):
            return ctx.enter_context(nc.semaphore(name))

        P = Queue(sem("s_pe"), False)
        V = Queue(sem("s_dve"), True)
        A = Queue(sem("s_act"), True)
        G = Queue(sem("s_pool"), True)
        S = []
        ring = sb("ring", NSLOT * PIECE)
        s_ring = [sem(f"s_ring{i}") for i in range(NSLOT)]
        xtok = sb("xtok", 2048)
        xT_t = sb("xT", 2048)
        cst = sb("cst", NC_COLS)
        pp = sb("pp", NP_COLS)
        ARENA = (212000 - 4 * (NSLOT * PIECE + 4096 + NC_COLS + NP_COLS)) // 4 // 8 * 8
        arena = sb("arena", ARENA)
        banks = [Held(ctx.enter_context(nc.psum_tensor(f"bank{i}", [128, 512], F32))) for i in range(8)]
        x3 = xtok[:, :].rearrange("p (t n) -> p t n", t=2)
        xT = xT_t[:, :].rearrange("p (c t) -> p c t", c=8)

        top = [0]

        def fence():
            toks = [q.last() for q in (P, V, A, G)]
            for q in (P, V, A, G):
                q.fence = q.fence + toks
            top[0] = 0
            return toks

        def ar(cols, dt=F32):
            a = top[0]
            top[0] += (cols + 7) // 8 * 8
            assert top[0] <= ARENA, (top[0], ARENA)
            return arena[:, a:a + cols]

        def ar3(a, b):
            return ar(a * b).rearrange("p (a b) -> p a b", a=a)

        def ar4(a, b, c):
            return ar(a * b * c).rearrange("p (a b c) -> p a b c", a=a, b=b)

        uses = [[] for _ in range(NSLOT)]
        n_load = [0]

        def load(src, cols):
            i = n_load[0] % NSLOT
            n_load[0] += 1
            h = Held(ring[:, i * PIECE:i * PIECE + cols])
            prev = uses[i][-1] if uses[i] else None
            uses[i].append(h)
            h.ready = (s_ring[i], 16 * len(uses[i]))
            S.append((prev.free if prev else [], (h.ap, src), s_ring[i]))
            return h

        n_once = [0]

        def load_once(dst, src, waits=()):
            n_once[0] += 1
            s = sem(f"s_once{n_once[0]}")
            S.append((list(waits), (dst, src), s))
            return (s, 16)

        s_out = sem("s_out")
        n_out = [0]

        def store(dst, src, *waits):
            n_out[0] += 16
            S.append((list(waits), (dst, src), s_out))


        rot = {"n": 0, "set": list(range(8))}

        def bank():
            b = banks[rot["set"][rot["n"] % len(rot["set"])]]
            rot["n"] += 1
            return b

        def mm(b, o, pairs, *waits):
            w = list(waits) + [list(b.free)] if b is not None else list(waits)
            n = len(pairs)
            t = None
            for i, (l, r) in enumerate(pairs):
                t = P.do(lambda e, l=l, r=r, i=i: e.matmul(o, l, r, start=(i == 0), stop=(i == n - 1)),
                         *(w if i == 0 else ()), inc=(i == n - 1))
            return t

        def tr(b, o, src, *waits):
            n = src.shape[0]
            return P.do(lambda e: e.transpose(o, src, ident[0:n, 0:n]), *waits, list(b.free))

        def act(o, i, f, *w, bias=None, scale=1.0, acc=None):
            kw = {}
            if bias is not None:
                kw["bias"] = bias
            if acc is not None:
                kw["accum_out"] = acc
            return A.do(lambda e: e.activation(o, i, f, scale=scale, **kw), *w)

        def tt(o, a, b, op, *w, q=None):
            return (q or V).do(lambda e: e.tensor_tensor(o, a, b, op), *w)

        def ts(o, a, s1, s2, o1, o2, *w, q=None):
            if o2 is None:
                return (q or V).do(lambda e: e.tensor_scalar(o, a, s1, None, o1), *w)
            return (q or V).do(lambda e: e.tensor_scalar(o, a, s1, s2, o1, o2), *w)

        def stt(o, a, s, b, o1, o2, *w):
            return V.do(lambda e: e.scalar_tensor_tensor(out=o, in0=a, scalar=s, in1=b, op0=o1, op1=o2), *w)

        def cp(o, i, *w, q=None):
            return (q or V).do(lambda e: e.tensor_copy(o, i), *w)

        def red(o, i, op, *w, neg=False):
            return V.do(lambda e: e.tensor_reduce(o, i, AX.X, op, negate=neg), *w)

        def recip(o, i, *w):
            return V.do(lambda e: e.reciprocal(o, i), *w)

        MUL, ADD, SUB, MAX, MIN, EQ = ALU.mult, ALU.add, ALU.subtract, ALU.max, ALU.min, ALU.is_equal

        ident = cst[:, C_ID:C_ID + 128]
        ones = cst[:, C_ONE:C_ONE + 128]
        iota = cst[:, C_IOTA:C_IOTA + 128]
        t_cst = load_once(cst[:, :], d["cst"])
        t_x = load_once(x3, d["x"].rearrange("(t p) n -> p t n", p=128))
        t_xT = load_once(xT, d["xT"].rearrange("(c p) t -> p c t", p=128))
        for q in (P, V, A, G):
            q.fence = [t_cst, t_x, t_xT]

        def transposes(dst4, src, n, *waits, evac=None):
            last = None
            for a in range(0, n, 4):
                b = bank()
                k = min(4, n - a)
                for j in range(k):
                    t = tr(b, b.ap[:, j * 128:j * 128 + 128], src(a + j), *(waits if a == 0 and j == 0 else ()))
                last = evac(a, k, b.ap[:, 0:k * 128].rearrange("p (k t) -> p k t", k=k), t)
                b.free = [last]
            return last

        def layer_norm(z, g_ap, b_ap, st, mv, dst, *w):
            for t in range(2):
                for h in range(2):
                    V.do(lambda e, t=t, h=h: e.bn_stats(st[:, 2 * t + h, :], z[:, t, h * 512:h * 512 + 512]), *w)
                V.do(lambda e, t=t: e.bn_aggr(mv[:, t, 0:2], st[:, 2 * t:2 * t + 2, :]))
            act(mv[:, :, 2:3], mv[:, :, 1:2], ACT.Sqrt, V.last(), bias=cst[:, C_E5:C_E5 + 1])
            recip(mv[:, :, 3:4], mv[:, :, 2:3], A.last())
            for t in range(2):
                ts(z[:, t, :], z[:, t, :], mv[:, t, 0:1], mv[:, t, 3:4], SUB, MUL)
            tt(z, z, bc(g_ap, 1, 2), MUL)
            return tt(dst, z, bc(b_ap, 1, 2), ADD)

        def to_xT(src3, waits):
            def evac(a, k, ps, t):
                tk, c0 = a // 8, a % 8
                return cp(xT[:, c0:c0 + k, tk * 128:tk * 128 + 128], ps, t) if (a // 4) % 2 else \
                    act(xT[:, c0:c0 + k, tk * 128:tk * 128 + 128], ps, ACT.Copy, t)
            transposes(None, lambda i: src3[:, i // 8, (i % 8) * 128:(i % 8) * 128 + 128], 16, *waits, evac=evac)

        def mixing(l, t_pp):
            fence()
            xpad = ar3(4, 259)
            gT = ar3(4, 256)
            qT = ar3(4, 256)
            kT = ar3(4, 256)
            vtok = ar3(2, 256)
            gates = ar3(2, 24)
            alibi = ar3(8, 256)
            t_al = load_once(alibi, d["alibi"].rearrange("p (h k) -> p h k", h=8),
                             [q.last() for q in (P, V, A, G)])

            def par(c, n=1):
                return pp[:, c:c + n]

            V.do(lambda e: e.memset(xpad[:, :, 0:3], 0.0))
            cw = []
            for j in range(4):
                pc = load(d["w_inA"][l, j], 4096)
                w = pc.ap.rearrange("p (c n) -> p c n", c=8)
                for half in range(2):
                    b = bank()
                    for k in range(2):
                        ct = half * 2 + k
                        t = mm(b, b.ap[:, k * 256:k * 256 + 256],
                               [(w[:, dc, ct * 128:ct * 128 + 128], xT[:, dc, :]) for dc in range(8)],
                               pc.ready, t_pp)
                    for k in range(2):
                        ct = half * 2 + k
                        dst = [xpad[:, ct, 3:259], gT[:, ct, :], qT[:, ct, :], kT[:, ct, :]][j]
                        src = b.ap[:, k * 256:k * 256 + 256]
                        if half:
                            e1 = ts(dst, src, par(P_BIN + 4 * j + ct), None, ADD, None, t, t_pp)
                        else:
                            e1 = act(dst, src, ACT.Identity, t, t_pp, bias=par(P_BIN + 4 * j + ct))
                    b.free = [e1]
                pc.free = [t]
            pc = load(d["w_inB"][l], 2240)
            w = pc.ap.rearrange("p (c n) -> p c n", c=8)
            for tk in range(2):
                b = bank()
                t = mm(b, b.ap[:, 0:280], [(xT[:, dc, tk * 128:tk * 128 + 128], w[:, dc, :]) for dc in range(8)],
                       pc.ready)
                tt(vtok[:, tk, :], b.ap[:, 0:256], par(P_BTOK, 256), ADD, t)
                tt(gates[:, tk, :], b.ap[:, 256:280], par(P_BTOK + 256, 24), ADD)
                b.free = [V.last()]
            pc.free = [t]
            act(gates, gates, ACT.Sigmoid, V.last())

            xc = ar3(4, 256)
            r = ar3(4, 256)
            ig = ar3(4, 256)
            aa = ar3(4, 256)
            th = ar3(4, 256)
            sp = ar(32)
            t_x = A.last()
            lam = par(P_LAM, 4)
            ts(sp[:, 0:4], lam, -1.0, None, MUL, None)
            tt(sp[:, 4:8], lam, sp[:, 0:4], MIN)
            act(sp[:, 8:12], sp[:, 4:8], ACT.Exp, V.last())
            ts(sp[:, 12:16], sp[:, 8:12], 2.0, None, ADD, None, A.last())
            recip(sp[:, 16:20], sp[:, 12:16])
            tt(sp[:, 12:16], sp[:, 8:12], sp[:, 16:20], MUL)
            tt(sp[:, 16:20], sp[:, 12:16], sp[:, 12:16], MUL)
            V.do(lambda e: e.memset(sp[:, 20:24], 2.0 / 17))
            for c in (15, 13, 11, 9, 7, 5, 3, 1):
                tt(sp[:, 20:24], sp[:, 20:24], sp[:, 16:20], MUL)
                ts(sp[:, 20:24], sp[:, 20:24], 2.0 / c, None, ADD, None)
            tt(sp[:, 20:24], sp[:, 20:24], sp[:, 12:16], MUL)
            ts(sp[:, 0:4], sp[:, 0:4], 0.0, None, MAX, None)
            tt(sp[:, 20:24], sp[:, 20:24], sp[:, 0:4], ADD)
            ts(sp[:, 20:24], sp[:, 20:24], -8.0, None, MUL, None)
            for ct in range(4):
                for j in range(4):
                    src = xpad[:, ct, j:j + 256]
                    wj = par(P_CW + 4 * j + ct)
                    if j == 0:
                        ts(xc[:, ct, :], src, wj, par(P_CB + ct), MUL, ADD, t_x)
                    else:
                        stt(xc[:, ct, :], src, wj, xc[:, ct, :], MUL, ADD)
            t_xc = V.last()
            for wcol, bcol, dst in ((P_WA, P_BA, r), (P_WX, P_BX, ig)):
                for ct in range(4):
                    b = bank()
                    t = mm(b, b.ap[:, 0:256], [(par(wcol + 128 * ct, 128), xc[:, ct, :])], t_xc)
                    b.free = [act(dst[:, ct, :], b.ap[:, 0:256], ACT.Sigmoid, t, bias=par(bcol + ct))]
            t_ri = A.last()
            for ct in range(4):
                ts(r[:, ct, :], r[:, ct, :], sp[:, 20 + ct:21 + ct], None, MUL, None, t_ri)
            tt(ig, ig, xc, MUL)
            t1 = V.last()
            act(th, r, ACT.Tanh, t1, scale=-1.0)
            act(aa, r, ACT.Exp)
            t2 = A.last()
            ts(r, th, 1.0, None, ADD, None, t2)
            recip(r, r)
            tt(r, r, th, MUL)
            act(th, r, ACT.Sqrt, V.last(), scale=2.0)
            tt(ig, ig, th, MUL, A.last())
            for ct in range(4):
                V.do(lambda e, ct=ct: e.tensor_tensor_scan(xc[:, ct, :], aa[:, ct, :], ig[:, ct, :], 0.0, MUL, ADD))
            act(gT, gT, ACT.Gelu_apprx_tanh)
            tt(xc, xc, gT, MUL, A.last())
            tt(th, xc, xc, MUL)
            ylT = xpad[:, :, 0:256]
            for ct in range(4):
                ts(ylT[:, ct, :], xc[:, ct, :], par(P_GL + ct), None, MUL, None)
            t_yl = V.last()
            ss = ar(16)
            b = bank()
            for tk in range(2):
                t = mm(b, b.ap[:, tk:tk + 1], [(th[:, ct, tk * 128:tk * 128 + 128], ones[:, 0:1]) for ct in range(4)],
                       t_yl)
            act(ss[:, 0:2], b.ap[:, 0:2], ACT.Sqrt, t, scale=1.0 / 512, bias=cst[:, C_E5:C_E5 + 1])
            b.free = [A.last()]
            recip(ss[:, 2:4], ss[:, 0:2], A.last())

            gk = ar(32)
            kcT = ar(16)
            vc = ar(128)
            kp = xc[:, 0:2, :].rearrange("p a b -> p (a b)")[:, 0:480].rearrange("p (c j) -> p c j", j=32)
            kz = ar(32 * 30).rearrange("p (j g c) -> p j g c", j=32, g=2)
            P_w = V.last()
            for n, (pos, b1, w2) in enumerate(((P_POSK, P_B1K, P_W2K), (P_POSV, P_B1V, P_W2V))):
                pc = load(d["cmp_w1"][l, n], 2048)
                w1 = pc.ap.rearrange("p (j e) -> p j e", j=32)
                V.do(lambda e: e.memset(kz, 0.0), P.last())
                for hf in range(2):
                    win = kT[:, n, hf * 16:hf * 16 + 240].rearrange("p (c j) -> p j c", j=16)
                    for g in range(2):
                        s = slice(64 * g, 64 * g + 64)
                        tt(kz[s, hf * 16:hf * 16 + 16, g, :], win[s, :, :],
                           bc(par(pos + hf * 16, 16), 2, 15)[s, :, :], ADD)
                b = bank()
                t = mm(b, b.ap[0:64, 0:30], [(w1[:, j, :], kz[:, j, :, :]) for j in range(32)], pc.ready, V.last())
                pc.free = [t]
                act(gk[0:64, 0:30], b.ap[0:64, 0:30], ACT.Gelu_apprx_tanh, t, bias=pp[0:64, b1:b1 + 1])
                b.free = [A.last()]
                if n == 0:
                    b = bank()
                    t = mm(b, b.ap[:, 0:30], [(pp[0:64, w2:w2 + 128], gk[0:64, 0:30])], A.last())
                    for g in range(2):
                        s = slice(64 * g, 64 * g + 64)
                        ts(kcT[s, 0:15], b.ap[s, 15 * g:15 * g + 15], pp[s, P_B2K:P_B2K + 1], None, ADD, None, t)
                    b.free = [V.last()]
                else:
                    b = bank()
                    for g in range(2):
                        t = mm(b, b.ap[0:15, 64 * g:64 * g + 64],
                               [(gk[0:64, 15 * g:15 * g + 15], pp[0:64, w2:w2 + 64])], A.last())
                    tt(vc[0:15, :].rearrange("p (g d) -> p g d", g=2),
                       b.ap[0:15, 0:128].rearrange("p (g d) -> p g d", g=2),
                       bc(pp[0:15, P_B2V:P_B2V + 64], 1, 2), ADD, t)
                    b.free = [V.last()]
            t_c = V.last()

            s_ = ar3(8, 256)
            pT = ar4(2, 8, 128)
            osum = ar3(2, 512)
            tmp = ar(512).rearrange("p (h d) -> p h d", h=8)
            st = ar(64)
            for tk in range(2):
                for br in range(3):
                    nk = 15 if br == 0 else 128 * (tk + 1)
                    per = 4 if br == 0 else 2
                    bs = []
                    for g in range(2):
                        for j0 in range(0, 4, per):
                            b = bank()
                            for jj in range(per):
                                j = j0 + jj
                                sl = slice(64 * g, 64 * g + 64)
                                key = kcT[sl, 0:15] if br == 0 else kT[sl, 1 + br, 0:nk]
                                t = mm(b, b.ap[:, jj * nk:jj * nk + nk], [(qT[sl, j, tk * 128:tk * 128 + 128], key)], t_c)
                            bias = cst[:, C_CB + tk * 120:C_CB + tk * 120 + 120].rearrange("p (h c) -> p h c", h=8) \
                                if br == 0 else alibi[:, :, 256 - nk:256]
                            h0 = 4 * g + j0
                            stt(s_[:, h0:h0 + per, 0:nk], b.ap[:, 0:per * nk].rearrange("p (h k) -> p h k", h=per), 0.125,
                                bias[:, h0:h0 + per, :], MUL, ADD, t, t_al, A.last(), P.last() if h0 == 0 else None)
                            b.free = [V.last()]
                    red(st[:, 0:8], s_[:, :, 0:nk], MAX, neg=True)
                    t = V.last()
                    for h in range(8):
                        act(s_[:, h, 0:nk], s_[:, h, 0:nk], ACT.Exp, t, bias=st[:, h:h + 1],
                            acc=st[:, 8 + h:9 + h])
                    t_p = A.last()
                    recip(st[:, 16:24], st[:, 8:16], t_p)
                    tt(st[:, 24:32], st[:, 16:24], gates[:, tk, br:24:3], MUL)
                    if br == 0 and tk == 0:
                        ts(st[:, 24:32], st[:, 24:32], cst[:, C_VAL:C_VAL + 1], None, MUL, None)
                    b_o = bank()
                    if br == 0:
                        for h0 in (0, 4):
                            b = bank()
                            for h in range(h0, h0 + 4):
                                t = tr(b, b.ap[0:15, (h - h0) * 128:(h - h0) * 128 + 128], s_[:, h, 0:15], t_p)
                            cp(pT[0:15, 0, h0:h0 + 4, :], b.ap[0:15, :].rearrange("p (h t) -> p h t", h=4), t)
                            b.free = [V.last()]
                        for h in range(8):
                            g = h // 4
                            t = mm(b_o, b_o.ap[:, h * 64:h * 64 + 64],
                                   [(pT[0:15, 0, h, :], vc[0:15, 64 * g:64 * g + 64])], V.last())
                    else:
                        for kt in range(tk + 1):
                            for h0 in (0, 4):
                                b = bank()
                                for h in range(h0, h0 + 4):
                                    t = tr(b, b.ap[:, (h - h0) * 128:(h - h0) * 128 + 128],
                                           s_[:, h, kt * 128:kt * 128 + 128], t_p)
                                cp(pT[:, kt, h0:h0 + 4, :], b.ap[:, :].rearrange("p (h t) -> p h t", h=4), t)
                                b.free = [V.last()]
                        vo = (br - 1) * 128
                        for h in range(8):
                            g = h // 4
                            t = mm(b_o, b_o.ap[:, h * 64:h * 64 + 64],
                                   [(pT[:, kt, h, :], vtok[:, kt, vo + 64 * g:vo + 64 * g + 64]) for kt in range(tk + 1)],
                                   V.last())
                    o3 = osum[:, tk, :].rearrange("p (h d) -> p h d", h=8)
                    dst = o3 if br == 0 else tmp
                    tt(dst, b_o.ap[:, :].rearrange("p (h d) -> p h d", h=8), bc(st[:, 24:32], 2, 64), MUL, t)
                    b_o.free = [V.last()]
                    if br:
                        tt(o3, o3, tmp, ADD)
                V.do(lambda e, tk=tk: e.tensor_tensor_reduce(
                    tmp.rearrange("p h d -> p (h d)"), osum[:, tk, :], osum[:, tk, :], 1.0, 0.0, MUL, ADD,
                    ss[:, 4 + tk:5 + tk]))
            act(ss[:, 6:8], ss[:, 4:6], ACT.Sqrt, V.last(), scale=1.0 / 512, bias=cst[:, C_E5:C_E5 + 1])
            recip(ss[:, 8:10], ss[:, 6:8], A.last())
            ynT = qT
            t_o = V.last()
            for tk in range(2):
                b = bank()
                for c in range(4):
                    t = tr(b, b.ap[:, c * 128:c * 128 + 128], osum[:, tk, c * 128:c * 128 + 128], t_o)
                for c in range(4):
                    ts(ynT[:, c, tk * 128:tk * 128 + 128], b.ap[:, c * 128:c * 128 + 128], par(P_GN + c), None,
                       MUL, None, t)
                b.free = [V.last()]
            t_yn = V.last()
            z = s_.rearrange("p h k -> p (h k)").rearrange("p (t n) -> p t n", t=2)
            lst = ar3(4, 6)
            mv = ar3(2, 4)
            ln = load(d["ln"][l, 0].partition_broadcast(128), 2048)
            pcs = [load(d["w_out"][l, k], 4096) for k in range(2)]
            ts(z, x3, ALPHA, None, MUL, None, A.last(), P.last())
            for k, yT in ((0, ylT), (1, ynT)):
                w = pcs[k].ap.rearrange("p (c n) -> p c n", c=4)
                for tk in range(2):
                    for dh in range(2):
                        b = bank()
                        t = mm(b, b.ap[:, :], [(yT[:, c, tk * 128:tk * 128 + 128], w[:, c, dh * 512:dh * 512 + 512])
                                               for c in range(4)], pcs[k].ready, t_yn)
                        zz = z[:, tk, dh * 512:dh * 512 + 512]
                        sc = ss[:, 2 + tk:3 + tk] if k == 0 else ss[:, 8 + tk:9 + tk]
                        stt(zz, b.ap[:, :], sc, zz, MUL, ADD, t)
                        b.free = [V.last()]
                pcs[k].free = [t]
            layer_norm(z, ln.ap[:, 0:1024], ln.ap[:, 1024:2048], lst, mv, x3, ln.ready)
            ln.free = [V.last()]
            to_xT(x3, [V.last()])

        def peer(l):
            fence()
            rot["set"] = list(range(6))
            eg = ar4(3, 2, 128).rearrange("p k t n -> p k (t n)")
            gs = ar4(3, 1, 256).rearrange("p k o n -> p k (o n)")
            gsb = ar(384).bitcast(BF16).rearrange("p (k n) -> p k n", k=3)
            gel = [Held(ar(256)) for _ in range(AHEAD + 1)]
            pt = [Held(ar(256)) for _ in range(3)]
            Aoh = [Held(ar(1024).bitcast(BF16).rearrange("p (t a) -> p t a", t=16)) for _ in range(3)]
            Boh = [Held(ar(768).bitcast(BF16).rearrange("p (k t b) -> p k t b", k=3, t=16)) for _ in range(2)]
            eqb = ar(512).rearrange("p (t b) -> p t b", t=16)
            mark = top[0]
            qT = ar3(16, 256)
            s_ = ar4(2, 16, 128)
            sk = pp[:, P_SK:P_SK + 256].rearrange("p (c k) -> p c k", c=2)
            for j in range(4):
                pc = load(d["peer_wq"][l, j], 4096)
                w = pc.ap.rearrange("p (c n) -> p c n", c=8)
                for hf in range(2):
                    b = bank()
                    for k in range(2):
                        ct = hf * 2 + k
                        t = mm(b, b.ap[:, k * 256:k * 256 + 256],
                               [(w[:, dc, ct * 128:ct * 128 + 128], xT[:, dc, :]) for dc in range(8)],
                               pc.ready, A.last(), V.last())
                    b.free = [act(qT[:, 4 * j + 2 * hf:4 * j + 2 * hf + 2, :],
                                  b.ap[:, :].rearrange("p (k t) -> p k t", k=2), ACT.Copy, t)]
                pc.free = [t]
            t_q = A.last()
            for tk in range(2):
                for h4 in range(4):
                    b = bank()
                    for k in range(4):
                        hc = 4 * h4 + k
                        t = mm(b, b.ap[:, k * 128:k * 128 + 128],
                               [(qT[:, hc, tk * 128:tk * 128 + 128], sk[:, hc % 2, :])], t_q)
                    b.free = [act(s_[:, tk, 4 * h4:4 * h4 + 4, :], b.ap[:, :].rearrange("p (k t) -> p k t", k=4),
                                  ACT.Copy, t)]
            t_s = A.last()
            t_pp_free = P.last()
            work = ar(256)
            sv = ar(256).rearrange("p (h c k) -> p h c k", h=8, c=2)
            si = ar(256).bitcast(U32).rearrange("p (h c k) -> p h c k", h=8, c=2)
            sif = ar(256).rearrange("p (h c k) -> p h c k", h=8, c=2)
            cand = ar(2048).rearrange("p (h a b) -> p h a b", h=8, a=16)
            cv = ar3(8, 16)
            ci = ar(128).bitcast(U32).rearrange("p (h k) -> p h k", h=8)
            cj = ar(256).bitcast(U32).rearrange("p (c n) -> p c n", c=2)
            cf = ar(256).rearrange("p (c h k) -> p c h k", c=2, h=8)
            ea = ar(384).rearrange("p (c n) -> p c n", c=3)
            sm = ar(32)

            def top16(src, vals, idx, wk):
                V.do(lambda e: e.max(vals[:, 0:8], src))
                V.do(lambda e: e.max_index(idx[:, 0:8], vals[:, 0:8], src))
                V.do(lambda e: e.match_replace(wk, vals[:, 0:8], src, -3.0e38))
                V.do(lambda e: e.max(vals[:, 8:16], wk))
                V.do(lambda e: e.max_index(idx[:, 8:16], vals[:, 8:16], wk))

            V.fence = V.fence + [t_s]
            bG = [banks[4], banks[5]]
            bU = [banks[6], banks[7]]
            up = {}

            def stage1(c):
                if c % 4 == 0:
                    up["u"] = load(d["peer_u"][l, c // 4], 4096)
                    if c >= AHEAD:
                        k = c // 4 - AHEAD // 4
                        up["v", k] = load(d["peer_v"][l, k], 4096)
                u = up["u"]
                w = u.ap.rearrange("p (i c a) -> p i c a", i=4, c=8)
                b = bU[c % 2]
                t = mm(b, b.ap[:, 0:256], [(w[:, c % 4, dc, :], xT[:, dc, :]) for dc in range(8)], u.ready)
                if c % 4 == 3:
                    u.free = [t]
                ge = gel[c % (AHEAD + 1)]
                ge.ready = act(ge.ap, b.ap[:, 0:256], ACT.Gelu_apprx_tanh, t, list(ge.free))
                b.free = [A.last()]

            for tk in range(2):
                for c in range(AHEAD // 2 * tk, AHEAD // 2 * (tk + 1)):
                    stage1(c)
                for hc in range(16):
                    top16(s_[:, tk, hc, :], sv[:, hc // 2, hc % 2, :], si[:, hc // 2, hc % 2, :], work[:, 0:128])
                cp(sif, si)
                tt(cand, bc(sv[:, :, 0, :], 3, 16), bc(sv[:, :, 1, :], 2, 16), ADD)
                for h in range(8):
                    top16(cand[:, h, :, :].rearrange("p a b -> p (a b)"), cv[:, h, :], ci[:, h, :], work)
                ts(cj[:, 0, :], ci.rearrange("p h k -> p (h k)"), 4, None, ALU.logical_shift_right, None)
                ts(cj[:, 1, :], ci.rearrange("p h k -> p (h k)"), 15, None, ALU.bitwise_and, None)
                cp(cf.rearrange("p c h k -> p c (h k)"), cj)
                for c in range(2):
                    eq = cand.rearrange("p h a b -> p (h a) b")
                    tt(eq, bc(cf[:, c, :, :].rearrange("p h k -> p (h k)"), 2, 16),
                       bc(cst[:, C_I16:C_I16 + 16], 1, 128), EQ)
                    tt(cand, cand, bc(sif[:, :, c, :], 2, 16), MUL)
                    red(ea[:, c, :], eq, ADD)
                cp(sm[:, 16:24], cv[:, :, 0])
                tt(cv, cv, bc(sm[:, 16:24], 2, 16), SUB)
                g3 = ea[:, 2, :].rearrange("p (h k) -> p h k", h=8)
                act(g3, cv, ACT.Exp, V.last())
                red(sm[:, 0:8], g3, ADD, A.last())
                recip(sm[:, 8:16], sm[:, 0:8])
                tt(g3, g3, bc(sm[:, 8:16], 2, 16), MUL)
                b = bG[tk]
                for c in range(3):
                    t = tr(b, b.ap[:, c * 128:c * 128 + 128], ea[:, c, :], V.last())
                cp(eg[:, :, tk * 128:tk * 128 + 128], b.ap[:, 0:384].rearrange("p (c t) -> p c t", c=3), t)
                b.free = [V.last()]
            cp(gsb[:, 0, :], eg[:, 2, :])
            cp(gs[:, 0, :], gsb[:, 0, :])
            tt(eg[:, 2, :], eg[:, 2, :], gs[:, 0, :], SUB)
            cp(gsb[:, 1, :], eg[:, 2, :])
            cp(gs[:, 1, :], gsb[:, 1, :])
            tt(gs[:, 2, :], eg[:, 2, :], gs[:, 1, :], SUB)
            t_g = V.last()
            v_topk = V.last()
            top[0] = mark
            Gq = [Held(ar3(32, 256)) for _ in range(2)]
            for g in Gq:
                g.free = [v_topk, t_s]
            acc = [banks[i] for i in range(4)]

            def prep_group(q, tg):
                n = q * 16 + tg
                ah, bh = Aoh[n % 3], Boh[n % 2]
                t0 = tg * 16
                if q == 0 and tg % 3:
                    ah.ready = tt(ah.ap, bc(iota, 1, 16), bc(eg[:, 0, t0:t0 + 16], 2, 128), EQ, list(ah.free), t_g)
                else:
                    for i in range(16):
                        ah.ready = ts(ah.ap[:, i, :], iota, eg[:, 0, t0 + i:t0 + i + 1], None, EQ, None,
                                      list(ah.free), t_g, q=G)
                tt(eqb, bc(iota[:, q * 32:q * 32 + 32], 1, 16), bc(eg[:, 1, t0:t0 + 16], 2, 32), EQ)
                for k in range(3):
                    tt(bh.ap[:, k, :, :], eqb, bc(gs[:, k, t0:t0 + 16], 2, 32), MUL, list(bh.free))
                bh.ready = V.last()

            def build_group(q, tg):
                n = q * 16 + tg
                ah, bh, g = Aoh[n % 3], Boh[n % 2], Gq[q % 2]
                t0 = tg * 16
                b = bG[n % 2]
                for i in range(16):
                    t = mm(b if i == 0 else None, b.ap[:, i * 32:i * 32 + 32],
                           [(ah.ap[:, i, :], bh.ap[:, k, i, :]) for k in range(3)], ah.ready, bh.ready)
                ah.free, bh.free = [t], [t]
                g.ready = act(g.ap[:, :, t0:t0 + 16].rearrange("p b t -> p t b"),
                              b.ap[:, :].rearrange("p (t b) -> p t b", t=16), ACT.Copy, t, list(g.free))
                b.free = [A.last()]

            for tg in range(16):
                prep_group(0, tg)
                build_group(0, tg)

            def weigh(c):
                ge, p_, g = gel[c % (AHEAD + 1)], pt[c % 3], Gq[(c // 32) % 2]
                p_.ready = tt(p_.ap, ge.ap, g.ap[:, c % 32, :], MUL, ge.ready, g.ready, list(p_.free))
                ge.free = [V.last()]
                if c % 32 == 31:
                    g.free = [V.last()]

            def stage2(c):
                v = up["v", c // 4]
                w = v.ap.rearrange("p (i n) -> p i n", i=4)
                p_ = pt[c % 3]
                for tk in range(2):
                    for dh in range(2):
                        b = acc[2 * tk + dh]
                        t = P.do(lambda e, b=b, tk=tk, dh=dh: e.matmul(
                            b.ap[:, :], p_.ap[:, tk * 128:tk * 128 + 128], w[:, c % 4, dh * 512:dh * 512 + 512],
                            start=(c == 0), stop=(c == 127)), p_.ready, v.ready, list(b.free) if c == 0 else None,
                            inc=(tk == 1 and dh == 1))
                p_.free = [t]
                if c % 4 == 3:
                    v.free = [t]
                return t

            for c in range(130):
                if c + AHEAD < 128:
                    stage1(c + AHEAD)
                elif c < 128 and c % 4 == 0:
                    up["v", c // 4] = load(d["peer_v"][l, c // 4], 4096)
                q = c // 32 + 1
                if c < 128:
                    weigh(c)
                    if q < 4:
                        if c % 2 == 0:
                            prep_group(q, (c % 32) // 2)
                        else:
                            build_group(q, (c % 32) // 2)
                if c >= 2:
                    t = stage2(c - 2)
            z = Gq[0].ap.rearrange("p b t -> p (b t)")[:, 0:2048].rearrange("p (t n) -> p t n", t=2)
            lst = Gq[1].ap[:, 0, 0:24].rearrange("p (a b) -> p a b", a=4)
            mv = Gq[1].ap[:, 1, 0:8].rearrange("p (a b) -> p a b", a=2)
            ln = load(d["ln"][l, 1].partition_broadcast(128), 2048)
            for tk in range(2):
                for dh in range(2):
                    b = acc[2 * tk + dh]
                    stt(z[:, tk, dh * 512:dh * 512 + 512], x3[:, tk, dh * 512:dh * 512 + 512], ALPHA, b.ap[:, :],
                        MUL, ADD, t)
                    b.free = [V.last()]
            layer_norm(z, ln.ap[:, 0:1024], ln.ap[:, 1024:2048], lst, mv, x3, ln.ready)
            ln.free = [V.last()]
            rot["set"] = list(range(8))
            rot["n"] = 0
            to_xT(x3, [V.last()])
            return t_pp_free

        def second():
            toks = fence()
            rot["set"] = list(range(8))
            t_qq = load_once(pp[:, 0:NQ_COLS], d["qq"], toks)
            for q in (P, V, A, G):
                q.fence = q.fence + [t_qq]
            keep = [0]

            def kp_(n):
                a = keep[0]
                keep[0] += n
                assert keep[0] <= 2048
                return xtok[:, a:a + n]

            def par(c, n=1):
                return pp[:, c:c + n]

            mod = kp_(96).rearrange("p (j v) -> p j v", v=2)
            coef = kp_(40).rearrange("p (k c) -> p k c", k=5)
            lb = kp_(64).rearrange("p (k d h) -> p k d h", k=4, d=2)
            sc = kp_(16)
            eps6 = cst[:, C_E6:C_E6 + 1]

            act(sc, par(Q_CC, 16), ACT.Silu)
            t_sc = A.last()
            bm = bank()
            for j in range(12):
                pc = load(d["w_mod"][j], 4096)
                w = pc.ap.rearrange("p (c n) -> p c n", c=8)
                for ct in range(4):
                    o = 2 * (4 * j + ct)
                    t = mm(bm, bm.ap[:, o:o + 2], [(w[:, dc, ct * 128:ct * 128 + 128], sc[:, 2 * dc:2 * dc + 2])
                                                   for dc in range(8)], pc.ready, t_sc)
                pc.free = [t]
            tt(mod, bm.ap[:, 0:96].rearrange("p (j v) -> p j v", v=2), bc(par(Q_BMOD, 48), 2, 2), ADD, t)
            bm.free = [V.last()]
            for k, (g, j, v) in enumerate(((Q_NMG, 8, 0), (Q_NMG, 8, 1), (Q_NFG, 32, 0))):
                stt(coef[:, k, :], mod[:, j:j + 8, v], 1.0, par(g, 8), ADD, MUL)
            l0, l1 = [pp[:, Q_LBL:Q_LBL + 32].rearrange("p (d e h) -> p d e h", d=2, e=2)[:, :, k, :] for k in (0, 1)]
            tt(lb[:, 0, :, :], l0, l1, MAX)
            tt(lb[:, 1, :, :], l0, lb[:, 0, :, :], SUB)
            tt(lb[:, 2, :, :], l1, lb[:, 0, :, :], SUB)
            act(lb[:, 1:3, :, :], lb[:, 1:3, :, :], ACT.Exp, V.last())
            tt(lb[:, 2, :, :], lb[:, 1, :, :], lb[:, 2, :, :], ADD, A.last())
            recip(lb[:, 3, :, :], lb[:, 2, :, :])
            tt(lb[:, 0, :, :], lb[:, 1, :, :], lb[:, 3, :, :], MUL)
            ts(lb[:, 1, :, :], lb[:, 0, :, :], -1.0, 1.0, MUL, ADD)

            def rms(src, n, cnt, dst, sq):
                c = src.shape[1]
                tt(sq, src, src, MUL)
                b = bank()
                t = mm(b, b.ap[:, 0:n], [(ones, sq[:, i, :]) for i in range(c)], V.last())
                act(dst, b.ap[:, 0:n], ACT.Sqrt, t, scale=1.0 / cnt, bias=eps6)
                b.free = [A.last()]
                return recip(dst, dst, A.last())

            def modulated(dst, src, k, shift, v, rstd, sq):
                rms(src, 256, 1024, rstd, sq)
                tt(sq, src, bc(rstd, 1, 8), MUL)
                for c in range(8):
                    ts(dst[:, c, :], sq[:, c, :], coef[:, k, c:c + 1], mod[:, shift + c, v:v + 1], MUL, ADD)

            def mixer():
                ym = ar3(8, 256)
                hT = ar3(8, 512)
                rstd = ar(512)
                mark0 = top[0]
                sq = ar3(8, 256)
                cT = ar3(8, 256)
                t_c = load_once(cT, d["ctxT"].rearrange("(c p) t -> p c t", p=128), toks)
                modulated(hT[:, :, 0:256], xT, 0, 0, 0, rstd[:, 0:256], sq)
                V.fence = V.fence + [t_c]
                modulated(hT[:, :, 256:512], cT, 1, 0, 1, rstd[:, 256:512], sq)
                t_h = V.last()
                fence()
                top[0] = mark0

                def project(src, n_ct, n, evac, ndc=8, rhs=None):
                    pc = load(src, ndc * n_ct * 128)
                    w = pc.ap.rearrange("p (c n) -> p c n", c=ndc)
                    r = rhs if rhs is not None else hT
                    for ct in range(n_ct):
                        b = bank()
                        t = mm(b, b.ap[:, 0:n], [(w[:, dc, ct * 128:ct * 128 + 128], r[:, dc, 0:n]) for dc in range(ndc)],
                               pc.ready, V.last() if ct == 0 else None, A.last() if ct == 0 else None)
                        b.free = [evac(ct, b.ap[:, 0:n], t)]
                    pc.free = [t]

                qn = ar3(8, 256)
                qr = ar3(8, 256)
                kn = ar3(8, 512)
                kr = ar(512)
                va = ar3(4, 1024)
                mark1 = top[0]
                qin = ar3(6, 256)
                ckv = ar3(2, 512)
                sq6 = ar3(6, 256)
                sw = ar(512)
                for j in range(2):
                    project(d["w_q"][j], 3, 256, lambda ct, ps, t, j=j: act(qin[:, 3 * j + ct, :], ps, ACT.Copy, t))

                def ev_kv(ct, ps, t):
                    return act(ckv[:, ct, :] if ct < 2 else kr, ps, ACT.Copy, t)

                project(d["w_kv"], 3, 512, ev_kv)
                V.fence = V.fence + [A.last()]
                rms(qin, 256, 768, rstd[:, 0:256], sq6)
                tt(qin, qin, bc(rstd[:, 0:256], 1, 6), MUL)
                for c in range(6):
                    ts(qin[:, c, :], qin[:, c, :], par(Q_QNG + c), None, MUL, None)
                sqk = sq6.rearrange("p c t -> p (c t)")[:, 0:1024].rearrange("p (c t) -> p c t", c=2)
                rms(ckv, 512, 256, rstd, sqk)
                tt(ckv, ckv, bc(rstd, 1, 2), MUL)
                for c in range(2):
                    ts(ckv[:, c, :], ckv[:, c, :], par(Q_KVG + c), None, MUL, None)

                perm = cst[:, C_PERM:C_PERM + 128]
                cos, sin = cst[:, C_COS:C_COS + 256], cst[:, C_SIN:C_SIN + 256]

                def rope(src, dsts, t):
                    b = bank()
                    t = mm(b, b.ap[:, 0:256], [(perm, src)], t)
                    tt(sw[:, 0:256], b.ap[:, 0:256], sin, MUL, t)
                    b.free = [V.last()]
                    tt(sw[:, 256:512], src, cos, MUL)
                    for s, o in dsts:
                        r = tt(o, sw[s, 0:256], sw[s, 256:512], ADD)
                    return r

                lo, hi, al = slice(0, 64), slice(64, 128), slice(0, 128)
                rope(kr[:, 0:256], [(al, kr[:, 0:256])], A.last())
                V.do(lambda e: e.memset(qr, 0.0))
                for j in range(2):
                    project(d["w_qb_n"][j], 4, 256, lambda ct, ps, t, j=j: act(qn[:, 4 * j + ct, :], ps, ACT.Copy, t),
                            ndc=6, rhs=qin)
                qrs = sq6

                project(d["w_qb_r"], 4, 256, lambda ct, ps, t: act(qrs[:, ct, :], ps, ACT.Copy, t), ndc=6, rhs=qin)
                for j in range(4):
                    rope(qrs[:, j, :], [(lo, qr[lo, 2 * j, :]), (hi, qr[hi, 2 * j + 1, :])], A.last())
                pc = load(d["w_kvb"], 4096)
                w = pc.ap.rearrange("p (v c n) -> p v c n", v=2, c=2)
                for h in range(8):
                    b = bank()
                    t = mm(b, b.ap[:, :], [(w[:, 0, c, h * 128:h * 128 + 128], ckv[:, c, :]) for c in range(2)],
                           pc.ready, V.last())
                    b.free = [act(kn[:, h, :], b.ap[:, :], ACT.Copy, t)]
                for k in range(4):
                    for hf in range(2):
                        b = bank()
                        t = mm(b, b.ap[:, :], [(ckv[:, c, k * 128:k * 128 + 128], w[:, 1, c, hf * 512:hf * 512 + 512])
                                               for c in range(2)])
                        b.free = [cp(va[:, k, hf * 512:hf * 512 + 512], b.ap[:, :], t)]
                pc.free = [t]
                t_kv = [A.last(), V.last()]
                top[0] = mark1
                for q in (P, V, A):
                    q.fence = q.fence + [P.last()] + t_kv
                pb = [Held(ar(512)) for _ in range(2)]
                pT = [Held(ar3(4, 256)) for _ in range(2)]
                st = ar(128)
                SC = 192.0 ** -0.5
                for h in range(8):
                    pt_ = pT[h % 2]
                    for tk in range(2):
                        n = 2 * h + tk
                        p_ = pb[n % 2]
                        ts_ = slice(tk * 128, tk * 128 + 128)
                        b = bank()
                        t = mm(b, b.ap[:, :], [(qn[:, h, ts_], kn[:, h, :]), (qr[:, h, ts_], kr)], t_kv)
                        c = 4 * n
                        red(st[:, c:c + 1], b.ap[:, :], MAX, t, neg=True)
                        ts(st[:, c + 1:c + 2], st[:, c:c + 1], SC, None, MUL, None)
                        act(p_.ap, b.ap[:, :], ACT.Exp, V.last(), list(p_.free), bias=st[:, c + 1:c + 2], scale=SC,
                            acc=st[:, c + 2:c + 3])
                        b.free = [A.last()]
                        recip(st[:, c + 3:c + 4], st[:, c + 2:c + 3], A.last())
                        ts(p_.ap, p_.ap, st[:, c + 3:c + 4], None, MUL, None)
                        t_n = V.last()
                        b = bank()
                        for k in range(4):
                            t = tr(b, b.ap[:, k * 128:k * 128 + 128], p_.ap[:, k * 128:k * 128 + 128], t_n)
                        p_.free = [t]
                        b.free = [cp(pt_.ap[:, :, ts_], b.ap[:, :].rearrange("p (k t) -> p k t", k=4), t, list(pt_.free))]
                    b = bank()
                    t = mm(b, b.ap[:, 0:256], [(va[:, k, h * 128:h * 128 + 128], pt_.ap[:, k, :]) for k in range(4)], V.last())
                    pt_.free = [t]
                    b.free = [act(ym[:, h, :], b.ap[:, 0:256], ACT.Copy, t)]
                fence()
                top[0] = mark0
                gsig = ar3(4, 256)
                for j in range(2):
                    project(d["w_hg"][10 + j], 4, 256, lambda ct, ps, t: act(gsig[:, ct, :], ps, ACT.Sigmoid, t, V.last()))
                    tt(ym[:, 4 * j:4 * j + 4, :], ym[:, 4 * j:4 * j + 4, :], gsig, MUL, A.last())
                fence()
                top[0] = mark0
                hm = ar4(2, 8, 128)
                t_hm = load_once(hm, d["hmask"].rearrange("r p (l t) -> p r l t", l=8), [q.last() for q in (P, V, A, G)])
                qh = ar3(4, 256)
                vh = ar3(4, 512)
                fk = ar4(2, 4, 256)
                gg = ar4(2, 4, 256)
                cum = ar4(2, 4, 256)
                kd = ar4(3, 4, 128)
                kdT = ar4(3, 4, 128)
                S2 = ar3(4, 128)
                S3 = ar3(4, 128)
                att = ar3(8, 128)
                Eb = [Held(ar(1024)) for _ in range(2)]
                qc = ar3(4, 256)
                ob = ar3(4, 256)
                gate = ar3(4, 256)
                sm = ar(32)
                nE = [0]
                for hh in range(2):
                    def all_done():
                        w = [q.last() for q in (P, V, A)]
                        for q in (P, V, A):
                            q.fence = q.fence + w

                    all_done()
                    project(d["w_hg"][hh], 4, 256, lambda ct, ps, t: act(qh[:, ct, :], ps, ACT.Silu, t))
                    ts(qh, qh, 128.0 ** -0.5, None, MUL, None, A.last())
                    pc = load(d["w_hg"][6 + hh], 4096)
                    w = pc.ap.rearrange("p (c n) -> p c n", c=8)
                    for k in range(4):
                        b = bank()
                        t = mm(b, b.ap[:, :], [(hT[:, dc, k * 128:k * 128 + 128], w[:, dc, :]) for dc in range(8)], pc.ready)
                        b.free = [cp(vh[:, k, :], b.ap[:, :], t)]
                    pc.free = [t]
                    for r in range(2):
                        all_done()

                        def ev_f(ct, ps, t):
                            return act(fk[:, :, ct, :], ps.rearrange("p (s t) -> p s t", s=2), ACT.Sigmoid, t)

                        project(d["w_hg"][2 + 2 * r + hh], 4, 512, ev_f)
                        for c in range(4):
                            h = 4 * hh + c
                            ts(fk[:, :, c, :], fk[:, :, c, :], lb[:, 1, r, h:h + 1], lb[:, 0, r, h:h + 1], MUL, ADD, A.last())
                        act(gg, fk, ACT.Ln, V.last())
                        ts(fk, fk, -1.0, 1.0, MUL, ADD, A.last())
                        msk = cst[:, (C_MF, C_MB)[r]:(C_MF, C_MB)[r] + 256]
                        for s in range(2):
                            for c in range(4):
                                o, m, g = cum[:, s, c, :], msk, gg[:, s, c, :]
                                if r:
                                    o, m, g = o[:, ::-1], m[:, ::-1], g[:, ::-1]
                                V.do(lambda e, o=o, m=m, g=g: e.tensor_tensor_scan(o, m, g, 0.0, MUL, ADD))
                        fst, last = (0, 127) if r == 0 else (1, 0)
                        ta = [(1, fst), (1, 1 - fst), (0, fst)]
                        for i, (s, k) in enumerate(ta):
                            cp(sm[:, 4 * i:4 * i + 4], cum[:, s, :, 128 * k + last])
                        act(sm[:, 16:20], sm[:, 8:12], ACT.Exp, V.last())
                        tt(sm[:, 0:4], sm[:, 0:4], sm[:, 4:8], ADD)
                        for i, (s, k) in enumerate(ta):
                            tt(kd[:, i, :, :], bc(sm[:, 4 * i:4 * i + 4], 2, 128), cum[:, s, :, 128 * k:128 * k + 128], SUB)
                        act(kd, kd, ACT.Exp, V.last())
                        act(qc, cum[:, 0, :, :], ACT.Exp)
                        for i, (s, k) in enumerate(ta):
                            tt(kd[:, i, :, :], kd[:, i, :, :], fk[:, s, :, 128 * k:128 * k + 128], MUL, A.last())
                        tt(qc, qc, qh, MUL)
                        t_k = V.last()
                        for i in range(3):
                            b = bank()
                            for c in range(4):
                                t = tr(b, b.ap[:, c * 128:c * 128 + 128], kd[:, i, c, :], t_k)
                            b.free = [act(kdT[:, i, :, :], b.ap[:, :].rearrange("p (c k) -> p c k", c=4), ACT.Copy, t)]
                        b2, b3 = bank(), bank()
                        for c in range(4):
                            cs = slice(c * 128, c * 128 + 128)
                            t2 = mm(b2, b2.ap[:, cs], [(kdT[:, i, c, :], vh[:, 2 + ta[i][1], cs]) for i in range(2)], A.last())
                            t3 = mm(b3, b3.ap[:, cs], [(kdT[:, 2, c, :], vh[:, fst, cs])], A.last())
                        cp(S2, b2.ap[:, :].rearrange("p (c v) -> p c v", c=4), t2)
                        b2.free = [V.last()]
                        for c in range(4):
                            stt(S3[:, c, :], S2[:, c, :], sm[:, 16 + c:17 + c], b3.ap[:, c * 128:c * 128 + 128], MUL, ADD, t3)
                        b3.free = [V.last()]
                        V.do(lambda e: e.memset(att, 0.0))
                        C = cum[:, 0, :, :].rearrange("p h t -> p (h t)")
                        K = fk[:, 0, :, :].rearrange("p h t -> p (h t)")
                        Q = qh.rearrange("p h t -> p (h t)")
                        t_kq = V.last()
                        for lv in [7] + list(range(7)):
                            if lv < 7:
                                w_ = LEVELS[lv]

                                def blk(x):
                                    return x.rearrange("p (n t) -> p n t", t=2 * w_)

                                eb = Eb[nE[0] % 2]
                                nE[0] += 1
                                e3, c3 = blk(eb.ap), blk(C)
                                f, s = slice(0, w_), slice(w_, 2 * w_)
                                if r == 0:
                                    ref = c3[:, :, w_ - 1:w_].broadcast_to([128, 512 // w_, w_])
                                    tt(e3[:, :, f], ref, c3[:, :, f], SUB, list(eb.free), t_kq, q=G)
                                    tt(e3[:, :, s], c3[:, :, s], ref, SUB, q=G)
                                else:
                                    ref = c3[:, :, w_:w_ + 1].broadcast_to([128, 512 // w_, w_])
                                    tt(e3[:, :, f], c3[:, :, f], ref, SUB, list(eb.free), t_kq, q=G)
                                    tt(e3[:, :, s], ref, c3[:, :, s], SUB, q=G)
                                act(eb.ap, eb.ap, ACT.Exp, G.last())
                                x1, x2 = (K, Q) if r == 0 else (Q, K)
                                tt(e3[:, :, f], e3[:, :, f], blk(x1)[:, :, f], MUL, A.last())
                                tt(e3[:, :, s], e3[:, :, s], blk(x2)[:, :, s], MUL)
                                ls = rs = eb.ap
                            else:
                                ls, rs = K, Q
                            t_e = V.last()
                            for u0 in (0, 4):
                                b = bank()
                                for u in range(u0, u0 + 4):
                                    us = slice(u * 128, u * 128 + 128)
                                    t = mm(b, b.ap[:, (u - u0) * 128:(u - u0) * 128 + 128], [(ls[:, us], rs[:, us])], t_e)
                                V.do(lambda e, u0=u0, b=b, lv=lv, r=r: e.copy_predicated(
                                    att[:, u0:u0 + 4, :], bc(hm[:, r, lv, :].bitcast(U32), 1, 4),
                                    b.ap[:, :].rearrange("p (u t) -> p u t", u=4)), t, t_hm)
                                b.free = [V.last()]
                            if lv < 7:
                                eb.free = [t]
                        for c0 in (0, 2):
                            b = bank()
                            for c in (c0, c0 + 1):
                                for k in range(2):
                                    o = (c - c0) * 256 + k * 128
                                    t = mm(b, b.ap[:, o:o + 128],
                                           [(vh[:, k, c * 128:c * 128 + 128], att[:, 2 * c + k, :]),
                                            ((S2 if k == fst else S3)[:, c, :], qc[:, c, k * 128:k * 128 + 128])], V.last())
                            o3 = ob[:, c0:c0 + 2, :]
                            ps = b.ap[:, :].rearrange("p (c t) -> p c t", c=2)
                            b.free = [cp(o3, ps, t) if r == 0 else tt(o3, o3, ps, ADD, t)]
                    all_done()
                    o2 = Eb[0].ap.rearrange("p (c t) -> p c t", c=4)
                    rs_ = Eb[1].ap.rearrange("p (c t) -> p c t", c=4)
                    tt(o2, ob, ob, MUL)
                    t_o2 = V.last()
                    for c0 in (0, 2):
                        b = bank()
                        t = mm(b, b.ap[:, :], [(ones, o2[:, c0:c0 + 2, :])], t_o2)
                        act(rs_[:, c0:c0 + 2, :], b.ap[:, :].rearrange("p (c t) -> p c t", c=2), ACT.Sqrt, t,
                            scale=1.0 / 128, bias=eps6)
                        b.free = [A.last()]
                    recip(rs_, rs_, A.last())
                    tt(ob, ob, rs_, MUL)
                    project(d["w_hg"][8 + hh], 4, 256, lambda ct, ps, t: act(gate[:, ct, :], ps, ACT.Silu, t))
                    stt(ob, ob, par(Q_HGN), gate, MUL, MUL, A.last())
                    project(d["w_hg"][12 + hh], 4, 256, lambda ct, ps, t: act(gate[:, ct, :], ps, ACT.Sigmoid, t, V.last()))
                    tt(ob, ob, gate, MUL, A.last())
                    tt(ym[:, 4 * hh:4 * hh + 4, :], ym[:, 4 * hh:4 * hh + 4, :], ob, ADD)
                t_y = V.last()
                for j in range(2):
                    def ev_o(ct, ps, t, j=j):
                        c = 4 * j + ct
                        return stt(xT[:, c, :], ps, mod[:, 16 + c, 0:1], xT[:, c, :], MUL, ADD, t)

                    project(d["w_o2"][j], 4, 256, ev_o, rhs=ym)
            mixer()
            fence()
            NB = 32 + EXTRA
            bd = ar(1024)
            bgu = ar(2048)
            gTt = ar(256)
            h2k = ar3(2, 1024)
            gd = ar3(2, 48)
            sl = ar3(2, 48)
            mk = ar3(2, 32)
            tri = ar(128)
            pidx = ar(8)
            selT = ar(48)
            xi = ar(16).bitcast(I32)
            tv = ar(32)
            ti = ar(16).bitcast(U32)
            tf = ar(32)
            ne = ar4(4, 1, 32).rearrange("p a o n -> p a (o n)")
            ex = ar(64)
            oh = ar3(EXTRA, 32)
            oh2 = ar3(EXTRA, 32)
            mark = top[0]
            h2 = ar3(8, 256)
            rstd = ar(256)
            sq = ar3(8, 256)
            lg = ar3(2, 32)
            V.do(lambda e: e.memset(bd, 0.0))
            V.do(lambda e: e.memset(gTt, 0.0))
            t_bd = load_once(bd[0:32, :], d["b_dn"], [V.last()])
            t_bgu = load_once(bgu[0:32, :], d["b_gu"], [V.last()])
            tt(tri, ident, iota, MUL)
            red(pidx[:, 0:1], tri, ADD)
            ts(tri, iota, pidx[:, 0:1], None, ALU.is_gt, None)
            cp(selT[:, 0:32], ident[:, 0:32])
            modulated(h2, xT, 2, 24, 0, rstd, sq)
            t_h2 = V.last()
            wr = par(Q_WR, 256).rearrange("p (c n) -> p c n", c=8)
            bl = [bank() for _ in range(2)]
            for tk in range(2):
                t = mm(bl[tk], bl[tk].ap[:, 0:32], [(h2[:, dc, tk * 128:tk * 128 + 128], wr[:, dc, :]) for dc in range(8)],
                       t_h2)
                tt(lg[:, tk, :], bl[tk].ap[:, 0:32], par(Q_BR, 32), ADD, t)
                bl[tk].free = [V.last()]

            def ev_h(a_, k, ps, t):
                tk, c0 = a_ // 8, a_ % 8
                return act(h2k[:, tk, c0 * 128:(c0 + k) * 128].rearrange("p (k t) -> p k t", k=k), ps, ACT.Copy, t)

            transposes(None, lambda i: h2[:, i % 8, (i // 8) * 128:(i // 8) * 128 + 128], 16, t_h2, evac=ev_h)
            t_h2k = A.last()
            for tk in range(2):
                V.do(lambda e, tk=tk: e.max(tv[:, 0:8], lg[:, tk, :]))
                V.do(lambda e, tk=tk: e.max_index(ti[:, 0:8], tv[:, 0:8], lg[:, tk, :]))
                cp(tf[:, 0:8], ti[:, 0:8])
                ts(tv[:, 8:9], tv[:, 0:1], -1.0, None, MUL, None)
                act(tv[:, 16:20], tv[:, 0:4], ACT.Exp, V.last(), bias=tv[:, 8:9], acc=tv[:, 20:21])
                recip(tv[:, 21:22], tv[:, 20:21], A.last())
                ts(tv[:, 16:20], tv[:, 16:20], tv[:, 21:22], None, MUL, None)
                for k in range(4):
                    o = mk[:, tk, :] if k == 0 else lg[:, tk, :]
                    ts(o, iota[:, 0:32], tf[:, k:k + 1], None, EQ, None)
                    if k == 0:
                        ts(gd[:, tk, 0:32], o, tv[:, 16:17], None, MUL, None)
                    else:
                        tt(mk[:, tk, :], mk[:, tk, :], o, ADD)
                        stt(gd[:, tk, 0:32], o, tv[:, 16 + k:17 + k], gd[:, tk, 0:32], MUL, ADD)
            t_mk = V.last()
            b = bank()
            t = tr(b, b.ap[0:32, 0:128], gd[:, 0, 0:32], t_mk)
            t = tr(b, b.ap[0:32, 128:256], gd[:, 1, 0:32])
            cp(gTt[0:32, :], b.ap[0:32, 0:256], t)
            b.free = [V.last()]
            t_g = V.last()
            b = bank()
            t = mm(b, b.ap[:, 0:32], [(tri, mk[:, 0, :])], t_mk)
            t = mm(None, b.ap[:, 32:64], [(ones, mk[:, 0, :]), (tri, mk[:, 1, :])])
            t = mm(None, b.ap[:, 64:96], [(ones, mk[:, 0, :]), (ones, mk[:, 1, :])])
            stt(sl[:, :, 0:32], b.ap[:, 0:64].rearrange("p (t n) -> p t n", t=2), 1.0, mk, ADD, MUL, t)
            ts(sl[:, :, 0:32], sl[:, :, 0:32], -1.0, None, ADD, None)
            cp(ne[:, 0, :], b.ap[:, 64:96])
            b.free = [V.last()]
            t_sl = V.last()
            top[0] = mark
            for q in (P, V, A, G):
                q.fence = q.fence + [V.last(), A.last(), P.last()]

            def further_blocks():
                cnt, nx, end, beg = [ne[:, i, :] for i in range(4)]
                kk = iota[:, 0:EXTRA]
                ek, st, off = ex[:, 0:EXTRA], ex[:, 16:16 + EXTRA], ex[:, 32:32 + EXTRA]
                ts(nx, cnt, SLOTS + 0.5, None, ALU.is_gt, None)
                for k in range(2, 256 // SLOTS):
                    stt(nx, cnt, k * SLOTS + 0.5, nx, ALU.is_gt, ADD)
                V.do(lambda e: e.tensor_tensor_scan(end, ones[:, 0:32], nx, 0.0, MUL, ADD))
                tt(beg, end, nx, SUB)
                tt(oh, bc(kk, 2, 32), bc(end, 1, EXTRA), ALU.is_ge)
                red(ek, oh, ADD)
                tt(oh, bc(ek, 2, 32), bc(iota[:, 0:32], 1, EXTRA), EQ)
                tt(oh2, oh, bc(beg, 1, EXTRA), MUL)
                red(st, oh2, ADD)
                tt(off, kk, st, SUB)
                ts(off, off, 1.0, float(SLOTS), ADD, MUL)
                for tk in range(2):
                    tt(oh2, oh, bc(sl[:, tk, 0:32], 1, EXTRA), MUL)
                    red(st, oh2, ADD)
                    tt(sl[:, tk, 32:NB], st, off, SUB)
                    tt(oh2, oh, bc(gd[:, tk, 0:32], 1, EXTRA), MUL)
                    red(gd[:, tk, 32:NB], oh2, ADD)
                ts(selT[:, 32:NB], ek, pidx[:, 0:1], None, EQ, None)
                cp(xi[:, 0:1], end[:, 31:32])
                ts(ek, ek, 31.0, None, MIN, None)
                return cp(xi[:, 1:1 + EXTRA], ek)

            acc = banks[0:4]
            rot["set"] = [4, 5, 6, 7]
            sel = [Held(ar3(2, 256)) for _ in range(2)]
            xe = [Held(ar3(8, 256)) for _ in range(2)]
            gs_ = [Held(ar3(2, 128)) for _ in range(2)]
            gsT = [Held(ar(256)) for _ in range(3)]
            gx = [Held(ar(512)) for _ in range(2)]
            ly = [Held(ar(512)) for _ in range(2)]
            sg = [Held(ar(512)) for _ in range(2)]
            aT = [Held(ar3(4, 128)) for _ in range(2)]
            ye = [Held(ar(512)) for _ in range(2)]

            def pick(j0, n, i, t_s):
                s_ = sel[i]
                w_ = n * SLOTS
                tt(s_.ap[:, :, 0:w_].rearrange("p t (n s) -> p t n s", n=n), bc(sl[:, :, j0:j0 + n], 3, SLOTS),
                   bc(bc(iota[:, 0:SLOTS], 1, n), 1, 2), EQ, list(s_.free), t_s)
                s_.ready = V.last()

            def gather(n, i):
                s_, x = sel[i], xe[i]
                w_ = n * SLOTS
                for dc in range(0, 8, 2):
                    b = bank()
                    for k in range(2):
                        t = mm(b if k == 0 else None, b.ap[:, k * 256:k * 256 + w_],
                               [(h2k[:, tk, (dc + k) * 128:(dc + k) * 128 + 128], s_.ap[:, tk, 0:w_]) for tk in range(2)],
                               s_.ready, t_h2k)
                    x.ready = act(x.ap[:, dc:dc + 2, 0:w_],
                                  b.ap[:, :].rearrange("p (k n) -> p k n", k=2)[:, :, 0:w_], ACT.Copy, t, list(x.free))
                    b.free = [A.last()]
                s_.free = [t]

            def up(j, i, k, src):
                x = xe[i]
                bb = []
                for v in range(2):
                    b = bank()
                    bb.append(b)
                    for g in range(2):
                        P.do(lambda e, b=b, v=v, g=g: e.matmul(
                            b.ap[64 * g:64 * g + 64, :], selT[0:32, j:j + 1].broadcast_to([32, 64]),
                            bgu[0:32, (2 * v + g) * 512:(2 * v + g) * 512 + 512], start=True, stop=False),
                            t_bgu, x.ready, list(b.free), inc=False)
                    for h in range(2):
                        pc = load(src("w_gu", 2 * v + h), 4096)
                        w = pc.ap.rearrange("p (c g n) -> p c g n", c=4, g=2)
                        for c in range(4):
                            for g in range(2):
                                end = c == 3 and g == 1
                                t = P.do(lambda e, b=b, w=w, c=c, g=g, h=h: e.matmul(
                                    b.ap[64 * g:64 * g + 64, :], x.ap[:, 4 * h + c, k * 64:k * 64 + 64], w[:, c, g, :],
                                    start=False, stop=(h == 1 and c == 3)), pc.ready, inc=end)
                        pc.free = [t]
                    bb[v].ready = t
                x.free = [t]
                gx_, y, z = gx[j % 2], ly[j % 2], sg[j % 2]
                ts(gx_.ap, bb[0].ap[:, :], 7.0, None, MIN, None, bb[0].ready)
                t_x = V.last()
                bb[0].free = [t_x]
                act(z.ap, gx_.ap, ACT.Sigmoid, t_x, list(z.free), scale=1.702)
                ts(y.ap, bb[1].ap[:, :], 7.0, -7.0, MIN, MAX, bb[1].ready, list(y.free))
                bb[1].free = [V.last()]
                stt(y.ap, y.ap, 1.0, gx_.ap, ADD, MUL)
                y.ready = tt(y.ap, y.ap, z.ap, MUL, A.last())
                z.free = [V.last()]
                g_ = gs_[j % 2]
                for tk in range(2):
                    g_.ready = ts(g_.ap[:, tk, :].rearrange("p (u s) -> p u s", u=2), bc(iota[:, 0:SLOTS], 1, 2),
                                  sl[:, tk, j:j + 1], gd[:, tk, j:j + 1], EQ, MUL, list(g_.free), t_sl, q=G)

            def turn(j):
                y, a, g_, gt = ly[j % 2], aT[j % 2], gs_[j % 2], gsT[j % 3]
                b = bank()
                for k in range(4):
                    t = tr(b, b.ap[:, k * 128:k * 128 + 128], y.ap[:, k * 128:k * 128 + 128], y.ready)
                y.free = [t]
                a.ready = act(a.ap, b.ap[:, :].rearrange("p (k t) -> p k t", k=4), ACT.Copy, t, list(a.free))
                b.free = [A.last()]
                b = bank()
                for tk in range(2):
                    t = tr(b, b.ap[:, tk * 128:tk * 128 + 128], g_.ap[:, tk, :], g_.ready)
                g_.free = [t]
                gt.ready = cp(gt.ap, b.ap[:, 0:256], t, list(gt.free))
                b.free = [V.last()]

            def down(j, src):
                a, y = aT[j % 2], ye[j % 2]
                b = bank()
                for hf in range(2):
                    pc = load(src("w_dn", hf), 4096)
                    w = pc.ap.rearrange("p (f n) -> p f n", f=4)
                    for f in range(4):
                        for g in range(2):
                            t = P.do(lambda e, b=b, w=w, f=f, g=g, hf=hf: e.matmul(
                                b.ap[64 * g:64 * g + 64, :], a.ap[:, f, 64 * hf:64 * hf + 64], w[:, f, g * 512:g * 512 + 512],
                                start=(hf == 0 and f == 0), stop=(hf == 1 and f == 3)),
                                pc.ready, a.ready, list(b.free), inc=(f == 3 and g == 1))
                    pc.free = [t]
                a.free = [t]
                y.ready = cp(y.ap, b.ap[:, :], t, list(y.free))
                b.free = [V.last()]

            def scatter(j):
                y, gt = ye[j % 2], gsT[j % 3]
                for tk in range(2):
                    for g in range(2):
                        t = P.do(lambda e, tk=tk, g=g: e.matmul(
                            acc[2 * tk + g].ap[:, :], gt.ap[64 * g:64 * g + 64, tk * 128:tk * 128 + 128],
                            y.ap[64 * g:64 * g + 64, :], start=(j == 0), stop=False), y.ready, gt.ready,
                            list(acc[2 * tk + g].free) if j == 0 else None, inc=(tk == 1 and g == 1))
                y.free, gt.free = [t], [t]
                return t

            pick(0, 4, 0, t_sl)
            gather(4, 0)
            for j in range(34):
                if j < 32:
                    up(j, j // 4 % 2, j % 4, lambda n, i, j=j: d[n][j, i])
                    if j % 4 == 1 and j < 29:
                        pick(j + 3, 4, (j // 4 + 1) % 2, t_sl)
                    if j % 4 == 2 and j < 30:
                        gather(4, (j // 4 + 1) % 2)
                if j == 1:
                    t_xi = further_blocks()
                if 1 <= j <= 32:
                    turn(j - 1)
                if j >= 2:
                    t = scatter(j - 2)
                if 1 <= j <= 32:
                    down(j - 1, lambda n, i, j=j: d[n][j - 1, i])
            fence()
            marks = (P, V, A, G)
            sems = [(q.sem, q.n) for q in marks]
            S.append(([t_xi], "begin", xi))
            for q in marks:
                q.ops.append((q.fence + [t_xi], "begin", xi))
                q.fence = []
                q.sem, q.n = sem(f"s_more{len(q.ops)}"), 0
            for k in range(EXTRA):
                S.append(([], "if", (k, xi)))
                for q in marks:
                    q.ops.append(([], "if", (k, None)))
                j = 32 + k
                pick(j, 1, k % 2, None)
                gather(1, k % 2)
                up(j, k % 2, 0, lambda n, i: lambda e: d[n][e, i])
                turn(j)
                down(j, lambda n, i: lambda e: d[n][e, i])
                scatter(j)
                done = [q.last() for q in marks]
                for q in marks:
                    q.ops.append((done, None, None))
            S.append(([], "end", None))
            for q, (s_, n) in zip(marks, sems):
                q.ops.append(([], "end", None))
                q.sem, q.n = s_, n
            for b in banks:
                b.free = []
            for tk in range(2):
                for dh in range(2):
                    t = P.do(lambda e, tk=tk, dh=dh: e.matmul(
                        acc[2 * tk + dh].ap[:, :], gTt[:, tk * 128:tk * 128 + 128], bd[:, dh * 512:dh * 512 + 512],
                        start=False, stop=True), t_bd)
            top[0] = mark
            rot["n"] = 0
            m = ar3(2, 1024)
            for tk in range(2):
                for dh in range(2):
                    cp(m[:, tk, dh * 512:dh * 512 + 512], acc[2 * tk + dh].ap[:, :], t)
            t_m = V.last()

            def ev_m(a_, k, ps, t):
                tk, c0 = a_ // 8, a_ % 8
                for i in range(k):
                    o = xT[:, c0 + i, tk * 128:tk * 128 + 128]
                    r = stt(o, ps[:, i, :], mod[:, 40 + c0 + i, 0:1], o, MUL, ADD, t)
                return r

            transposes(None, lambda i: m[:, i // 8, (i % 8) * 128:(i % 8) * 128 + 128], 16, t_m, evac=ev_m)
            rstd = ar(256)
            sq = ar3(8, 256)
            rms(xT, 256, 1024, rstd, sq)
            for c in range(8):
                stt(sq[:, c, :], xT[:, c, :], par(Q_FNG + c), rstd, MUL, MUL)
            t_f = V.last()

            def ev_y(a_, k, ps, t):
                tk, c0 = a_ // 8, a_ % 8
                o = m[:, tk, c0 * 128:(c0 + k) * 128].rearrange("p (k t) -> p k t", k=k)
                return cp(o, ps, t)

            transposes(None, lambda i: sq[:, i % 8, (i // 8) * 128:(i // 8) * 128 + 128], 16, t_f, evac=ev_y)
            store(out.rearrange("(t p) n -> p t n", p=128), m, V.last())

        free_pp = []
        for l in range(2):
            t_pp = load_once(pp[:, :], d["pp"][l], free_pp)
            mixing(l, t_pp)
            free_pp = [peer(l)]
        second()

        block = ctx.enter_context(nc.Block())

        @block.sync
        def _(e):
            def issue(what, sem_, regs):
                dst, src = what
                e.dma_start(dst, src(regs["e"]) if callable(src) else src).then_inc(sem_, 16)

            walk(e, S, issue)
            if n_out[0]:
                e.wait_ge(s_out, n_out[0])

        @block.tensor
        def _(e):
            P.emit(e)

        @block.vector
        def _(e):
            V.emit(e)

        @block.scalar
        def _(e):
            A.emit(e)

        @block.gpsimd
        def _(e):
            G.emit(e)



def _constants():
    c = np.zeros((128, NC_COLS), np.float32)
    i = np.arange(128)
    c[:, C_ID:C_ID + 128] = np.eye(128)
    c[:, C_ONE:C_ONE + 128] = 1.0
    c[:, C_IOTA:C_IOTA + 128] = i[None, :]
    c[:, C_I16:C_I16 + 16] = np.arange(16)[None, :]
    c[i, C_PERM + (i // 64) * 64 + (i % 64 + 32) % 64] = 1.0
    c[:, C_VAL] = i >= 31
    c[:, C_E5] = 1e-5
    c[:, C_E6] = 1e-6
    slopes = np.array([2.0 ** (-8.0 * (h + 1) / 8) for h in range(8)], np.float32)
    end = np.arange(15) * 16 + 31
    for tk in range(2):
        t = tk * 128 + i
        dist = (t[:, None] - end[None, :]).astype(np.float32)
        b = np.where(dist[:, None, :] >= 0, -slopes[None, :, None] * np.abs(dist)[:, None, :], np.float32(-1e30))
        c[:, C_CB + tk * 120:C_CB + tk * 120 + 120] = b.reshape(128, 120)
    t = np.arange(256)
    c[:, C_MF:C_MF + 256] = (t % 128 != 0)[None, :]
    c[:, C_MB:C_MB + 256] = (t % 128 != 127)[None, :]
    inv = np.float32(10000.0) ** (-np.arange(16, dtype=np.float32) / np.float32(16))
    ang = np.concatenate([(t // 64).astype(np.float32)[:, None] * inv, (t % 64).astype(np.float32)[:, None] * inv], -1)
    cos, sin = np.cos(ang).astype(np.float32).T, np.sin(ang).astype(np.float32).T
    c[:, C_COS:C_COS + 256] = np.concatenate([cos, cos, cos, cos])
    c[:, C_SIN:C_SIN + 256] = np.concatenate([-sin, sin, -sin, sin])
    dist = 128 + i[:, None] - t[None, :]
    alibi = np.where(dist[:, None, :] >= 0, -slopes[None, :, None] * dist[:, None, :].astype(np.float32),
                     np.float32(-1e30)).astype(np.float32).reshape(128, 2048)
    m = np.zeros((2, 128, 8, 128), np.float32)
    for l, w in enumerate(LEVELS):
        same = (i[:, None] // (2 * w)) == (i[None, :] // (2 * w))
        first = (i % (2 * w)) < w
        m[0, :, l, :] = same & first[:, None] & ~first[None, :]
        m[1, :, l, :] = same & ~first[:, None] & first[None, :]
    m[:, :, 7, :] = np.eye(128)
    return c, alibi, m.reshape(2, 128, 1024)


def _cols(v, n):
    return v.reshape(n, 128).T


def _rows(w):
    return w.reshape(-1, 128, w.shape[1]).transpose(1, 0, 2).reshape(128, -1)


def _layout(x):
    a = {}
    a["cst"], a["alibi"], a["hmask"] = _constants()
    a["x"] = x["x"][0]
    a["xT"] = x["x"][0].T
    head = np.concatenate([np.concatenate([np.arange(64) + 64 * j, np.arange(64) + 64 * (4 + j)]) for j in range(4)])
    order = np.concatenate([np.arange(1024), 1024 + head, np.arange(1536, 1920), np.arange(2048, 2176)])
    tok = np.concatenate([np.arange(1920, 2048), np.arange(2176, 2328)])
    w = x["w_in"]
    a["w_inA"] = np.stack([np.stack([_rows(w[l][:, order[512 * j:512 * j + 512]]) for j in range(4)]) for l in range(2)])
    a["w_inB"] = np.stack([_rows(w[l][:, tok]) for l in range(2)])
    a["cmp_w1"] = np.stack([np.stack([np.concatenate([x[n][l].reshape(32, 64, 64).transpose(1, 0, 2)] * 2)
                                      .reshape(128, 2048) for n in ("cmpk_w1", "cmpv_w1")]) for l in range(2)])
    pp = np.zeros((2, 128, NP_COLS), np.float32)
    for l in range(2):
        p = pp[l]
        p[:, P_BIN:P_BIN + 16] = _cols(x["b_in"][l][order], 16)
        p[:, P_CW:P_CW + 16] = x["conv_w"][l].reshape(4, 4, 128).transpose(2, 0, 1).reshape(128, 16)
        for c, n in ((P_CB, "conv_b"), (P_BA, "lru_ba"), (P_BX, "lru_bx"), (P_LAM, "lru_lambda"), (P_GL, "gn_lru_g"),
                     (P_GN, "gn_nsa_g")):
            p[:, c:c + 4] = _cols(x[n][l], 4)
        p[:, P_POSK:P_POSK + 32] = np.concatenate([x["cmp_pos_k"][l].T] * 2)
        p[:, P_POSV:P_POSV + 32] = np.concatenate([x["cmp_pos_v"][l].T] * 2)
        for c, n in ((P_B1K, "cmpk_b1"), (P_B2K, "cmpk_b2"), (P_B1V, "cmpv_b1")):
            p[:, c] = np.concatenate([x[n][l]] * 2)
        p[:, P_B2V:P_B2V + 64] = x["cmpv_b2"][l][None, :]
        p[:, P_BTOK:P_BTOK + 280] = x["b_in"][l][tok][None, :]
        p[0:64, P_W2K:P_W2K + 128] = np.concatenate([x["cmpk_w2"][l]] * 2, 1)
        p[0:64, P_W2V:P_W2V + 64] = x["cmpv_w2"][l]
        p[:, P_SK:P_SK + 256] = x["peer_subkeys"][l].transpose(2, 0, 1).reshape(128, 256)
        for c, n in ((P_WA, "lru_wa"), (P_WX, "lru_wx")):
            for b in range(8):
                s = 64 * (b % 2)
                p[s:s + 64, c + 128 * (b // 2) + s:c + 128 * (b // 2) + s + 64] = x[n][l][b]
    a["pp"] = pp
    a["ln"] = np.stack([np.stack([np.concatenate([x["ln1_g"][l], x["ln1_b"][l]]),
                                  np.concatenate([x["ln2_g"][l], x["ln2_b"][l]])]) for l in range(2)])
    a["w_out"] = np.stack([np.stack([_rows(x["w_out"][l][512 * k:512 * k + 512]) for k in range(2)]) for l in range(2)])
    a["peer_wq"] = np.stack([np.stack([_rows(x["peer_wq"][l][:, 512 * j:512 * j + 512]) for j in range(4)])
                             for l in range(2)])
    a["peer_u"] = x["peer_u"].reshape(2, 128, 32, 4, 8, 128).transpose(0, 2, 5, 3, 4, 1).reshape(2, 32, 128, 4096)
    a["peer_v"] = x["peer_v"].reshape(2, 128, 32, 4096).transpose(0, 2, 1, 3)
    _layout2(x, a)
    return {k: np.ascontiguousarray(v) for k, v in a.items()}


def _layout2(x, a):
    x = {k[:-2]: v for k, v in x.items() if k.endswith("_2")}
    a["ctxT"] = x["ctx"][0].T
    q = np.zeros((128, NQ_COLS), np.float32)
    q[:, Q_CC:Q_CC + 16] = np.stack([_cols(x["c"][0], 8), _cols(x["c_ctx"], 8)], -1).reshape(128, 16)
    q[:, Q_BMOD:Q_BMOD + 48] = _cols(x["b_mod"][0], 48)
    q[:, Q_NMG:Q_NMG + 8] = _cols(x["norm_mix_g"][0], 8)
    q[:, Q_QNG:Q_QNG + 6] = _cols(x["mla_q_norm_g"][0], 6)
    q[:, Q_KVG:Q_KVG + 2] = _cols(x["mla_kv_norm_g"][0], 2)
    q[:, Q_LBL:Q_LBL + 32] = x["hg_lb_logits"].reshape(2, 2, 8, 128).transpose(3, 0, 1, 2).reshape(128, 32)
    q[:, Q_HGN] = x["hg_norm_g"][0]
    q[:, Q_NFG:Q_NFG + 8] = _cols(x["norm_ffn_g"][0], 8)
    q[:, Q_BR:Q_BR + 32] = x["b_router"][0][None, :]
    q[:, Q_WR:Q_WR + 256] = _rows(x["w_router"][0])
    q[:, Q_FNG:Q_FNG + 8] = _cols(x["final_norm_g"], 8)
    a["qq"] = q
    w = x["w_mod"][0]
    a["w_mod"] = np.stack([_rows(w[:, 512 * j:512 * j + 512]) for j in range(12)])
    w = x["w_in"][0]
    a["w_q"] = np.stack([_rows(w[:, 384 * j:384 * j + 384]) for j in range(2)])
    a["w_kv"] = _rows(np.concatenate([w[:, 768:1088], w[:, 1024:1088]], 1))
    a["w_hg"] = np.stack([_rows(w[:, 1088 + 512 * j:1088 + 512 * j + 512]) for j in range(14)])
    w = x["w_q_b"][0].reshape(768, 8, 192)
    a["w_qb_n"] = np.stack([_rows(w[:, 4 * j:4 * j + 4, 0:128].reshape(768, 512)) for j in range(2)])
    a["w_qb_r"] = _rows(w[:, :, 128:192].reshape(768, 512))
    w = x["w_kv_b"][0].reshape(256, 8, 256)
    a["w_kvb"] = np.concatenate([_rows(w[:, :, 0:128].reshape(256, 1024)), _rows(w[:, :, 128:256].reshape(256, 1024))], 1)
    a["w_o2"] = np.stack([_rows(x["w_out"][0][:, 512 * j:512 * j + 512]) for j in range(2)])
    a["w_gu"] = x["w_gate_up"][0].reshape(32, 2, 4, 128, 2, 512, 2).transpose(0, 6, 1, 3, 2, 4, 5).reshape(32, 4, 128, 4096)
    a["b_gu"] = x["b_gate_up"][0].reshape(32, 1024, 2).transpose(0, 2, 1).reshape(32, 2048)
    a["w_dn"] = x["w_down"][0].reshape(32, 2, 4, 128, 1024).transpose(0, 1, 3, 2, 4).reshape(32, 2, 128, 4096)
    a["b_dn"] = x["b_down"][0]


def kernel(**inputs):
    import concourse.bacc as _bacc
    from concourse.bass_utils import run_bass_kernel_spmd as _run

    nc = _bacc.Bacc("TRN2", target_bir_lowering=False, num_devices=1)
    arrays, args = {}, {}
    for name, a in _layout({k: np.asarray(v) for k, v in inputs.items()}).items():
        arrays[f"in_{name}_dram"] = a
        args[name] = nc.dram_tensor(f"in_{name}_dram", a.shape, F32, kind="ExternalInput").ap()
    out = nc.dram_tensor("out_0_dram", (256, 1024), F32, kind="ExternalOutput").ap()
    build(nc, args, out)
    r = _run(nc, [arrays], core_ids=[0])
    return r.results[0]["out_0_dram"].reshape(1, 256, 1024)
```

```python
from contextlib import ExitStack

import numpy as np
import concourse.bass as bass
from concourse import mybir

F32 = mybir.dt.float32
BF16 = mybir.dt.bfloat16
F32R = mybir.dt.float32r
U32 = mybir.dt.uint32
I32 = mybir.dt.int32
ALU = mybir.AluOpType
ACT = mybir.ActivationFunctionType
AX = mybir.AxisListType

ALPHA = 4.0 ** 0.25
NSLOT = 3
PIECE = 4096
AHEAD = 12
EARLY = 12
SLOTS = 64
EXTRA = 15
LEVELS = [64, 32, 16, 8, 4, 2, 1]

C_ID, C_ONE, C_IOTA, C_I16, C_PERM, C_VAL, C_E5, C_E6, C_CB, C_MF, C_MB, C_COS, C_SIN = (
    0, 128, 256, 384, 400, 528, 529, 530, 531, 771, 1027, 1283, 1539)
NC_COLS = 1795
(P_BIN, P_CW, P_CB, P_BA, P_BX, P_LAM, P_POSK, P_POSV, P_B1K, P_B2K, P_B1V, P_GL, P_GN, P_B2V, P_BTOK,
 P_W2K, P_W2V, P_SK, P_WA, P_WX) = (0, 16, 32, 36, 40, 44, 48, 80, 112, 113, 114, 115, 119, 123, 187,
                                    467, 595, 659, 915, 1427)
NP_COLS = 1939
(Q_NMG, Q_QNG, Q_KVG, Q_LBL, Q_HGN, Q_NFG, Q_BR, Q_WR, Q_FNG) = (
    0, 8, 14, 16, 48, 49, 57, 89, 345)
NQ_COLS = 353


class Queue:

    def __init__(self, sem, in_order):
        self.sem, self.in_order, self.n, self.ops, self.fence, self.lag = sem, in_order, 0, [], [], 0

    def do(self, fn, *waits, inc=True):
        w = list(waits) + self.fence
        self.fence = []
        if self.in_order and self.n:
            w.append((self.sem, self.n - self.lag))
        self.ops.append((w, fn, self.sem if inc else None))
        if inc:
            self.n += 1
        return (self.sem, self.n + (not inc))

    def last(self):
        return (self.sem, self.n)

    def emit(self, eng):
        walk(eng, self.ops, lambda fn, inc, regs: self.issue(eng, fn, inc))

    def issue(self, eng, fn, inc):
        r = fn(eng)
        if inc:
            r.then_inc(inc, 1)


def walk(eng, ops, issue):
    seen, saved, stack, regs = {}, None, None, {}

    def wait(w):
        if w is None:
            return
        if isinstance(w, list):
            for x in w:
                wait(x)
            return
        s, v = w
        if v > seen.get(s, 0):
            eng.wait_ge(s, v)
            seen[s] = v

    for w, what, extra in ops:
        if what == "end":
            stack.close()
            seen = saved
            continue
        wait(list(w))
        if what == "begin":
            regs["n"] = eng.value_load(extra[0:1, 0:1], min_val=0, max_val=EXTRA)
            saved, stack = dict(seen), ExitStack()
        elif what == "if":
            k, ap = extra
            stack.enter_context(eng.If(regs["n"] > k))
            if ap is not None:
                regs["e"] = eng.value_load(ap[0:1, k + 1:k + 2], min_val=0, max_val=31)
        elif what is not None:
            issue(what, extra, regs)


class Held:

    def __init__(self, ap):
        self.ap, self.ready, self.free = ap, None, []


def bc(ap, axis, n):
    ap = ap.unsqueeze(axis)
    shape = list(ap.shape)
    shape[axis] = n
    return ap.broadcast_to(shape)


def build(nc, d, out):
    with ExitStack() as ctx:
        def sb(name, cols, dt=F32):
            return ctx.enter_context(nc.sbuf_tensor(name, [128, cols], dt))

        def sem(name):
            return ctx.enter_context(nc.semaphore(name))

        P = Queue(sem("s_pe"), False)
        V = Queue(sem("s_dve"), True)
        A = Queue(sem("s_act"), True)
        G = Queue(sem("s_pool"), True)
        S = []
        ring = sb("ring", NSLOT * PIECE)
        s_ring = [sem(f"s_ring{i}") for i in range(NSLOT)]
        xtok = sb("xtok", 2048)
        xT_t = sb("xT", 2048)
        cst = sb("cst", NC_COLS)
        pp = sb("pp", NP_COLS)
        mq = sb("mq", 64)
        mod_t = sb("mod", 96)
        sc_t = sb("sc", 256)
        mod = mod_t[:, :].rearrange("p (j v) -> p j v", v=2)
        sc = sc_t[:, :].rearrange("p (c r) -> p c r", r=32)
        ARENA = (212800 - 4 * (NSLOT * PIECE + 4096 + NC_COLS + NP_COLS + 416 + 5632)) // 4 // 8 * 8
        arena = sb("arena", ARENA)
        vhi_t, vlo_t = sb("vhi", 2048, F32R), sb("vlo", 2048, F32R)
        phi_t, plo_t = sb("phi", 768, F32R), sb("plo", 768, F32R)
        banks = [Held(ctx.enter_context(nc.psum_tensor(f"bank{i}", [128, 512], F32))) for i in range(8)]
        x3 = xtok[:, :].rearrange("p (t n) -> p t n", t=2)
        xT = xT_t[:, :].rearrange("p (c t) -> p c t", c=8)

        top = [0]

        def fence():
            toks = [q.last() for q in (P, V, A, G)]
            for q in (P, V, A, G):
                q.fence = q.fence + toks
            top[0] = 0
            return toks

        def ar(cols, dt=F32):
            a = top[0]
            top[0] += (cols + 7) // 8 * 8
            assert top[0] <= ARENA, (top[0], ARENA)
            return arena[:, a:a + cols]

        def ar3(a, b):
            return ar(a * b).rearrange("p (a b) -> p a b", a=a)

        def ar4(a, b, c):
            return ar(a * b * c).rearrange("p (a b c) -> p a b c", a=a, b=b)

        slots = [ring[:, i * PIECE:(i + 1) * PIECE] for i in range(NSLOT)]
        uses = [[] for _ in range(NSLOT)]
        n_load = [0]

        def more_slots(n):
            for _ in range(n):
                slots.append(ar(PIECE))
                uses.append([])
                s_ring.append(sem(f"s_ring{len(s_ring)}"))
            n_load[0] = NSLOT

        def load(src, cols):
            i = n_load[0] % len(slots)
            n_load[0] += 1
            h = Held(slots[i][:, 0:cols])
            prev = uses[i][-1] if uses[i] else None
            uses[i].append(h)
            h.ready = (s_ring[i], 16 * len(uses[i]))
            assert prev is None or prev.free
            S.append((prev.free if prev else [], (h.ap, src), s_ring[i]))
            return h

        n_once = [0]

        def load_once(dst, src, waits=()):
            n_once[0] += 1
            s = sem(f"s_once{n_once[0]}")
            S.append((list(waits), (dst, src), s))
            return (s, 16)

        s_out = sem("s_out")
        n_out = [0]

        def store(dst, src, *waits):
            n_out[0] += 16
            S.append((list(waits), (dst, src), s_out))


        rot = {"n": 0, "set": list(range(8))}

        def bank():
            b = banks[rot["set"][rot["n"] % len(rot["set"])]]
            rot["n"] += 1
            return b

        def mm(b, o, pairs, *waits):
            w = list(waits) + [list(b.free)] if b is not None else list(waits)
            n = len(pairs)
            t = None
            for i, (l, r) in enumerate(pairs):
                t = P.do(lambda e, l=l, r=r, i=i: e.matmul(o, l, r, start=(i == 0), stop=(i == n - 1)),
                         *(w if i == 0 else ()), inc=(i == n - 1))
            return t

        def tr(b, o, src, *waits):
            n = src.shape[0]
            return P.do(lambda e: e.transpose(o, src, ident[0:n, 0:n]), *waits, list(b.free))

        def act(o, i, f, *w, bias=None, scale=1.0, acc=None):
            kw = {}
            if bias is not None:
                kw["bias"] = bias
            if acc is not None:
                kw["accum_out"] = acc
            return A.do(lambda e: e.activation(o, i, f, scale=scale, **kw), *w)

        def tt(o, a, b, op, *w, q=None):
            return (q or V).do(lambda e: e.tensor_tensor(o, a, b, op), *w)

        def ts(o, a, s1, s2, o1, o2, *w, q=None):
            if o2 is None:
                return (q or V).do(lambda e: e.tensor_scalar(o, a, s1, None, o1), *w)
            return (q or V).do(lambda e: e.tensor_scalar(o, a, s1, s2, o1, o2), *w)

        def stt(o, a, s, b, o1, o2, *w):
            return V.do(lambda e: e.scalar_tensor_tensor(out=o, in0=a, scalar=s, in1=b, op0=o1, op1=o2), *w)

        def cp(o, i, *w, q=None):
            return (q or V).do(lambda e: e.tensor_copy(o, i), *w)

        def red(o, i, op, *w, neg=False):
            return V.do(lambda e: e.tensor_reduce(o, i, AX.X, op, negate=neg), *w)

        def recip(o, i, *w):
            return V.do(lambda e: e.reciprocal(o, i), *w)

        MUL, ADD, SUB, MAX, MIN, EQ = ALU.mult, ALU.add, ALU.subtract, ALU.max, ALU.min, ALU.is_equal

        ident = cst[:, C_ID:C_ID + 128]
        ones = cst[:, C_ONE:C_ONE + 128]
        iota = cst[:, C_IOTA:C_IOTA + 128]
        t_xT = load_once(xT, d["xT"].rearrange("(c p) t -> p c t", p=128))
        P.fence = [t_xT]

        def first_loads():
            ts_ = [load_once(cst[:, :], d["cst"]), load_once(x3, d["x"].rearrange("(t p) n -> p t n", p=128)),
                   load_once(mq[:, :], d["mq"])]
            for q in (P, V, A, G):
                q.fence = q.fence + ts_

        mods = {"j": 0, "p": None}

        def mod_step(more=True):
            j = mods["j"]
            if j % 6 == 0 and more:
                mods["t"] = [ar(128) for _ in range(2)]
            if j == 0:
                V.do(lambda e: e.memset(sc, 0.0))
                mods["sc"] = act(sc[:, :, 0:2], mq[:, 0:16].rearrange("p (c v) -> p c v", v=2), ACT.Silu, V.last())
            if mods["p"] is not None:
                b = bank()
                t = tr(b, b.ap[:, 0:128], mods["t"][(j - 1) % 2], mods["p"])
                b.free = [tt(mod[:, 4 * j - 4:4 * j, :],
                             b.ap[:, 0:128].rearrange("p (g r) -> p g r", g=4)[:, :, 0:2],
                             bc(mq[:, 16 + 4 * j - 4:16 + 4 * j], 2, 2), ADD, t)]
            mods["p"] = None
            if more:
                mods["j"] += 1
                pc = load(d["w_mod"][j], 4096)
                w = pc.ap.rearrange("p (c n) -> p c n", c=8)
                b = bank()
                for dc in range(8):
                    for g in range(4):
                        end = dc == 7 and g == 3
                        t = P.do(lambda e, dc=dc, g=g: e.matmul(
                            b.ap[32 * g:32 * g + 32, 0:128], sc[:, dc, :], w[:, dc, g * 128:g * 128 + 128],
                            start=(dc == 0), stop=(dc == 7)), pc.ready, mods["sc"], list(b.free), inc=end)
                pc.free = [t]
                mods["p"] = cp(mods["t"][j % 2], b.ap[:, 0:128], t)
                b.free = [V.last()]

        def transposes(dst4, src, n, *waits, evac=None):
            last = None
            for a in range(0, n, 4):
                b = bank()
                k = min(4, n - a)
                for j in range(k):
                    t = tr(b, b.ap[:, j * 128:j * 128 + 128], src(a + j), *(waits if a == 0 and j == 0 else ()))
                last = evac(a, k, b.ap[:, 0:k * 128].rearrange("p (k t) -> p k t", k=k), t)
                b.free = [last]
            return last

        def layer_norm(z, g_ap, b_ap, st, mv, dst, *w):
            for t in range(2):
                V.do(lambda e, t=t: e.bn_stats(st[:, 2 * t, :], z[:, t, 0:512]), *w)
                V.lag = 1
                V.do(lambda e, t=t: e.bn_stats(st[:, 2 * t + 1, :], z[:, t, 512:1024]))
                V.lag = 0
                V.do(lambda e, t=t: e.bn_aggr(mv[:, t, 0:2], st[:, 2 * t:2 * t + 2, :]))
                act(mv[:, t, 2:3], mv[:, t, 1:2], ACT.Sqrt, V.last(), bias=cst[:, C_E5:C_E5 + 1])
            for t in range(2):
                recip(mv[:, t, 3:4], mv[:, t, 2:3], A.last())
                ts(z[:, t, :], z[:, t, :], mv[:, t, 0:1], mv[:, t, 3:4], SUB, MUL)
                tt(z[:, t, :], z[:, t, :], g_ap, MUL)
                tt(dst[:, t, :], z[:, t, :], b_ap, ADD)
                to_xT(dst, t, [V.last()])
            return V.last()

        def to_xT(src3, tk, waits):
            def evac(a, k, ps, t):
                return act(xT[:, a:a + k, tk * 128:tk * 128 + 128], ps, ACT.Copy, t)
            transposes(None, lambda i: src3[:, tk, i * 128:i * 128 + 128], 8, *waits, evac=evac)

        def mixing(l, waits_pp):
            fence()
            xpad = ar3(4, 259)
            gT = ar3(4, 256)
            qT = ar3(4, 256)
            kT = ar3(4, 256)
            vtok = ar3(2, 256)
            gates = ar3(2, 24)
            alibi = ar3(8, 256)
            xc = ar3(4, 256)
            r = ar3(4, 256)
            ig = ar3(4, 256)
            aa = ar3(4, 256)
            th = ar3(4, 256)
            sp = ar(32)
            ss = ar(16)
            z = ar3(2, 1024)
            lst = ar3(4, 6)
            mv = ar3(2, 4)
            rot["set"] = list(range(8))

            def par(c, n=1):
                return pp[:, c:c + n]

            def conv():
                for ct in range(4):
                    for j in range(4):
                        src = xpad[:, ct, j:j + 256]
                        wj = par(P_CW + 4 * j + ct)
                        if j == 0:
                            ts(xc[:, ct, :], src, wj, par(P_CB + ct), MUL, ADD, t_in[0])
                        else:
                            stt(xc[:, ct, :], src, wj, xc[:, ct, :], MUL, ADD)
                return V.last()

            def softplus():
                lam = par(P_LAM, 4)
                ts(sp[:, 0:4], lam, -1.0, None, MUL, None, t_pp)
                tt(sp[:, 4:8], lam, sp[:, 0:4], MIN)
                act(sp[:, 8:12], sp[:, 4:8], ACT.Exp, V.last())
                ts(sp[:, 12:16], sp[:, 8:12], 2.0, None, ADD, None, A.last())
                recip(sp[:, 16:20], sp[:, 12:16])
                tt(sp[:, 12:16], sp[:, 8:12], sp[:, 16:20], MUL)
                tt(sp[:, 16:20], sp[:, 12:16], sp[:, 12:16], MUL)
                V.do(lambda e: e.memset(sp[:, 20:24], 2.0 / 17))
                for c in (15, 13, 11, 9, 7, 5, 3, 1):
                    tt(sp[:, 20:24], sp[:, 20:24], sp[:, 16:20], MUL)
                    ts(sp[:, 20:24], sp[:, 20:24], 2.0 / c, None, ADD, None)
                tt(sp[:, 20:24], sp[:, 20:24], sp[:, 12:16], MUL)
                ts(sp[:, 0:4], sp[:, 0:4], 0.0, None, MAX, None)
                tt(sp[:, 20:24], sp[:, 20:24], sp[:, 0:4], ADD)
                ts(sp[:, 20:24], sp[:, 20:24], -8.0, None, MUL, None)

            def lru_gates():
                for wcol, bcol, dst in ((P_WA, P_BA, r), (P_WX, P_BX, ig)):
                    for ct in range(4):
                        b = bank()
                        t = mm(b, b.ap[:, 0:256], [(par(wcol + 128 * ct, 128), xc[:, ct, :])], t_xc)
                        b.free = [act(dst[:, ct, :], b.ap[:, 0:256], ACT.Sigmoid, t, bias=par(bcol + ct))]
                t_ri = A.last()
                for ct in range(4):
                    ts(r[:, ct, :], r[:, ct, :], sp[:, 20 + ct:21 + ct], None, MUL, None, t_ri)
                tt(ig, ig, xc, MUL)
                t1 = V.last()
                act(th, r, ACT.Tanh, t1, scale=-1.0)
                act(aa, r, ACT.Exp)
                return A.last()

            def lru_scan():
                ts(r, th, 1.0, None, ADD, None, t_ta)
                recip(r, r)
                tt(r, r, th, MUL)
                act(th, r, ACT.Sqrt, V.last(), scale=2.0)
                tt(ig, ig, th, MUL, A.last())
                for ct in range(4):
                    V.do(lambda e, ct=ct: e.tensor_tensor_scan(xc[:, ct, :], aa[:, ct, :], ig[:, ct, :], 0.0, MUL, ADD))
                tt(xc, xc, gT, MUL, t_gelu)
                tt(th, xc, xc, MUL)
                for ct in range(4):
                    ts(ylT[:, ct, :], xc[:, ct, :], par(P_GL + ct), None, MUL, None)
                return V.last()

            def lru_norm():
                b = bank()
                for tk in range(2):
                    t = mm(b if tk == 0 else None, b.ap[:, tk:tk + 1],
                           [(th[:, ct, tk * 128:tk * 128 + 128], ones[:, 0:1]) for ct in range(4)], t_yl)
                act(ss[:, 0:2], b.ap[:, 0:2], ACT.Sqrt, t, scale=1.0 / 512, bias=cst[:, C_E5:C_E5 + 1])
                b.free = [A.last()]
                recip(ss[:, 2:4], ss[:, 0:2], A.last())

            V.do(lambda e: e.memset(xpad[:, :, 0:3], 0.0))
            ylT = xpad[:, :, 0:256]
            t_in = []
            for j in range(4):
                pc = load(d["w_inA"][l, j], 4096)
                if j == 0:
                    t_pp = load_once(pp[:, :], d["pp"][l], waits_pp)
                    if l == 0:
                        first_loads()
                    softplus()
                w = pc.ap.rearrange("p (c n) -> p c n", c=8)
                e1 = [None, None]
                for half in range(2):
                    b = bank()
                    for k in range(2):
                        ct = half * 2 + k
                        t = mm(b if k == 0 else None, b.ap[:, k * 256:k * 256 + 256],
                               [(w[:, dc, ct * 128:ct * 128 + 128], xT[:, dc, :]) for dc in range(8)], pc.ready)
                    for k in range(2):
                        ct = half * 2 + k
                        dst = [xpad[:, ct, 3:259], gT[:, ct, :], qT[:, ct, :], kT[:, ct, :]][j]
                        src = b.ap[:, k * 256:k * 256 + 256]
                        if half:
                            e1[1] = ts(dst, src, par(P_BIN + 4 * j + ct), None, ADD, None, t, t_pp)
                        else:
                            e1[0] = act(dst, src, ACT.Identity, t, t_pp, bias=par(P_BIN + 4 * j + ct))
                    b.free = [e1[half]]
                pc.free = [t]
                t_in.append(e1)
                if j == 0:
                    t_xc = conv()
                if j == 1:
                    t_gelu = act(gT, gT, ACT.Gelu_apprx_tanh, t_in[1])
                    t_ta = lru_gates()
                if j == 2:
                    t_yl = lru_scan()
            pc = load(d["w_inB"][l], 2240)
            w = pc.ap.rearrange("p (c n) -> p c n", c=8)
            for tk in range(2):
                b = bank()
                t = mm(b, b.ap[:, 0:280], [(xT[:, dc, tk * 128:tk * 128 + 128], w[:, dc, :]) for dc in range(8)],
                       pc.ready)
                tt(vtok[:, tk, :], b.ap[:, 0:256], par(P_BTOK, 256), ADD, t)
                tt(gates[:, tk, :], b.ap[:, 256:280], par(P_BTOK + 256, 24), ADD)
                b.free = [V.last()]
            pc.free = [t]
            t_v = V.last()
            t_gates = act(gates, gates, ACT.Sigmoid, t_v)
            t_al = load_once(alibi, d["alibi"].rearrange("p (h k) -> p h k", h=8))

            lnb = ar(2048)
            t_ln = load_once(lnb, d["ln"][l, 0].partition_broadcast(128))

            gk = ar(32)
            kcT = ar(16)
            vc = ar(128)
            kzs = [ar(32 * 30).rearrange("p (j g c) -> p j g c", j=32, g=2) for _ in range(2)]

            def compress(n):
                pos, b1, w2 = ((P_POSK, P_B1K, P_W2K), (P_POSV, P_B1V, P_W2V))[n]
                kz = kzs[n]
                pc = load(d["cmp_w1"][l, n], 2048)
                w1 = pc.ap.rearrange("p (j e) -> p j e", j=32)
                b = bank()
                t = mm(b, b.ap[0:64, 0:30], [(w1[:, j, :], kz[:, j, :, :]) for j in range(32)], pc.ready, t_kz)
                pc.free = [t]
                act(gk[0:64, 0:30], b.ap[0:64, 0:30], ACT.Gelu_apprx_tanh, t, bias=pp[0:64, b1:b1 + 1])
                b.free = [A.last()]
                if n == 0:
                    b = bank()
                    t = mm(b, b.ap[:, 0:30], [(pp[0:64, w2:w2 + 128], gk[0:64, 0:30])], A.last())
                    for g in range(2):
                        s = slice(64 * g, 64 * g + 64)
                        ts(kcT[s, 0:15], b.ap[s, 15 * g:15 * g + 15], pp[s, P_B2K:P_B2K + 1], None, ADD, None, t)
                    b.free = [V.last()]
                else:
                    b = bank()
                    for g in range(2):
                        t = mm(b if g == 0 else None, b.ap[0:15, 64 * g:64 * g + 64],
                               [(gk[0:64, 15 * g:15 * g + 15], pp[0:64, w2:w2 + 64])], A.last())
                    tt(vc[0:15, :].rearrange("p (g d) -> p g d", g=2),
                       b.ap[0:15, 0:128].rearrange("p (g d) -> p g d", g=2),
                       bc(pp[0:15, P_B2V:P_B2V + 64], 1, 2), ADD, t)
                    b.free = [V.last()]
                return V.last()

            sbuf = [Held(ar3(8, 256)) for _ in range(2)]
            pbuf = [Held(ar4(2, 8, 128)) for _ in range(2)]
            sts = [ar(32) for _ in range(2)]
            osum = xc.rearrange("p a b -> p (a b)").rearrange("p (t n) -> p t n", t=2)
            tmp = r[:, 0:2, :].rearrange("p a b -> p (a b)").rearrange("p (h d) -> p h d", h=8)
            its = [(0, 1), (0, 2), (1, 1), (1, 2), (0, 0), (1, 0)]

            def scores(i):
                tk, br = its[i]
                s, st = sbuf[i % 2], sts[i % 2]
                nk = 15 if br == 0 else 128 * (tk + 1)
                per = 4 if br == 0 else 2
                for g in range(2):
                    for j0 in range(0, 4, per):
                        b = bank()
                        for jj in range(per):
                            j = j0 + jj
                            sl = slice(64 * g, 64 * g + 64)
                            key = kcT[sl, 0:15] if br == 0 else kT[sl, 1 + br, 0:nk]
                            t = mm(b if jj == 0 else None, b.ap[:, jj * nk:jj * nk + nk],
                                   [(qT[sl, j, tk * 128:tk * 128 + 128], key)], t_in[2], t_in[3],
                                   t_kc if br == 0 else None)
                        bias = cst[:, C_CB + tk * 120:C_CB + tk * 120 + 120].rearrange("p (h c) -> p h c", h=8) \
                            if br == 0 else alibi[:, :, 256 - nk:256]
                        h0 = 4 * g + j0
                        stt(s.ap[:, h0:h0 + per, 0:nk], b.ap[:, 0:per * nk].rearrange("p (h k) -> p h k", h=per), 0.125,
                            bias[:, h0:h0 + per, :], MUL, ADD, t, t_al, list(s.free))
                        b.free = [V.last()]
                s.ready = red(st[:, 0:8], s.ap[:, :, 0:nk], MAX, neg=True)

            def exps(i):
                tk, br = its[i]
                s, st = sbuf[i % 2], sts[i % 2]
                nk = 15 if br == 0 else 128 * (tk + 1)
                for h in range(8):
                    t = act(s.ap[:, h, 0:nk], s.ap[:, h, 0:nk], ACT.Exp, s.ready, bias=st[:, h:h + 1],
                            acc=st[:, 8 + h:9 + h])
                s.ready = t

            def turns(i):
                tk, br = its[i]
                s, p_ = sbuf[i % 2], pbuf[i % 2]
                n, nt = (15, 1) if br == 0 else (128, tk + 1)
                for kt in range(nt):
                    for h0 in (0, 4):
                        b = bank()
                        for h in range(h0, h0 + 4):
                            t = tr(b, b.ap[0:n, (h - h0) * 128:(h - h0) * 128 + 128],
                                   s.ap[:, h, kt * 128:kt * 128 + n], s.ready)
                        p_.ready = act(p_.ap[0:n, kt, h0:h0 + 4, :], b.ap[0:n, :].rearrange("p (h t) -> p h t", h=4),
                                       ACT.Copy, t, list(p_.free))
                        b.free = [p_.ready]
                s.free = [t]

            def values(i):
                tk, br = its[i]
                s, p_, st = sbuf[i % 2], pbuf[i % 2], sts[i % 2]
                recip(st[:, 16:24], st[:, 8:16], s.ready)
                tt(st[:, 24:32], st[:, 16:24], gates[:, tk, br:24:3], MUL, t_gates)
                if br == 0 and tk == 0:
                    ts(st[:, 24:32], st[:, 24:32], cst[:, C_VAL:C_VAL + 1], None, MUL, None)
                b = bank()
                vo = (br - 1) * 128
                for h in range(8):
                    g = h // 4
                    if br == 0:
                        pairs = [(p_.ap[0:15, 0, h, :], vc[0:15, 64 * g:64 * g + 64])]
                    else:
                        pairs = [(p_.ap[:, kt, h, :], vtok[:, kt, vo + 64 * g:vo + 64 * g + 64]) for kt in range(tk + 1)]
                    t = mm(b if h == 0 else None, b.ap[:, h * 64:h * 64 + 64], pairs, p_.ready, t_v,
                           t_vc if br == 0 else None)
                p_.free = [t]
                o3 = osum[:, tk, :].rearrange("p (h d) -> p h d", h=8)
                tt(o3 if br == 1 else tmp, b.ap[:, :].rearrange("p (h d) -> p h d", h=8), bc(st[:, 24:32], 2, 64), MUL, t)
                b.free = [V.last()]
                if br != 1:
                    tt(o3, o3, tmp, ADD)

            def project_out(k, yT, col, t_y):
                pc = load(d["w_out"][l, k], 4096)
                w = pc.ap.rearrange("p (c n) -> p c n", c=4)
                for tk in range(2):
                    for dh in range(2):
                        b = bank()
                        t = mm(b, b.ap[:, :], [(yT[:, c, tk * 128:tk * 128 + 128], w[:, c, dh * 512:dh * 512 + 512])
                                               for c in range(4)], pc.ready, t_y)
                        zz = z[:, tk, dh * 512:dh * 512 + 512]
                        stt(zz, b.ap[:, :], ss[:, col + tk:col + tk + 1], zz, MUL, ADD, t)
                        b.free = [V.last()]
                pc.free = [t]

            def pads():
                for n in range(2):
                    V.do(lambda e, n=n: e.memset(kzs[n], 0.0))
                    for hf in range(2):
                        win = kT[:, n, hf * 16:hf * 16 + 240].rearrange("p (c j) -> p j c", j=16)
                        for g in range(2):
                            s = slice(64 * g, 64 * g + 64)
                            tt(kzs[n][s, hf * 16:hf * 16 + 16, g, :], win[s, :, :],
                               bc(par((P_POSK, P_POSV)[n] + hf * 16, 16), 2, 15)[s, :, :], ADD, t_in[3])
                return V.last()

            scores(0)
            exps(0)
            t_kz = pads()
            ts(z, x3, ALPHA, None, MUL, None)
            for i in range(6):
                if i < 5:
                    scores(i + 1)
                turns(i)
                if i < 5:
                    exps(i + 1)
                mod_step()
                if i == 0:
                    t_kc = compress(0)
                if i == 1:
                    t_vc = compress(1)
                    lru_norm()
                values(i)
                if i == 5:
                    mod_step(False)
                if i == 3:
                    project_out(0, ylT, 2, t_yl)
            t_os = V.last()
            sqb = sbuf[0].ap[:, 0:2, :].rearrange("p a b -> p (a b)")
            for tk in range(2):
                act(sqb, osum[:, tk, :], ACT.Square, t_os, acc=ss[:, 4 + tk:5 + tk])
            t_o = V.last()
            act(ss[:, 6:8], ss[:, 4:6], ACT.Sqrt, scale=1.0 / 512, bias=cst[:, C_E5:C_E5 + 1])
            t_s8 = A.last()
            ynT = qT
            for tk in range(2):
                b = bank()
                for c in range(4):
                    t = tr(b, b.ap[:, c * 128:c * 128 + 128], osum[:, tk, c * 128:c * 128 + 128], t_o)
                for c in range(4):
                    ts(ynT[:, c, tk * 128:tk * 128 + 128], b.ap[:, c * 128:c * 128 + 128], par(P_GN + c), None,
                       MUL, None, t)
                b.free = [V.last()]
            t_yn = V.last()
            recip(ss[:, 8:10], ss[:, 6:8], t_s8)
            project_out(1, ynT, 8, t_yn)
            layer_norm(z, lnb[:, 0:1024], lnb[:, 1024:2048], lst, mv, x3, t_ln)

        def peer(l):
            fence()
            rot["set"] = list(range(6))
            eg = ar4(3, 2, 128).rearrange("p k t n -> p k (t n)")
            gs = ar4(3, 1, 256).rearrange("p k o n -> p k (o n)")
            gsb = ar(384).bitcast(BF16).rearrange("p (k n) -> p k n", k=3)
            gel = [Held(ar(256)) for _ in range(AHEAD + 1)]
            p32 = ar(256)
            pt = [Held((phi_t[:, i * 256:i * 256 + 256], plo_t[:, i * 256:i * 256 + 256])) for i in range(3)]
            vt = [Held((vhi_t[:, i * 1024:i * 1024 + 1024], vlo_t[:, i * 1024:i * 1024 + 1024])) for i in range(2)]
            Aoh = [Held(ar(1024).bitcast(BF16).rearrange("p (t a) -> p t a", t=16)) for _ in range(3)]
            Boh = [Held(ar(768).bitcast(BF16).rearrange("p (k t b) -> p k t b", k=3, t=16)) for _ in range(2)]
            eqb = ar(512).rearrange("p (t b) -> p t b", t=16)
            mark = top[0]
            assert mark + 16384 <= ARENA
            gel0 = [Held(arena[:, mark + 16384 - 256 * (EARLY - i):mark + 16384 - 256 * (EARLY - i - 1)]) for i in range(EARLY)]
            qT = [Held(ar3(4, 256)) for _ in range(2)]
            s_ = [Held(ar4(2, 4, 128)) for _ in range(4)]
            sk = pp[:, P_SK:P_SK + 256].rearrange("p (c k) -> p c k", c=2)
            work = [ar(256) for _ in range(2)]
            sv = ar(512).rearrange("p (t h c k) -> p t h c k", t=2, h=8, c=2)
            si = ar(512).bitcast(U32).rearrange("p (t h c k) -> p t h c k", t=2, h=8, c=2)
            sif = ar(512).rearrange("p (t h c k) -> p t h c k", t=2, h=8, c=2)
            cand = ar4(2, 16, 16)
            eq = [ar(512).rearrange("p (n k) -> p n k", k=16) for _ in range(2)]
            cv = ar4(2, 8, 16)
            ci = ar(256).bitcast(U32).rearrange("p (t h k) -> p t h k", t=2, h=8)
            cj = ar(64).bitcast(U32).rearrange("p (c n) -> p c n", c=2)
            cf = ar(64).rearrange("p (c n) -> p c n", c=2)
            ea = ar4(2, 3, 128)
            sm = ar(64).rearrange("p (t n) -> p t n", t=2)
            bG = [banks[4], banks[5]]
            bU = [banks[6], banks[7]]
            up = {}

            def queries(j):
                pc = load(d["peer_wq"][l, j], 4096)
                w = pc.ap.rearrange("p (c n) -> p c n", c=8)
                q_ = qT[j % 2]
                for hf in range(2):
                    b = bank()
                    for k in range(2):
                        ct = hf * 2 + k
                        t = mm(b if k == 0 else None, b.ap[:, k * 256:k * 256 + 256],
                               [(w[:, dc, ct * 128:ct * 128 + 128], xT[:, dc, :]) for dc in range(8)], pc.ready)
                    q_.ready = act(q_.ap[:, 2 * hf:2 * hf + 2, :], b.ap[:, :].rearrange("p (k t) -> p k t", k=2),
                                   ACT.Copy, t, list(q_.free))
                    b.free = [q_.ready]
                pc.free = [t]

            def scores(j):
                q_, s = qT[j % 2], s_[j]
                for tk in range(2):
                    b = bank()
                    for k in range(4):
                        t = mm(b if k == 0 else None, b.ap[:, k * 128:k * 128 + 128],
                               [(q_.ap[:, k, tk * 128:tk * 128 + 128], sk[:, k % 2, :])], q_.ready)
                    s.ready = act(s.ap[:, tk, :, :], b.ap[:, :].rearrange("p (k t) -> p k t", k=4), ACT.Copy, t,
                                  list(s.free))
                    b.free = [s.ready]
                q_.free = [t]

            def top16(jobs, *w):
                steps = [lambda e, s, v, i, k: e.max(v[:, 0:8], s),
                         lambda e, s, v, i, k: e.max_index(i[:, 0:8], v[:, 0:8], s),
                         lambda e, s, v, i, k: e.match_replace(k, v[:, 0:8], s, -3.0e38),
                         lambda e, s, v, i, k: e.max(v[:, 8:16], k),
                         lambda e, s, v, i, k: e.max_index(i[:, 8:16], v[:, 8:16], k)]
                for f in steps:
                    for job in jobs:
                        V.do(lambda e, f=f, job=job: f(e, *job), *w)
                        V.lag = 1
                V.lag = 0

            def choose(j):
                s = s_[j]
                hs = slice(2 * j, 2 * j + 2)
                for tk in range(2):
                    for h in range(2):
                        top16([(s.ap[:, tk, 2 * h + c, :], sv[:, tk, 2 * j + h, c, :], si[:, tk, 2 * j + h, c, :],
                                work[c][:, 0:128]) for c in range(2)], s.ready)
                    if tk:
                        s.free = [V.last()]
                    cp(sif[:, tk, hs, :, :], si[:, tk, hs, :, :])
                    tt(cand, bc(sv[:, tk, hs, 0, :], 3, 16), bc(sv[:, tk, hs, 1, :], 2, 16), ADD)
                    top16([(cand[:, h, :, :].rearrange("p a b -> p (a b)"), cv[:, tk, 2 * j + h, :],
                            ci[:, tk, 2 * j + h, :], work[h]) for h in range(2)])
                    i2 = ci[:, tk, hs, :].rearrange("p h k -> p (h k)")
                    ts(cj[:, 0, :], i2, 4, None, ALU.logical_shift_right, None)
                    ts(cj[:, 1, :], i2, 15, None, ALU.bitwise_and, None)
                    cp(cf, cj)
                    for c in range(2):
                        tt(eq[c], bc(cf[:, c, :], 2, 16), bc(cst[:, C_I16:C_I16 + 16], 1, 32), EQ)
                        V.lag = 1
                    for c in range(2):
                        e4 = eq[c].rearrange("p (h a) k -> p h a k", h=2)
                        tt(e4, e4, bc(sif[:, tk, hs, c, :], 2, 16), MUL)
                    for c in range(2):
                        red(ea[:, tk, c, 32 * j:32 * j + 32], eq[c], ADD)
                    V.lag = 0

            def gelu_of(c):
                return gel0[c] if c < EARLY else gel[(c - EARLY) % (AHEAD + 1)]

            def stage1(c):
                if c % 4 == 0:
                    up["u"] = load(d["peer_u"][l, c // 4], 4096)
                u = up["u"]
                w = u.ap.rearrange("p (i c a) -> p i c a", i=4, c=8)
                b = bU[c % 2]
                t = mm(b, b.ap[:, 0:256], [(w[:, c % 4, dc, :], xT[:, dc, :]) for dc in range(8)], u.ready)
                if c % 4 == 3:
                    u.free = [t]
                ge = gelu_of(c)
                ge.ready = act(ge.ap, b.ap[:, 0:256], ACT.Gelu_apprx_tanh, t, list(ge.free))
                b.free = [A.last()]

            for j in range(4):
                queries(j)
                scores(j)
                choose(j)
            t_s = A.last()
            t_pp_free = P.last()
            assert top[0] <= mark + 16384 - 256 * EARLY
            for c in range(EARLY):
                stage1(c)
            cp(sm[:, :, 0:8], cv[:, :, :, 0])
            tt(cv, cv, bc(sm[:, :, 0:8], 3, 16), SUB)
            g3 = ea[:, :, 2, :].rearrange("p t (h k) -> p t h k", h=8)
            act(g3, cv, ACT.Exp, V.last())
            red(sm[:, :, 8:16], g3, ADD, A.last())
            recip(sm[:, :, 16:24], sm[:, :, 8:16])
            tt(g3, g3, bc(sm[:, :, 16:24], 3, 16), MUL)
            t_ea = V.last()
            for tk in range(2):
                b = bG[tk]
                for c in range(3):
                    t = tr(b, b.ap[:, c * 128:c * 128 + 128], ea[:, tk, c, :], t_ea)
                cp(eg[:, :, tk * 128:tk * 128 + 128], b.ap[:, 0:384].rearrange("p (c t) -> p c t", c=3), t)
                b.free = [V.last()]
            cp(gsb[:, 0, :], eg[:, 2, :])
            cp(gs[:, 0, :], gsb[:, 0, :])
            tt(eg[:, 2, :], eg[:, 2, :], gs[:, 0, :], SUB)
            cp(gsb[:, 1, :], eg[:, 2, :])
            cp(gs[:, 1, :], gsb[:, 1, :])
            tt(gs[:, 2, :], eg[:, 2, :], gs[:, 1, :], SUB)
            t_g = V.last()
            v_topk = V.last()
            top[0] = mark
            Gq = [Held(ar3(32, 256)) for _ in range(2)]
            for g in Gq:
                g.free = [v_topk, t_s]
            acc = [banks[i] for i in range(4)]

            def prep_group(q, tg):
                n = q * 16 + tg
                ah, bh = Aoh[n % 3], Boh[n % 2]
                t0 = tg * 16
                if q == 0 and tg % 3 or q == 1 and tg % 3 == 0:
                    ah.ready = tt(ah.ap, bc(iota, 1, 16), bc(eg[:, 0, t0:t0 + 16], 2, 128), EQ, list(ah.free), t_g)
                else:
                    for i in range(16):
                        ah.ready = ts(ah.ap[:, i, :], iota, eg[:, 0, t0 + i:t0 + i + 1], None, EQ, None,
                                      list(ah.free), t_g, q=G)
                tt(eqb, bc(iota[:, q * 32:q * 32 + 32], 1, 16), bc(eg[:, 1, t0:t0 + 16], 2, 32), EQ)
                for k in range(3):
                    tt(bh.ap[:, k, :, :], eqb, bc(gs[:, k, t0:t0 + 16], 2, 32), MUL, list(bh.free))
                    V.lag = k + 1
                V.lag = 0
                bh.ready = V.last()

            def build_group(q, tg):
                n = q * 16 + tg
                ah, bh, g = Aoh[n % 3], Boh[n % 2], Gq[q % 2]
                t0 = tg * 16
                b = bG[n % 2]
                for i in range(16):
                    t = mm(b if i == 0 else None, b.ap[:, i * 32:i * 32 + 32],
                           [(ah.ap[:, i, :], bh.ap[:, k, i, :]) for k in range(3)], ah.ready, bh.ready)
                ah.free, bh.free = [t], [t]
                g.ready = act(g.ap[:, :, t0:t0 + 16].rearrange("p b t -> p t b"),
                              b.ap[:, :].rearrange("p (t b) -> p t b", t=16), ACT.Copy, t, list(g.free))
                b.free = [A.last()]

            for tg in range(16):
                prep_group(0, tg)
                if tg < AHEAD:
                    stage1(EARLY + tg)
                build_group(0, tg)

            def weigh(c):
                ge, p_, g = gelu_of(c), pt[c % 3], Gq[(c // 32) % 2]
                hi, lo = p_.ap
                tt(p32, ge.ap, g.ap[:, c % 32, :], MUL, ge.ready, g.ready)
                ge.free = [V.last()]
                if c % 32 == 31:
                    g.free = [V.last()]
                cp(hi, p32, list(p_.free))
                p_.ready = tt(lo, p32, hi.bitcast(F32), SUB)

            def split_v(c):
                v, t_ = up["v", c // 4], vt[c % 2]
                hi, lo = t_.ap
                w = v.ap.rearrange("p (i n) -> p i n", i=4)[:, c % 4, :]
                act(hi, w, ACT.Copy, v.ready, list(t_.free))
                t_.ready = tt(lo, w, hi.bitcast(F32), SUB, A.last())
                if c % 4 == 3:
                    v.free = [t_.ready]

            def stage2(c):
                p_, t_ = pt[c % 3], vt[c % 2]
                for tk in range(2):
                    for dh in range(2):
                        b = acc[2 * tk + dh]
                        for i, (x, y) in enumerate(((0, 0), (0, 1), (1, 0))):
                            t = P.do(lambda e, b=b, tk=tk, dh=dh, i=i, x=x, y=y: e.matmul(
                                b.ap[:, :], p_.ap[x][:, tk * 128:tk * 128 + 128], t_.ap[y][:, dh * 512:dh * 512 + 512],
                                start=(c == 0 and i == 0), stop=(c == 127 and i == 2)), p_.ready, t_.ready,
                                list(b.free) if c == 0 else None, inc=(tk == 1 and dh == 1 and i == 2))
                p_.free, t_.free = [t], [t]
                return t

            when = {}
            for q in range(1, 4):
                for tg in range(16):
                    c = EARLY + 1 + tg if q == 1 else 32 * (q - 1) + 2 * tg
                    when.setdefault(c, []).insert(0, lambda q=q, tg=tg: prep_group(q, tg))
                    when.setdefault(c + 1, []).append(lambda q=q, tg=tg: build_group(q, tg))

            for c in range(130):
                if EARLY <= c < 128 - AHEAD:
                    stage1(c + AHEAD)
                if c < 128:
                    if c % 4 == 0:
                        up["v", c // 4] = load(d["peer_v"][l, c // 4], 4096)
                    weigh(c)
                    if c == EARLY - 1:
                        Gq[1].free = [V.last()]
                    for step in when.get(c, ()):
                        step()
                if c >= 2:
                    t = stage2(c - 2)
                if c < 128:
                    split_v(c)
            z = Gq[0].ap.rearrange("p b t -> p (b t)")[:, 0:2048].rearrange("p (t n) -> p t n", t=2)
            lst = Gq[1].ap[:, 0, 0:24].rearrange("p (a b) -> p a b", a=4)
            mv = Gq[1].ap[:, 1, 0:8].rearrange("p (a b) -> p a b", a=2)
            ln = load(d["ln"][l, 1].partition_broadcast(128), 2048)
            for tk in range(2):
                for dh in range(2):
                    b = acc[2 * tk + dh]
                    stt(z[:, tk, dh * 512:dh * 512 + 512], x3[:, tk, dh * 512:dh * 512 + 512], ALPHA, b.ap[:, :],
                        MUL, ADD, t)
                    b.free = [V.last()]
            rot["set"] = [4, 5, 6, 7]
            rot["n"] = 0
            layer_norm(z, ln.ap[:, 0:1024], ln.ap[:, 1024:2048], lst, mv, x3, ln.ready)
            ln.free = [V.last()]
            rot["set"] = list(range(8))
            return t_pp_free

        def second():
            toks = fence()
            rot["set"] = list(range(8))
            t_qq = load_once(pp[:, 0:NQ_COLS], d["qq"], toks)
            for q in (P, V, A, G):
                q.fence = q.fence + [t_qq]
            keep = [0]

            def kp_(n):
                a = keep[0]
                keep[0] += n
                assert keep[0] <= 2048
                return xtok[:, a:a + n]

            def par(c, n=1):
                return pp[:, c:c + n]

            coef = kp_(40).rearrange("p (k c) -> p k c", k=5)
            lb = kp_(64).rearrange("p (k d h) -> p k d h", k=4, d=2)
            eps6 = cst[:, C_E6:C_E6 + 1]

            for k, (g, j, v) in enumerate(((Q_NMG, 8, 0), (Q_NMG, 8, 1), (Q_NFG, 32, 0))):
                stt(coef[:, k, :], mod[:, j:j + 8, v], 1.0, par(g, 8), ADD, MUL)
            l0, l1 = [pp[:, Q_LBL:Q_LBL + 32].rearrange("p (d e h) -> p d e h", d=2, e=2)[:, :, k, :] for k in (0, 1)]
            tt(lb[:, 0, :, :], l0, l1, MAX)
            tt(lb[:, 1, :, :], l0, lb[:, 0, :, :], SUB)
            tt(lb[:, 2, :, :], l1, lb[:, 0, :, :], SUB)
            act(lb[:, 1:3, :, :], lb[:, 1:3, :, :], ACT.Exp, V.last())
            tt(lb[:, 2, :, :], lb[:, 1, :, :], lb[:, 2, :, :], ADD, A.last())
            recip(lb[:, 3, :, :], lb[:, 2, :, :])
            tt(lb[:, 0, :, :], lb[:, 1, :, :], lb[:, 3, :, :], MUL)
            ts(lb[:, 1, :, :], lb[:, 0, :, :], -1.0, 1.0, MUL, ADD)

            def rms(src, n, cnt, dst, sq):
                tt(sq, src, src, MUL)
                return rms_from(sq, n, cnt, dst, V.last())

            def rms_from(sq, n, cnt, dst, t):
                b = bank()
                t = mm(b, b.ap[:, 0:n], [(ones, sq[:, i, :]) for i in range(sq.shape[1])], t)
                act(dst, b.ap[:, 0:n], ACT.Sqrt, t, scale=1.0 / cnt, bias=eps6)
                b.free = [A.last()]
                return recip(dst, dst, A.last())

            def modulated(dst, src, k, shift, v, rstd, sq):
                rms(src, 256, 1024, rstd, sq)
                tt(sq, src, bc(rstd, 1, 8), MUL)
                for c in range(8):
                    ts(dst[:, c, :], sq[:, c, :], coef[:, k, c:c + 1], mod[:, shift + c, v:v + 1], MUL, ADD)

            def mixer():
                ym = ar3(8, 256)
                hT = ar3(8, 512)
                mark_r = top[0]
                rstd = ar(512)
                mark0 = top[0]
                sq = [ar3(8, 256) for _ in range(2)]
                cT = ar3(8, 256)
                t_c = load_once(cT, d["ctxT"].rearrange("(c p) t -> p c t", p=128), toks)
                tt(sq[0], xT, xT, MUL)
                t_s0 = V.last()
                t_s1 = act(sq[1], cT, ACT.Square, t_c)
                rms_from(sq[0], 256, 1024, rstd[:, 0:256], t_s0)
                rms_from(sq[1], 256, 1024, rstd[:, 256:512], t_s1)
                t_r = V.last()
                tt(sq[1], cT, bc(rstd[:, 256:512], 1, 8), MUL, t_r, q=G)
                tt(sq[0], xT, bc(rstd[:, 0:256], 1, 8), MUL)
                for c in range(8):
                    ts(hT[:, c, 0:256], sq[0][:, c, :], coef[:, 0, c:c + 1], mod[:, c, 0:1], MUL, ADD)
                t_m = G.last()
                for c in range(8):
                    A.do(lambda e, c=c: e.activation(hT[:, c, 256:512], sq[1][:, c, :], ACT.Identity,
                                                     bias=mod[:, c, 1:2], scale=coef[:, 1, c:c + 1]), t_m, t_r)
                t_h = [V.last(), A.last()]
                top[0] = mark0

                def project(src, n_ct, n, evac, ndc=8, rhs=None, waits=None):
                    if waits is None:
                        waits = [V.last(), A.last()]
                    pc = load(src, ndc * n_ct * 128)
                    w = pc.ap.rearrange("p (c n) -> p c n", c=ndc)
                    r = rhs if rhs is not None else hT
                    for ct in range(n_ct):
                        b = bank()
                        t = mm(b, b.ap[:, 0:n], [(w[:, dc, ct * 128:ct * 128 + 128], r[:, dc, 0:n]) for dc in range(ndc)],
                               pc.ready, waits if ct == 0 else None)
                        b.free = [evac(ct, b.ap[:, 0:n], t)]
                    pc.free = [t]

                qn = ar3(8, 256)
                qr = ar3(8, 256)
                kn = ar3(8, 512)
                kr = ar(512)
                va = ar3(4, 1024)
                gsig = ar3(8, 256)
                mark1 = top[0]
                qin = ar3(6, 256)
                ckv = ar3(2, 512)
                sq6 = ar3(6, 256)
                sqk = va[:, 0, :].rearrange("p (c t) -> p c t", c=2)
                sw = kp_(512)
                for j in range(2):
                    project(d["w_q"][j], 3, 256, lambda ct, ps, t, j=j: act(qin[:, 3 * j + ct, :], ps, ACT.Copy, t),
                            waits=[t_h])

                def ev_kv(ct, ps, t):
                    return act(ckv[:, ct, :] if ct < 2 else kr, ps, ACT.Copy, t)

                project(d["w_kv"], 3, 512, ev_kv, waits=[t_h])
                t_qc = A.last()
                V.fence = V.fence + [t_qc]
                V.do(lambda e: e.memset(qr, 0.0))
                tt(sq6, qin, qin, MUL)
                t_q6 = V.last()
                tt(sqk, ckv, ckv, MUL)
                t_k2 = V.last()
                for j in range(2):
                    project(d["w_hg"][10 + j], 4, 256,
                            lambda ct, ps, t, j=j: act(gsig[:, 4 * j + ct, :], ps, ACT.Sigmoid, t), waits=[t_h])
                    if j == 0:
                        rq = ar(256)
                        rms_from(sq6, 256, 768, rq, t_q6)
                        rms_from(sqk, 512, 256, rstd, t_k2)
                        tt(qin, qin, bc(rq, 1, 6), MUL)
                        for c in range(6):
                            ts(qin[:, c, :], qin[:, c, :], par(Q_QNG + c), None, MUL, None)
                        t_qin = V.last()
                        tt(ckv, ckv, bc(rstd, 1, 2), MUL)
                        for c in range(2):
                            ts(ckv[:, c, :], ckv[:, c, :], par(Q_KVG + c), None, MUL, None)
                        t_ckv = V.last()

                perm = cst[:, C_PERM:C_PERM + 128]
                cos, sin = cst[:, C_COS:C_COS + 256], cst[:, C_SIN:C_SIN + 256]

                def rope(src, dsts, t):
                    b = bank()
                    t = mm(b, b.ap[:, 0:256], [(perm, src)], t)
                    tt(sw[:, 0:256], b.ap[:, 0:256], sin, MUL, t)
                    b.free = [V.last()]
                    tt(sw[:, 256:512], src, cos, MUL)
                    for s, o in dsts:
                        r = tt(o, sw[s, 0:256], sw[s, 256:512], ADD)
                    return r

                lo, hi, al = slice(0, 64), slice(64, 128), slice(0, 128)
                pc = load(d["w_kvb"], 4096)
                w = pc.ap.rearrange("p (v c n) -> p v c n", v=2, c=2)
                for h in range(8):
                    b = bank()
                    t = mm(b, b.ap[:, :], [(w[:, 0, c, h * 128:h * 128 + 128], ckv[:, c, :]) for c in range(2)],
                           pc.ready, t_ckv)
                    b.free = [act(kn[:, h, :], b.ap[:, :], ACT.Copy, t)]
                for k in range(4):
                    for hf in range(2):
                        b = bank()
                        t = mm(b, b.ap[:, :], [(ckv[:, c, k * 128:k * 128 + 128], w[:, 1, c, hf * 512:hf * 512 + 512])
                                               for c in range(2)])
                        b.free = [cp(va[:, k, hf * 512:hf * 512 + 512], b.ap[:, :], t)]
                pc.free = [t]
                rope(kr[:, 0:256], [(al, kr[:, 0:256])], t_qc)
                for j in range(2):
                    project(d["w_qb_n"][j], 4, 256, lambda ct, ps, t, j=j: act(qn[:, 4 * j + ct, :], ps, ACT.Copy, t),
                            ndc=6, rhs=qin, waits=[t_qin])
                qrs = sq6

                project(d["w_qb_r"], 4, 256, lambda ct, ps, t: act(qrs[:, ct, :], ps, ACT.Copy, t), ndc=6, rhs=qin,
                        waits=[t_qin])
                for j in range(4):
                    rope(qrs[:, j, :], [(lo, qr[lo, 2 * j, :]), (hi, qr[hi, 2 * j + 1, :])], A.last())
                t_kv = [A.last(), V.last()]
                top[0] = mark1
                for q in (P, V, A):
                    q.fence = q.fence + [P.last()] + t_kv
                pb = [Held(ar(512)) for _ in range(3)]
                pT = [Held(ar3(4, 256)) for _ in range(2)]
                st = ar(128)
                SC = 192.0 ** -0.5
                def qk(n):
                    h, tk = n // 2, n % 2
                    ts_ = slice(tk * 128, tk * 128 + 128)
                    b = bank()
                    t = mm(b, b.ap[:, :], [(qn[:, h, ts_], kn[:, h, :]), (qr[:, h, ts_], kr)], t_kv)
                    p_ = pb[n % 3]
                    c = 4 * n
                    red(st[:, c:c + 1], b.ap[:, :], MAX, t, neg=True)
                    ts(st[:, c + 1:c + 2], st[:, c:c + 1], SC, None, MUL, None)
                    p_.ready = act(p_.ap, b.ap[:, :], ACT.Exp, V.last(), list(p_.free), bias=st[:, c + 1:c + 2], scale=SC,
                                   acc=st[:, c + 2:c + 3])
                    b.free = [p_.ready]

                def norm(n):
                    p_ = pb[n % 3]
                    c = 4 * n
                    recip(st[:, c + 3:c + 4], st[:, c + 2:c + 3], p_.ready)
                    p_.ready = ts(p_.ap, p_.ap, st[:, c + 3:c + 4], None, MUL, None)

                def turn_p(n):
                    h, tk = n // 2, n % 2
                    ts_ = slice(tk * 128, tk * 128 + 128)
                    p_, pt_ = pb[n % 3], pT[h % 2]
                    b = bank()
                    for k in range(4):
                        t = tr(b, b.ap[:, k * 128:k * 128 + 128], p_.ap[:, k * 128:k * 128 + 128], p_.ready)
                    p_.free = [t]
                    pt_.ready = cp(pt_.ap[:, :, ts_], b.ap[:, :].rearrange("p (k t) -> p k t", k=4), t, list(pt_.free))
                    b.free = [pt_.ready]

                def av(h):
                    pt_ = pT[h % 2]
                    b = bank()
                    t = mm(b, b.ap[:, 0:256], [(va[:, k, h * 128:h * 128 + 128], pt_.ap[:, k, :]) for k in range(4)],
                           pt_.ready)
                    pt_.free = [t]
                    b.free = [tt(ym[:, h, :], b.ap[:, 0:256], gsig[:, h, :], MUL, t)]

                qk(0)
                qk(1)
                for n in range(16):
                    norm(n)
                    if n < 14:
                        qk(n + 2)
                    if n % 2 == 0 and n:
                        av(n // 2 - 1)
                    turn_p(n)
                av(7)
                all_q = [q.last() for q in (P, V, A, G)]
                for q in (V, A, G):
                    q.fence = q.fence + all_q
                top[0] = mark_r
                hm = ar4(2, 8, 128)
                qh = ar3(4, 256)
                vh = ar3(4, 512)
                fb = [Held(ar4(2, 4, 256)) for _ in range(2)]
                cum = ar4(2, 4, 256)
                kd = ar4(3, 4, 128)
                kdT = ar4(3, 4, 128)
                S2 = sw.rearrange("p (c v) -> p c v", c=4)
                S3 = pp[:, NQ_COLS + 1024:NQ_COLS + 1536].rearrange("p (c v) -> p c v", c=4)
                att = ar3(8, 128)
                Eb = [Held(ar(1024)) for _ in range(2)]
                qc = ar3(4, 256)
                ob = ar3(4, 256)
                gA = pp[:, NQ_COLS:NQ_COLS + 1024].rearrange("p (c t) -> p c t", c=4)
                gB = kp_(1024).rearrange("p (c t) -> p c t", c=4)
                sm = ar(32)
                nE = [0]
                units = [(0, 0), (0, 1), (1, 0), (1, 1)]

                def tasks(src, put, n=256, rows=False):
                    st_ = {}

                    def step(ct):
                        if ct == 0:
                            st_["pc"] = load(src, 4096)
                        pc = st_["pc"]
                        w = pc.ap.rearrange("p (c n) -> p c n", c=8)
                        cs = slice(ct * 128, ct * 128 + 128)
                        b = bank()
                        if rows:
                            t = mm(b, b.ap[:, :], [(hT[:, dc, cs], w[:, dc, :]) for dc in range(8)], pc.ready)
                        else:
                            t = mm(b, b.ap[:, 0:n], [(w[:, dc, cs], hT[:, dc, 0:n]) for dc in range(8)], pc.ready)
                        if ct == 3:
                            pc.free = [t]
                        b.free = [put(ct, b.ap[:, 0:n] if not rows else b.ap[:, :], t)]

                    return [lambda ct=ct: step(ct) for ct in range(4)]

                def f_tasks(u):
                    hh, r = units[u]
                    f = fb[u % 2]

                    def put(ct, ps, t):
                        f.ready = act(f.ap[:, :, ct, :], ps.rearrange("p (s t) -> p s t", s=2), ACT.Copy, t, list(f.free))
                        return f.ready

                    return tasks(d["w_hg"][2 + 2 * r + hh], put, 512)

                def q_tasks(hh):
                    return tasks(d["w_hg"][hh], lambda ct, ps, t: act(qh[:, ct, :], ps, ACT.Copy, t, list(q_free)))

                def v_tasks(hh):
                    return tasks(d["w_hg"][6 + hh], lambda k, ps, t: act(vh[:, k, :], ps, ACT.Copy, t), rows=True)

                def gate_tasks(hh):
                    return [x for i, g in ((8, gA), (12, gB)) for x in
                            tasks(d["w_hg"][i + hh], lambda ct, ps, t, g=g: act(g[:, ct, :], ps, ACT.Copy, t, list(g_free)))]

                q_free, g_free = [], []
                todo = []

                def fill(n):
                    for _ in range(min(n, len(todo))):
                        todo.pop(0)()

                for step in f_tasks(0):
                    step()
                t_hm = load_once(hm, d["hmask"].rearrange("r p (l t) -> p r l t", l=8), all_q)
                t_out = None
                for u, (hh, r) in enumerate(units):
                    fk, gg = fb[u % 2].ap, fb[(u + 1) % 2].ap
                    for q in (V, A, G):
                        q.fence = q.fence + [t_out, V.last(), A.last(), G.last()]
                    act(fk, fk, ACT.Sigmoid, fb[u % 2].ready)
                    t_sg = A.last()
                    for c in range(4):
                        h = 4 * hh + c
                        ts(fk[:, :, c, :], fk[:, :, c, :], lb[:, 1, r, h:h + 1], lb[:, 0, r, h:h + 1], MUL, ADD, t_sg)
                    act(gg, fk, ACT.Ln, V.last())
                    ts(fk, fk, -1.0, 1.0, MUL, ADD, A.last())
                    msk = cst[:, (C_MF, C_MB)[r]:(C_MF, C_MB)[r] + 256]
                    for s in range(2):
                        for c in range(4):
                            o, m, g = cum[:, s, c, :], msk, gg[:, s, c, :]
                            if r:
                                o, m, g = o[:, ::-1], m[:, ::-1], g[:, ::-1]
                            V.do(lambda e, o=o, m=m, g=g: e.tensor_tensor_scan(o, m, g, 0.0, MUL, ADD))
                    fb[(u + 1) % 2].free = [V.last()]
                    G.do(lambda e: e.memset(att, 0.0))
                    t_att = G.last()
                    fst, last = (0, 127) if r == 0 else (1, 0)
                    ta = [(1, fst), (1, 1 - fst), (0, fst)]
                    for i, (s, k) in enumerate(ta):
                        cp(sm[:, 4 * i:4 * i + 4], cum[:, s, :, 128 * k + last])
                    t_sm = V.last()
                    tt(sm[:, 0:4], sm[:, 0:4], sm[:, 4:8], ADD)
                    for i, (s, k) in enumerate(ta):
                        tt(kd[:, i, :, :], bc(sm[:, 4 * i:4 * i + 4], 2, 128), cum[:, s, :, 128 * k:128 * k + 128], SUB)
                    t_kd = V.last()
                    act(qc, cum[:, 0, :, :], ACT.Exp, t_sm)
                    act(sm[:, 16:20], sm[:, 8:12], ACT.Exp)
                    act(kd, kd, ACT.Exp, t_kd)
                    t_e = A.last()
                    if u == 0:
                        todo += q_tasks(0) + v_tasks(0)
                    fill(len(todo))
                    if r == 0:
                        act(qh, qh, ACT.Silu)
                        ts(qh, qh, 128.0 ** -0.5, None, MUL, None, A.last())
                    for i, (s, k) in enumerate(ta):
                        tt(kd[:, i, :, :], kd[:, i, :, :], fk[:, s, :, 128 * k:128 * k + 128], MUL, t_e)
                    t_k = V.last()
                    tt(qc, qc, qh, MUL)
                    t_qc = V.last()
                    if r == 0:
                        todo += f_tasks(u + 1) + gate_tasks(hh)
                    elif hh == 0:
                        todo += f_tasks(u + 1)
                    C = cum[:, 0, :, :].rearrange("p h t -> p (h t)")
                    K = fk[:, 0, :, :].rearrange("p h t -> p (h t)")
                    Q = qh.rearrange("p h t -> p (h t)")

                    def decays(lv):
                        w_ = LEVELS[lv]
                        eb = Eb[lv % 2]
                        e3, c3 = [x.rearrange("p (n t) -> p n t", t=2 * w_) for x in (eb.ap, C)]
                        f, s = slice(0, w_), slice(w_, 2 * w_)
                        i = w_ - 1 if r == 0 else w_
                        ref = c3[:, :, i:i + 1].broadcast_to([128, 512 // w_, w_])
                        x, y = (f, s) if r == 0 else (s, f)
                        tt(e3[:, :, x], ref, c3[:, :, x], SUB, list(eb.free), t_sm, q=G)
                        tt(e3[:, :, y], c3[:, :, y], ref, SUB, q=G)
                        eb.ready = act(eb.ap, eb.ap, ACT.Exp, G.last())

                    def weigh(lv):
                        w_ = LEVELS[lv]
                        eb = Eb[lv % 2]
                        e3, k3, q3 = [x.rearrange("p (n t) -> p n t", t=2 * w_) for x in (eb.ap, K, Q)]
                        f, s = slice(0, w_), slice(w_, 2 * w_)
                        x, y = (f, s) if r == 0 else (s, f)
                        tt(e3[:, :, x], e3[:, :, x], k3[:, :, x], MUL, eb.ready)
                        eb.ready = tt(e3[:, :, y], e3[:, :, y], q3[:, :, y], MUL)

                    def pairs(lv):
                        ls, rs, t_r = (K, Q, t_qc) if lv == 7 else (Eb[lv % 2].ap, Eb[lv % 2].ap, Eb[lv % 2].ready)
                        bs = []
                        for u0 in (0, 4):
                            b = bank()
                            for i in range(u0, u0 + 4):
                                us = slice(i * 128, i * 128 + 128)
                                t = mm(b if i == u0 else None, b.ap[:, (i - u0) * 128:(i - u0) * 128 + 128],
                                       [(ls[:, us], rs[:, us])], t_r)
                            bs.append((b, t))
                        if lv < 7:
                            Eb[lv % 2].free = [t]
                        return bs

                    def keep_pairs(lv, bs):
                        for u0, (b, t) in zip((0, 4), bs):
                            V.do(lambda e, u0=u0, b=b, r=r: e.copy_predicated(
                                att[:, u0:u0 + 4, :], bc(hm[:, r, lv, :].bitcast(U32), 1, 4),
                                b.ap[:, :].rearrange("p (u t) -> p u t", u=4)), t, t_hm, t_att)
                            b.free = [V.last()]

                    for eb in Eb:
                        eb.free = []
                    decays(0)
                    decays(1)
                    for i in range(3):
                        b = bank()
                        for c in range(4):
                            t = tr(b, b.ap[:, c * 128:c * 128 + 128], kd[:, i, c, :], t_k)
                        b.free = [act(kdT[:, i, :, :], b.ap[:, :].rearrange("p (c k) -> p c k", c=4), ACT.Copy, t)]
                    t_kt = A.last()
                    bs = pairs(7)
                    weigh(0)
                    keep_pairs(7, bs)
                    b2, b3 = bank(), bank()
                    for c in range(4):
                        cs = slice(c * 128, c * 128 + 128)
                        t2 = mm(b2 if c == 0 else None, b2.ap[:, cs],
                                [(kdT[:, i, c, :], vh[:, 2 + ta[i][1], cs]) for i in range(2)], t_kt)
                        t3 = mm(b3 if c == 0 else None, b3.ap[:, cs], [(kdT[:, 2, c, :], vh[:, fst, cs])])
                    cp(S2, b2.ap[:, :].rearrange("p (c v) -> p c v", c=4), t2)
                    b2.free = [V.last()]
                    for c in range(4):
                        stt(S3[:, c, :], S2[:, c, :], sm[:, 16 + c:17 + c], b3.ap[:, c * 128:c * 128 + 128], MUL, ADD, t3)
                    b3.free = [V.last()]
                    for lv in range(7):
                        bs = pairs(lv)
                        if lv % 2 == 0:
                            fill(1)
                        if lv < 6:
                            weigh(lv + 1)
                        keep_pairs(lv, bs)
                        if lv < 5:
                            decays(lv + 2)
                    if r:
                        q_free[:] = [V.last()]
                    t_a = V.last()
                    if (hh, r) == (0, 1):
                        todo += v_tasks(1) + q_tasks(1)
                    for c0 in (0, 2):
                        b = bank()
                        for c in (c0, c0 + 1):
                            for k in range(2):
                                o = (c - c0) * 256 + k * 128
                                t = mm(b if (c, k) == (c0, 0) else None, b.ap[:, o:o + 128],
                                       [(vh[:, k, c * 128:c * 128 + 128], att[:, 2 * c + k, :]),
                                        ((S2 if k == fst else S3)[:, c, :], qc[:, c, k * 128:k * 128 + 128])], t_a)
                        o3 = ob[:, c0:c0 + 2, :]
                        ps = b.ap[:, :].rearrange("p (c t) -> p c t", c=2)
                        b.free = [cp(o3, ps, t) if r == 0 else tt(o3, o3, ps, ADD, t)]
                    t_out = t
                    if r == 0:
                        continue
                    o2 = Eb[0].ap.rearrange("p (c t) -> p c t", c=4)
                    rs_ = Eb[1].ap.rearrange("p (c t) -> p c t", c=4)
                    tt(o2, ob, ob, MUL)
                    t_o2 = V.last()
                    act(gA, gA, ACT.Silu)
                    t_ga = A.last()
                    act(gB, gB, ACT.Sigmoid)
                    t_gb = A.last()
                    fill(1)
                    for c0 in (0, 2):
                        b = bank()
                        t = mm(b, b.ap[:, :], [(ones, o2[:, c0:c0 + 2, :])], t_o2)
                        act(rs_[:, c0:c0 + 2, :], b.ap[:, :].rearrange("p (c t) -> p c t", c=2), ACT.Sqrt, t,
                            scale=1.0 / 128, bias=eps6)
                        b.free = [A.last()]
                    recip(rs_, rs_, A.last())
                    tt(ob, ob, rs_, MUL)
                    stt(ob, ob, par(Q_HGN), gA, MUL, MUL, t_ga)
                    tt(ob, ob, gB, MUL, t_gb)
                    tt(ym[:, 4 * hh:4 * hh + 4, :], ym[:, 4 * hh:4 * hh + 4, :], ob, ADD)
                    g_free[:] = [V.last()]
                t_y = V.last()
                for j in range(2):
                    def ev_o(ct, ps, t, j=j):
                        c = 4 * j + ct
                        return stt(xT[:, c, :], ps, mod[:, 16 + c, 0:1], xT[:, c, :], MUL, ADD, t)

                    project(d["w_o2"][j], 4, 256, ev_o, rhs=ym, waits=[t_y])
            mixer()
            fence()
            NB = 32 + EXTRA
            bd = ar(1024)
            bgu = ar(2048)
            gTt = ar(256)
            h2k = ar3(2, 1024)
            gd = ar3(2, 48)
            sl = ar3(2, 48)
            mk = ar3(2, 32)
            tri = ar(128)
            pidx = ar(8)
            selT = ar(48)
            xi = ar(16).bitcast(I32)
            tv = ar(32)
            ti = ar(16).bitcast(U32)
            tf = ar(32)
            ne = ar4(4, 1, 32).rearrange("p a o n -> p a (o n)")
            ex = ar(64)
            oh = ar3(EXTRA, 32)
            oh2 = ar3(EXTRA, 32)
            mark = top[0]
            h2 = ar3(8, 256)
            rstd = ar(256)
            sq = ar3(8, 256)
            lg = ar3(2, 32)
            V.do(lambda e: e.memset(bd, 0.0))
            V.do(lambda e: e.memset(gTt, 0.0))
            early = [load(d["w_gu"][0, i], 4096) for i in range(NSLOT)]
            t_bd = load_once(bd[0:32, :], d["b_dn"], [V.last()])
            t_bgu = load_once(bgu[0:32, :], d["b_gu"], [V.last()])
            tt(tri, ident, iota, MUL)
            red(pidx[:, 0:1], tri, ADD)
            ts(tri, iota, pidx[:, 0:1], None, ALU.is_gt, None)
            cp(selT[:, 0:32], ident[:, 0:32])
            modulated(h2, xT, 2, 24, 0, rstd, sq)
            t_h2 = V.last()
            wr = par(Q_WR, 256).rearrange("p (c n) -> p c n", c=8)
            bl = [bank() for _ in range(2)]
            for tk in range(2):
                t = mm(bl[tk], bl[tk].ap[:, 0:32], [(h2[:, dc, tk * 128:tk * 128 + 128], wr[:, dc, :]) for dc in range(8)],
                       t_h2)
                tt(lg[:, tk, :], bl[tk].ap[:, 0:32], par(Q_BR, 32), ADD, t)
                bl[tk].free = [V.last()]

            def ev_h(a_, k, ps, t):
                tk, c0 = a_ // 8, a_ % 8
                return act(h2k[:, tk, c0 * 128:(c0 + k) * 128].rearrange("p (k t) -> p k t", k=k), ps, ACT.Copy, t)

            transposes(None, lambda i: h2[:, i % 8, (i // 8) * 128:(i // 8) * 128 + 128], 16, t_h2, evac=ev_h)
            t_h2k = A.last()
            for tk in range(2):
                V.do(lambda e, tk=tk: e.max(tv[:, 0:8], lg[:, tk, :]))
                V.do(lambda e, tk=tk: e.max_index(ti[:, 0:8], tv[:, 0:8], lg[:, tk, :]))
                cp(tf[:, 0:8], ti[:, 0:8])
                ts(tv[:, 8:9], tv[:, 0:1], -1.0, None, MUL, None)
                act(tv[:, 16:20], tv[:, 0:4], ACT.Exp, V.last(), bias=tv[:, 8:9], acc=tv[:, 20:21])
                recip(tv[:, 21:22], tv[:, 20:21], A.last())
                ts(tv[:, 16:20], tv[:, 16:20], tv[:, 21:22], None, MUL, None)
                for k in range(4):
                    o = mk[:, tk, :] if k == 0 else lg[:, tk, :]
                    ts(o, iota[:, 0:32], tf[:, k:k + 1], None, EQ, None)
                    if k == 0:
                        ts(gd[:, tk, 0:32], o, tv[:, 16:17], None, MUL, None)
                    else:
                        tt(mk[:, tk, :], mk[:, tk, :], o, ADD)
                        stt(gd[:, tk, 0:32], o, tv[:, 16 + k:17 + k], gd[:, tk, 0:32], MUL, ADD)
            t_mk = V.last()
            b = bank()
            t = tr(b, b.ap[0:32, 0:128], gd[:, 0, 0:32], t_mk)
            t = tr(b, b.ap[0:32, 128:256], gd[:, 1, 0:32])
            cp(gTt[0:32, :], b.ap[0:32, 0:256], t)
            b.free = [V.last()]
            t_g = V.last()
            b = bank()
            t = mm(b, b.ap[:, 0:32], [(tri, mk[:, 0, :])], t_mk)
            t = mm(None, b.ap[:, 32:64], [(ones, mk[:, 0, :]), (tri, mk[:, 1, :])])
            t = mm(None, b.ap[:, 64:96], [(ones, mk[:, 0, :]), (ones, mk[:, 1, :])])
            stt(sl[:, :, 0:32], b.ap[:, 0:64].rearrange("p (t n) -> p t n", t=2), 1.0, mk, ADD, MUL, t)
            ts(sl[:, :, 0:32], sl[:, :, 0:32], -1.0, None, ADD, None)
            cp(ne[:, 0, :], b.ap[:, 64:96])
            b.free = [V.last()]
            t_sl = V.last()
            top[0] = mark
            for q in (P, V, A, G):
                q.fence = q.fence + [V.last(), A.last(), P.last()]

            def further_blocks():
                cnt, nx, end, beg = [ne[:, i, :] for i in range(4)]
                kk = iota[:, 0:EXTRA]
                ek, st, off = ex[:, 0:EXTRA], ex[:, 16:16 + EXTRA], ex[:, 32:32 + EXTRA]
                ts(nx, cnt, SLOTS + 0.5, None, ALU.is_gt, None)
                for k in range(2, 256 // SLOTS):
                    stt(nx, cnt, k * SLOTS + 0.5, nx, ALU.is_gt, ADD)
                V.do(lambda e: e.tensor_tensor_scan(end, ones[:, 0:32], nx, 0.0, MUL, ADD))
                tt(beg, end, nx, SUB)
                tt(oh, bc(kk, 2, 32), bc(end, 1, EXTRA), ALU.is_ge)
                red(ek, oh, ADD)
                tt(oh, bc(ek, 2, 32), bc(iota[:, 0:32], 1, EXTRA), EQ)
                tt(oh2, oh, bc(beg, 1, EXTRA), MUL)
                red(st, oh2, ADD)
                tt(off, kk, st, SUB)
                ts(off, off, 1.0, float(SLOTS), ADD, MUL)
                for tk in range(2):
                    tt(oh2, oh, bc(sl[:, tk, 0:32], 1, EXTRA), MUL)
                    red(st, oh2, ADD)
                    tt(sl[:, tk, 32:NB], st, off, SUB)
                    tt(oh2, oh, bc(gd[:, tk, 0:32], 1, EXTRA), MUL)
                    red(gd[:, tk, 32:NB], oh2, ADD)
                ts(selT[:, 32:NB], ek, pidx[:, 0:1], None, EQ, None)
                cp(xi[:, 0:1], end[:, 31:32])
                ts(ek, ek, 31.0, None, MIN, None)
                return cp(xi[:, 1:1 + EXTRA], ek)

            acc = banks[0:4]
            rot["set"] = [4, 5, 6, 7]
            sel = [Held(ar3(2, 256)) for _ in range(2)]
            xe = [Held(ar3(8, 256)) for _ in range(2)]
            gs_ = [Held(ar3(2, 128)) for _ in range(2)]
            gsT = [Held(ar(256)) for _ in range(3)]
            gx = [Held(ar(512)) for _ in range(2)]
            ly = [Held(ar(512)) for _ in range(2)]
            sg = [Held(ar(512)) for _ in range(2)]
            aT = [Held(ar3(4, 128)) for _ in range(2)]
            ye = [Held(ar(512)) for _ in range(2)]

            more_slots((ARENA - top[0]) // PIECE)

            def pick(j0, n, i, t_s):
                s_ = sel[i]
                w_ = n * SLOTS
                tt(s_.ap[:, :, 0:w_].rearrange("p t (n s) -> p t n s", n=n), bc(sl[:, :, j0:j0 + n], 3, SLOTS),
                   bc(bc(iota[:, 0:SLOTS], 1, n), 1, 2), EQ, list(s_.free), t_s)
                s_.ready = V.last()

            def gather(n, i):
                s_, x = sel[i], xe[i]
                w_ = n * SLOTS
                for dc in range(0, 8, 2):
                    b = bank()
                    for k in range(2):
                        t = mm(b if k == 0 else None, b.ap[:, k * 256:k * 256 + w_],
                               [(h2k[:, tk, (dc + k) * 128:(dc + k) * 128 + 128], s_.ap[:, tk, 0:w_]) for tk in range(2)],
                               s_.ready, t_h2k)
                    x.ready = act(x.ap[:, dc:dc + 2, 0:w_],
                                  b.ap[:, :].rearrange("p (k n) -> p k n", k=2)[:, :, 0:w_], ACT.Copy, t, list(x.free))
                    b.free = [A.last()]
                s_.free = [t]

            def up(j, i, k, src):
                x = xe[i]
                bb = []
                for v in range(2):
                    b = bank()
                    bb.append(b)
                    for g in range(2):
                        P.do(lambda e, b=b, v=v, g=g: e.matmul(
                            b.ap[64 * g:64 * g + 64, :], selT[0:32, j:j + 1].broadcast_to([32, 64]),
                            bgu[0:32, (2 * v + g) * 512:(2 * v + g) * 512 + 512], start=True, stop=False),
                            t_bgu, x.ready, list(b.free), inc=False)
                    for h in range(2):
                        pc = early.pop(0) if early else load(src("w_gu", 2 * v + h), 4096)
                        w = pc.ap.rearrange("p (c g n) -> p c g n", c=4, g=2)
                        for c in range(4):
                            for g in range(2):
                                end = c == 3 and g == 1
                                t = P.do(lambda e, b=b, w=w, c=c, g=g, h=h: e.matmul(
                                    b.ap[64 * g:64 * g + 64, :], x.ap[:, 4 * h + c, k * 64:k * 64 + 64], w[:, c, g, :],
                                    start=False, stop=(h == 1 and c == 3)), pc.ready, inc=end)
                        pc.free = [t]
                    bb[v].ready = t
                x.free = [t]
                gx_, y, z = gx[j % 2], ly[j % 2], sg[j % 2]
                ts(gx_.ap, bb[0].ap[:, :], 7.0, None, MIN, None, bb[0].ready)
                t_x = V.last()
                bb[0].free = [t_x]
                act(z.ap, gx_.ap, ACT.Sigmoid, t_x, list(z.free), scale=1.702)
                ts(y.ap, bb[1].ap[:, :], 7.0, -7.0, MIN, MAX, bb[1].ready, list(y.free))
                bb[1].free = [V.last()]
                stt(y.ap, y.ap, 1.0, gx_.ap, ADD, MUL)
                y.ready = tt(y.ap, y.ap, z.ap, MUL, A.last())
                z.free = [V.last()]
                g_ = gs_[j % 2]
                for tk in range(2):
                    g_.ready = ts(g_.ap[:, tk, :].rearrange("p (u s) -> p u s", u=2), bc(iota[:, 0:SLOTS], 1, 2),
                                  sl[:, tk, j:j + 1], gd[:, tk, j:j + 1], EQ, MUL, list(g_.free), t_sl, q=G)

            def turn(j):
                y, a, g_, gt = ly[j % 2], aT[j % 2], gs_[j % 2], gsT[j % 3]
                b = bank()
                for k in range(4):
                    t = tr(b, b.ap[:, k * 128:k * 128 + 128], y.ap[:, k * 128:k * 128 + 128], y.ready)
                y.free = [t]
                a.ready = act(a.ap, b.ap[:, :].rearrange("p (k t) -> p k t", k=4), ACT.Copy, t, list(a.free))
                b.free = [A.last()]
                b = bank()
                for tk in range(2):
                    t = tr(b, b.ap[:, tk * 128:tk * 128 + 128], g_.ap[:, tk, :], g_.ready)
                g_.free = [t]
                gt.ready = cp(gt.ap, b.ap[:, 0:256], t, list(gt.free))
                b.free = [V.last()]

            def down(j, src):
                a, y = aT[j % 2], ye[j % 2]
                b = bank()
                for hf in range(2):
                    pc = load(src("w_dn", hf), 4096)
                    w = pc.ap.rearrange("p (f n) -> p f n", f=4)
                    for f in range(4):
                        for g in range(2):
                            t = P.do(lambda e, b=b, w=w, f=f, g=g, hf=hf: e.matmul(
                                b.ap[64 * g:64 * g + 64, :], a.ap[:, f, 64 * hf:64 * hf + 64], w[:, f, g * 512:g * 512 + 512],
                                start=(hf == 0 and f == 0), stop=(hf == 1 and f == 3)),
                                pc.ready, a.ready, list(b.free), inc=(f == 3 and g == 1))
                    pc.free = [t]
                a.free = [t]
                y.ready = cp(y.ap, b.ap[:, :], t, list(y.free))
                b.free = [V.last()]

            def scatter(j):
                y, gt = ye[j % 2], gsT[j % 3]
                for tk in range(2):
                    for g in range(2):
                        t = P.do(lambda e, tk=tk, g=g: e.matmul(
                            acc[2 * tk + g].ap[:, :], gt.ap[64 * g:64 * g + 64, tk * 128:tk * 128 + 128],
                            y.ap[64 * g:64 * g + 64, :], start=(j == 0), stop=False), y.ready, gt.ready,
                            list(acc[2 * tk + g].free) if j == 0 else None, inc=(tk == 1 and g == 1))
                y.free, gt.free = [t], [t]
                return t

            pick(0, 4, 0, t_sl)
            gather(4, 0)
            for j in range(34):
                if j < 32:
                    up(j, j // 4 % 2, j % 4, lambda n, i, j=j: d[n][j, i])
                    if j % 4 == 1 and j < 29:
                        pick(j + 3, 4, (j // 4 + 1) % 2, t_sl)
                    if j % 4 == 2 and j < 30:
                        gather(4, (j // 4 + 1) % 2)
                if j == 1:
                    t_xi = further_blocks()
                if 1 <= j <= 32:
                    turn(j - 1)
                if j >= 2:
                    t = scatter(j - 2)
                if 1 <= j <= 32:
                    down(j - 1, lambda n, i, j=j: d[n][j - 1, i])
            fence()
            marks = (P, V, A, G)
            sems = [(q.sem, q.n) for q in marks]
            S.append(([t_xi], "begin", xi))
            for q in marks:
                q.ops.append((q.fence + [t_xi], "begin", xi))
                q.fence = []
                q.sem, q.n = sem(f"s_more{len(q.ops)}"), 0
            for k in range(EXTRA):
                S.append(([], "if", (k, xi)))
                for q in marks:
                    q.ops.append(([], "if", (k, None)))
                j = 32 + k
                pick(j, 1, k % 2, None)
                gather(1, k % 2)
                up(j, k % 2, 0, lambda n, i: lambda e: d[n][e, i])
                turn(j)
                down(j, lambda n, i: lambda e: d[n][e, i])
                scatter(j)
                done = [q.last() for q in marks]
                for q in marks:
                    q.ops.append((done, None, None))
            S.append(([], "end", None))
            for q, (s_, n) in zip(marks, sems):
                q.ops.append(([], "end", None))
                q.sem, q.n = s_, n
            for b in banks:
                b.free = []
            for tk in range(2):
                for dh in range(2):
                    t = P.do(lambda e, tk=tk, dh=dh: e.matmul(
                        acc[2 * tk + dh].ap[:, :], gTt[:, tk * 128:tk * 128 + 128], bd[:, dh * 512:dh * 512 + 512],
                        start=False, stop=True), t_bd)
            top[0] = mark
            rot["n"] = 0
            m = ar3(2, 1024)
            for tk in range(2):
                for dh in range(2):
                    cp(m[:, tk, dh * 512:dh * 512 + 512], acc[2 * tk + dh].ap[:, :], t)
            t_m = V.last()

            def ev_m(a_, k, ps, t):
                tk, c0 = a_ // 8, a_ % 8
                for i in range(k):
                    o = xT[:, c0 + i, tk * 128:tk * 128 + 128]
                    r = stt(o, ps[:, i, :], mod[:, 40 + c0 + i, 0:1], o, MUL, ADD, t)
                return r

            transposes(None, lambda i: m[:, i // 8, (i % 8) * 128:(i % 8) * 128 + 128], 16, t_m, evac=ev_m)
            rstd = ar(256)
            sq = ar3(8, 256)
            rms(xT, 256, 1024, rstd, sq)
            for c in range(8):
                stt(sq[:, c, :], xT[:, c, :], par(Q_FNG + c), rstd, MUL, MUL)
            t_f = V.last()

            def ev_y(a_, k, ps, t):
                tk, c0 = a_ // 8, a_ % 8
                o = m[:, tk, c0 * 128:(c0 + k) * 128].rearrange("p (k t) -> p k t", k=k)
                return cp(o, ps, t)

            transposes(None, lambda i: sq[:, i % 8, (i // 8) * 128:(i // 8) * 128 + 128], 16, t_f, evac=ev_y)
            store(out.rearrange("(t p) n -> p t n", p=128), m, V.last())

        free_pp = []
        for l in range(2):
            mixing(l, free_pp)
            free_pp = [peer(l)]
        second()

        block = ctx.enter_context(nc.Block())

        @block.sync
        def _(e):
            def issue(what, sem_, regs):
                dst, src = what
                e.dma_start(dst, src(regs["e"]) if callable(src) else src).then_inc(sem_, 16)

            walk(e, S, issue)
            if n_out[0]:
                e.wait_ge(s_out, n_out[0])

        @block.tensor
        def _(e):
            P.emit(e)

        @block.vector
        def _(e):
            V.emit(e)

        @block.scalar
        def _(e):
            A.emit(e)

        @block.gpsimd
        def _(e):
            G.emit(e)



def _constants():
    c = np.zeros((128, NC_COLS), np.float32)
    i = np.arange(128)
    c[:, C_ID:C_ID + 128] = np.eye(128)
    c[:, C_ONE:C_ONE + 128] = 1.0
    c[:, C_IOTA:C_IOTA + 128] = i[None, :]
    c[:, C_I16:C_I16 + 16] = np.arange(16)[None, :]
    c[i, C_PERM + (i // 64) * 64 + (i % 64 + 32) % 64] = 1.0
    c[:, C_VAL] = i >= 31
    c[:, C_E5] = 1e-5
    c[:, C_E6] = 1e-6
    slopes = np.array([2.0 ** (-8.0 * (h + 1) / 8) for h in range(8)], np.float32)
    end = np.arange(15) * 16 + 31
    for tk in range(2):
        t = tk * 128 + i
        dist = (t[:, None] - end[None, :]).astype(np.float32)
        b = np.where(dist[:, None, :] >= 0, -slopes[None, :, None] * np.abs(dist)[:, None, :], np.float32(-1e30))
        c[:, C_CB + tk * 120:C_CB + tk * 120 + 120] = b.reshape(128, 120)
    t = np.arange(256)
    c[:, C_MF:C_MF + 256] = (t % 128 != 0)[None, :]
    c[:, C_MB:C_MB + 256] = (t % 128 != 127)[None, :]
    inv = np.float32(10000.0) ** (-np.arange(16, dtype=np.float32) / np.float32(16))
    ang = np.concatenate([(t // 64).astype(np.float32)[:, None] * inv, (t % 64).astype(np.float32)[:, None] * inv], -1)
    cos, sin = np.cos(ang).astype(np.float32).T, np.sin(ang).astype(np.float32).T
    c[:, C_COS:C_COS + 256] = np.concatenate([cos, cos, cos, cos])
    c[:, C_SIN:C_SIN + 256] = np.concatenate([-sin, sin, -sin, sin])
    dist = 128 + i[:, None] - t[None, :]
    alibi = np.where(dist[:, None, :] >= 0, -slopes[None, :, None] * dist[:, None, :].astype(np.float32),
                     np.float32(-1e30)).astype(np.float32).reshape(128, 2048)
    m = np.zeros((2, 128, 8, 128), np.float32)
    for l, w in enumerate(LEVELS):
        same = (i[:, None] // (2 * w)) == (i[None, :] // (2 * w))
        first = (i % (2 * w)) < w
        m[0, :, l, :] = same & first[:, None] & ~first[None, :]
        m[1, :, l, :] = same & ~first[:, None] & first[None, :]
    m[:, :, 7, :] = np.eye(128)
    return c, alibi, m.reshape(2, 128, 1024)


def _cols(v, n):
    return v.reshape(n, 128).T


def _rows(w):
    return w.reshape(-1, 128, w.shape[1]).transpose(1, 0, 2).reshape(128, -1)


def _layout(x):
    a = {}
    a["cst"], a["alibi"], a["hmask"] = _constants()
    a["x"] = x["x"][0]
    a["xT"] = x["x"][0].T
    head = np.concatenate([np.concatenate([np.arange(64) + 64 * j, np.arange(64) + 64 * (4 + j)]) for j in range(4)])
    order = np.concatenate([np.arange(1024), 1024 + head, np.arange(1536, 1920), np.arange(2048, 2176)])
    tok = np.concatenate([np.arange(1920, 2048), np.arange(2176, 2328)])
    w = x["w_in"]
    a["w_inA"] = np.stack([np.stack([_rows(w[l][:, order[512 * j:512 * j + 512]]) for j in range(4)]) for l in range(2)])
    a["w_inB"] = np.stack([_rows(w[l][:, tok]) for l in range(2)])
    a["cmp_w1"] = np.stack([np.stack([np.concatenate([x[n][l].reshape(32, 64, 64).transpose(1, 0, 2)] * 2)
                                      .reshape(128, 2048) for n in ("cmpk_w1", "cmpv_w1")]) for l in range(2)])
    pp = np.zeros((2, 128, NP_COLS), np.float32)
    for l in range(2):
        p = pp[l]
        p[:, P_BIN:P_BIN + 16] = _cols(x["b_in"][l][order], 16)
        p[:, P_CW:P_CW + 16] = x["conv_w"][l].reshape(4, 4, 128).transpose(2, 0, 1).reshape(128, 16)
        for c, n in ((P_CB, "conv_b"), (P_BA, "lru_ba"), (P_BX, "lru_bx"), (P_LAM, "lru_lambda"), (P_GL, "gn_lru_g"),
                     (P_GN, "gn_nsa_g")):
            p[:, c:c + 4] = _cols(x[n][l], 4)
        p[:, P_POSK:P_POSK + 32] = np.concatenate([x["cmp_pos_k"][l].T] * 2)
        p[:, P_POSV:P_POSV + 32] = np.concatenate([x["cmp_pos_v"][l].T] * 2)
        for c, n in ((P_B1K, "cmpk_b1"), (P_B2K, "cmpk_b2"), (P_B1V, "cmpv_b1")):
            p[:, c] = np.concatenate([x[n][l]] * 2)
        p[:, P_B2V:P_B2V + 64] = x["cmpv_b2"][l][None, :]
        p[:, P_BTOK:P_BTOK + 280] = x["b_in"][l][tok][None, :]
        p[0:64, P_W2K:P_W2K + 128] = np.concatenate([x["cmpk_w2"][l]] * 2, 1)
        p[0:64, P_W2V:P_W2V + 64] = x["cmpv_w2"][l]
        p[:, P_SK:P_SK + 256] = x["peer_subkeys"][l].transpose(2, 0, 1).reshape(128, 256)
        for c, n in ((P_WA, "lru_wa"), (P_WX, "lru_wx")):
            for b in range(8):
                s = 64 * (b % 2)
                p[s:s + 64, c + 128 * (b // 2) + s:c + 128 * (b // 2) + s + 64] = x[n][l][b]
    a["pp"] = pp
    a["ln"] = np.stack([np.stack([np.concatenate([x["ln1_g"][l], x["ln1_b"][l]]),
                                  np.concatenate([x["ln2_g"][l], x["ln2_b"][l]])]) for l in range(2)])
    a["w_out"] = np.stack([np.stack([_rows(x["w_out"][l][512 * k:512 * k + 512]) for k in range(2)]) for l in range(2)])
    a["peer_wq"] = np.stack([np.stack([_rows(x["peer_wq"][l][:, 512 * j:512 * j + 512]) for j in range(4)])
                             for l in range(2)])
    a["peer_u"] = x["peer_u"].reshape(2, 128, 32, 4, 8, 128).transpose(0, 2, 5, 3, 4, 1).reshape(2, 32, 128, 4096)
    a["peer_v"] = x["peer_v"].reshape(2, 128, 32, 4096).transpose(0, 2, 1, 3)
    _layout2(x, a)
    return {k: np.ascontiguousarray(v) for k, v in a.items()}


def _layout2(x, a):
    x = {k[:-2]: v for k, v in x.items() if k.endswith("_2")}
    a["ctxT"] = x["ctx"][0].T
    q = np.zeros((128, NQ_COLS), np.float32)
    q[:, Q_NMG:Q_NMG + 8] = _cols(x["norm_mix_g"][0], 8)
    q[:, Q_QNG:Q_QNG + 6] = _cols(x["mla_q_norm_g"][0], 6)
    q[:, Q_KVG:Q_KVG + 2] = _cols(x["mla_kv_norm_g"][0], 2)
    q[:, Q_LBL:Q_LBL + 32] = x["hg_lb_logits"].reshape(2, 2, 8, 128).transpose(3, 0, 1, 2).reshape(128, 32)
    q[:, Q_HGN] = x["hg_norm_g"][0]
    q[:, Q_NFG:Q_NFG + 8] = _cols(x["norm_ffn_g"][0], 8)
    q[:, Q_BR:Q_BR + 32] = x["b_router"][0][None, :]
    q[:, Q_WR:Q_WR + 256] = _rows(x["w_router"][0])
    q[:, Q_FNG:Q_FNG + 8] = _cols(x["final_norm_g"], 8)
    a["qq"] = q
    a["mq"] = np.concatenate([np.stack([_cols(x["c"][0], 8), _cols(x["c_ctx"], 8)], -1).reshape(128, 16),
                              _cols(x["b_mod"][0], 48)], 1)
    w = x["w_mod"][0]
    a["w_mod"] = np.stack([_rows(w[:, 512 * j:512 * j + 512]) for j in range(12)])
    w = x["w_in"][0]
    a["w_q"] = np.stack([_rows(w[:, 384 * j:384 * j + 384]) for j in range(2)])
    a["w_kv"] = _rows(np.concatenate([w[:, 768:1088], w[:, 1024:1088]], 1))
    a["w_hg"] = np.stack([_rows(w[:, 1088 + 512 * j:1088 + 512 * j + 512]) for j in range(14)])
    w = x["w_q_b"][0].reshape(768, 8, 192)
    a["w_qb_n"] = np.stack([_rows(w[:, 4 * j:4 * j + 4, 0:128].reshape(768, 512)) for j in range(2)])
    a["w_qb_r"] = _rows(w[:, :, 128:192].reshape(768, 512))
    w = x["w_kv_b"][0].reshape(256, 8, 256)
    a["w_kvb"] = np.concatenate([_rows(w[:, :, 0:128].reshape(256, 1024)), _rows(w[:, :, 128:256].reshape(256, 1024))], 1)
    a["w_o2"] = np.stack([_rows(x["w_out"][0][:, 512 * j:512 * j + 512]) for j in range(2)])
    a["w_gu"] = x["w_gate_up"][0].reshape(32, 2, 4, 128, 2, 512, 2).transpose(0, 6, 1, 3, 2, 4, 5).reshape(32, 4, 128, 4096)
    a["b_gu"] = x["b_gate_up"][0].reshape(32, 1024, 2).transpose(0, 2, 1).reshape(32, 2048)
    a["w_dn"] = x["w_down"][0].reshape(32, 2, 4, 128, 1024).transpose(0, 1, 3, 2, 4).reshape(32, 2, 128, 4096)
    a["b_dn"] = x["b_down"][0]


def kernel(**inputs):
    import concourse.bacc as _bacc
    from concourse.bass_utils import run_bass_kernel_spmd as _run

    nc = _bacc.Bacc("TRN2", target_bir_lowering=False, num_devices=1)
    arrays, args = {}, {}
    for name, a in _layout({k: np.asarray(v) for k, v in inputs.items()}).items():
        arrays[f"in_{name}_dram"] = a
        args[name] = nc.dram_tensor(f"in_{name}_dram", a.shape, F32, kind="ExternalInput").ap()
    out = nc.dram_tensor("out_0_dram", (256, 1024), F32, kind="ExternalOutput").ap()
    build(nc, args, out)
    r = _run(nc, [arrays], core_ids=[0])
    return r.results[0]["out_0_dram"].reshape(1, 256, 1024)
```
